# Optimizing a Trainium2 kernel written in Bass

```python
import jax, jax.numpy as jnp
from jax import lax
import numpy as np
import math
import jax
import jax.numpy as jnp

D_MODEL = 1024
BATCH = 1
SEQ = 512
DEPTH = 1

CHUNK = 64
N_PREV_CHUNKS = 8
BAND_CHUNKS = N_PREV_CHUNKS + 1
N_HEADS = 16
HEAD_DIM = 64
D_ATTN = N_HEADS * HEAD_DIM
D_CONV = D_MODEL
CONV_WIDTH = 3
MAX_REL = 256
D_FF = 4 * D_MODEL
N_BRANCHES = 2
EPS = 1e-6
NEG_INF = -1e30


def rms_norm(x, g):
    xf = x.astype(jnp.float32)
    y = xf * lax.rsqrt(jnp.mean(xf * xf, axis=-1, keepdims=True) + EPS)
    return (y * g.astype(jnp.float32)).astype(x.dtype)

def chunk_band(t):
    b, nc, c, h, dh = t.shape
    tp = jnp.pad(t, ((0, 0), (N_PREV_CHUNKS, 0), (0, 0), (0, 0), (0, 0)))
    band = jnp.stack([tp[:, o:o + nc] for o in range(BAND_CHUNKS)], axis=2)
    return band.reshape(b, nc, BAND_CHUNKS * c, h, dh)

def chunked_relpos_attention(q, k, v, q_norm_g, k_norm_g, rel_bias):
    b, s, _ = q.shape
    nc = s // CHUNK
    kw = BAND_CHUNKS * CHUNK
    q = rms_norm(q.reshape(b, nc, CHUNK, N_HEADS, HEAD_DIM), q_norm_g)
    k = rms_norm(k.reshape(b, nc, CHUNK, N_HEADS, HEAD_DIM), k_norm_g)
    v = v.reshape(b, nc, CHUNK, N_HEADS, HEAD_DIM)
    kb = chunk_band(k)
    vb = chunk_band(v)

    q_idx = jnp.arange(CHUNK)[:, None]
    k_idx = jnp.arange(kw)[None, :]
    dist = q_idx - k_idx + N_PREV_CHUNKS * CHUNK
    rel_idx = jnp.clip(dist, -MAX_REL, MAX_REL) + MAX_REL
    bias = rel_bias[:, rel_idx].astype(jnp.float32)

    key_chunk = jnp.arange(nc)[:, None] + (jnp.arange(kw) // CHUNK)[None, :] - N_PREV_CHUNKS
    valid = key_chunk >= 0

    scale = HEAD_DIM ** -0.5
    scores = jnp.einsum('bnqhd,bnkhd->bnhqk', q, kb).astype(jnp.float32) * scale
    scores = scores + bias[None, None]
    scores = jnp.where(valid[None, :, None, None, :], scores, NEG_INF)
    probs = jax.nn.softmax(scores, axis=-1).astype(vb.dtype)
    out = jnp.einsum('bnhqk,bnkhd->bnqhd', probs, vb)
    return out.reshape(b, s, D_ATTN)

def gated_short_conv(bg, cg, xc, conv_w, conv_b):
    s = xc.shape[1]
    u = cg * xc
    up = jnp.pad(u, ((0, 0), (CONV_WIDTH - 1, 0), (0, 0)))
    conv = conv_b + sum(conv_w[j] * up[:, j:j + s] for j in range(CONV_WIDTH))
    return bg * conv

def first_inputs(seed: int = 0) -> dict:
    key = jax.random.key(seed)
    ks = jax.random.split(key, 20)
    f32 = jnp.float32
    d_in = 3 * D_ATTN + 3 * D_CONV
    return {
        "x": jax.random.normal(ks[0], (BATCH, SEQ, D_MODEL), f32),
        "norm1_g": 1.0 + 0.05 * jax.random.normal(ks[1], (D_MODEL,), f32),
        "w_in": jax.random.normal(ks[2], (D_MODEL, d_in), f32) * D_MODEL ** -0.5,
        "q_norm_g": 1.0 + 0.05 * jax.random.normal(ks[3], (HEAD_DIM,), f32),
        "k_norm_g": 1.0 + 0.05 * jax.random.normal(ks[4], (HEAD_DIM,), f32),
        "rel_bias": 0.5 * jax.random.normal(ks[5], (N_HEADS, 2 * MAX_REL + 1), f32),
        "conv_w": jax.random.normal(ks[6], (CONV_WIDTH, D_CONV), f32) * CONV_WIDTH ** -0.5,
        "conv_b": 0.02 * jax.random.normal(ks[7], (D_CONV,), f32),
        "w_attn_proj": jax.random.normal(ks[8], (D_ATTN, D_MODEL), f32) * D_ATTN ** -0.5,
        "w_conv_proj": jax.random.normal(ks[9], (D_CONV, D_MODEL), f32) * D_CONV ** -0.5,
        "w_gate": jax.random.normal(ks[10], (D_MODEL, N_BRANCHES * D_MODEL), f32) * D_MODEL ** -0.5,
        "b_gate": 0.02 * jax.random.normal(ks[11], (N_BRANCHES * D_MODEL,), f32),
        "w_out": jax.random.normal(ks[12], (D_MODEL, D_MODEL), f32) * D_MODEL ** -0.5,
        "norm2_g": 1.0 + 0.05 * jax.random.normal(ks[13], (D_MODEL,), f32),
        "w_up": jax.random.normal(ks[14], (D_MODEL, D_FF), f32) * D_MODEL ** -0.5,
        "w_down": jax.random.normal(ks[15], (D_FF, D_MODEL), f32) * D_FF ** -0.5,
    }

def first_block(x, norm1_g, w_in, q_norm_g, k_norm_g, rel_bias, conv_w, conv_b,
              w_attn_proj, w_conv_proj, w_gate, b_gate, w_out, norm2_g, w_up, w_down):
    for _ in range(DEPTH):
        h = rms_norm(x, norm1_g)
        proj = jnp.einsum('bsd,de->bse', h, w_in)
        q, k, v, bg, cg, xc = jnp.split(
            proj,
            [D_ATTN, 2 * D_ATTN, 3 * D_ATTN,
             3 * D_ATTN + D_CONV, 3 * D_ATTN + 2 * D_CONV],
            axis=-1)

        y_attn = chunked_relpos_attention(q, k, v, q_norm_g, k_norm_g, rel_bias)
        y_conv = gated_short_conv(bg, cg, xc, conv_w, conv_b)

        y_attn = jnp.einsum('bse,ed->bsd', y_attn, w_attn_proj)
        y_conv = jnp.einsum('bse,ed->bsd', y_conv, w_conv_proj)

        gates = jax.nn.sigmoid(jnp.einsum('bsd,de->bse', h, w_gate) + b_gate)
        g_attn, g_conv = jnp.split(gates, 2, axis=-1)
        merged = g_attn * y_attn + g_conv * y_conv
        x = x + jnp.einsum('bsd,de->bse', merged, w_out)

        h2 = rms_norm(x, norm2_g)
        u = jnp.square(jax.nn.relu(jnp.einsum('bsd,df->bsf', h2, w_up)))
        x = x + jnp.einsum('bsf,fd->bsd', u, w_down)
    return x


DEPTH_2 = 2

F32 = jnp.float32
N_MIXERS = 4
GRID_W = 64
MEM_LEN = 256
NORM_EPS = 1e-6

ATT_HEADS = 16
ATT_KV_HEADS = 4
ATT_HEAD_DIM = D_MODEL // ATT_HEADS
ATT_Q_W = ATT_HEADS * ATT_HEAD_DIM
ATT_KV_W = ATT_KV_HEADS * ATT_HEAD_DIM
ROPE_THETA = 10000.0
WINDOW = 128
ATT_BLOCK = 128

NA_ROWS_MAX = 8
NA_COLS = 16
NA_QCOLS = 16
NA_KCOLS = NA_QCOLS + NA_COLS

X_HEADS = 4
X_HEAD_DIM = 128
X_W = X_HEADS * X_HEAD_DIM

HG_KEY_DIM = 128
HG_HEADS = D_MODEL // HG_KEY_DIM
HG_VAL_DIM = D_MODEL // HG_HEADS
HG_W = HG_HEADS * HG_KEY_DIM
HG_CHUNK = 16

SSM_INNER = 2 * D_MODEL
SSM_HEAD_DIM = 64
SSM_HEADS = SSM_INNER // SSM_HEAD_DIM
SSM_GROUPS = 8
SSM_HEADS_PER_GROUP = SSM_HEADS // SSM_GROUPS
SSM_STATE = 128
SSM_CONV = 5
SSM_CHUNK = 64
SSM_CONV_DIM = SSM_INNER + 2 * SSM_GROUPS * SSM_STATE

D_FF_2 = 2816
FFN_CONV = 3

A_IN_W = ATT_Q_W + 2 * ATT_KV_W + X_W
B_IN_W = 5 * HG_W + X_W
C_IN_W = SSM_INNER + SSM_CONV_DIM + 2 * SSM_HEADS + X_W
D_IN_W = ATT_Q_W + 2 * ATT_KV_W + X_W


def _layers_of(m):
    return (DEPTH_2 - m + N_MIXERS - 1) // N_MIXERS

def rmsnorm(x, g):
    xf = x.astype(F32)
    y = xf * lax.rsqrt(jnp.mean(xf * xf, axis=-1, keepdims=True) + NORM_EPS)
    return (y * g.astype(F32)).astype(x.dtype)

def flip_t(a):
    return jnp.flip(a, axis=1)

def rope(x, pos):
    half = x.shape[-1] // 2
    inv = ROPE_THETA ** (-jnp.arange(half, dtype=F32) / half)
    ang = pos.astype(F32)[:, None] * inv[None, :]
    cos = jnp.cos(ang)[None, :, None, :]
    sin = jnp.sin(ang)[None, :, None, :]
    xf = x.astype(F32)
    x1, x2 = xf[..., :half], xf[..., half:]
    return jnp.concatenate([x1 * cos - x2 * sin, x2 * cos + x1 * sin], axis=-1).astype(x.dtype)

def dwconv_centred(x, w, b):
    k, c = w.shape
    y = lax.conv_general_dilated(x, w[:, None, :].astype(x.dtype), window_strides=(1,),
                                 padding=[(k // 2, k // 2)],
                                 dimension_numbers=('NWC', 'WIO', 'NWC'),
                                 feature_group_count=c)
    return y + b.astype(x.dtype)

def memory_cross_attn(xq, mem_kv):
    bsz, t, _ = xq.shape
    q = xq.reshape(bsz, t, X_HEADS, X_HEAD_DIM)
    k, v = jnp.split(mem_kv, 2, axis=-1)
    k = k.reshape(bsz, -1, X_HEADS, X_HEAD_DIM)
    v = v.reshape(bsz, -1, X_HEADS, X_HEAD_DIM)
    s = jnp.einsum('bthd,bmhd->bhtm', q, k, preferred_element_type=F32) * (X_HEAD_DIM ** -0.5)
    p = jax.nn.softmax(s, axis=-1)
    o = jnp.einsum('bhtm,bmhd->bthd', p.astype(v.dtype), v)
    return o.reshape(bsz, t, X_W)

def window_gqa_sink(q, k, v, sink):
    bsz, t, hq, d = q.shape
    hkv = k.shape[2]
    grp = hq // hkv
    nb = t // ATT_BLOCK
    band = ATT_BLOCK + 2 * WINDOW
    pad = ((0, 0), (WINDOW, WINDOW), (0, 0), (0, 0))
    idx = np.arange(nb)[:, None] * ATT_BLOCK + np.arange(band)[None, :]
    kb = jnp.pad(k, pad)[:, idx]
    vb = jnp.pad(v, pad)[:, idx]
    qb = q.reshape(bsz, nb, ATT_BLOCK, hkv, grp, d)
    s = jnp.einsum('bnqhgd,bnkhd->bnhgqk', qb, kb, preferred_element_type=F32) * (d ** -0.5)
    qpos = np.arange(nb)[:, None] * ATT_BLOCK + np.arange(ATT_BLOCK)[None, :]
    kpos = idx - WINDOW
    valid = ((np.abs(qpos[:, :, None] - kpos[:, None, :]) <= WINDOW)
             & (kpos >= 0)[:, None, :] & (kpos < t)[:, None, :])
    s = jnp.where(valid[None, :, None, None], s, -jnp.inf)
    sk = sink.astype(F32).reshape(hkv, grp)[None, None, :, :, None, None]
    m = jnp.maximum(jnp.max(s, axis=-1, keepdims=True), sk)
    p = jnp.exp(s - m)
    p = p / (jnp.sum(p, axis=-1, keepdims=True) + jnp.exp(sk - m))
    o = jnp.einsum('bnhgqk,bnkhd->bnqhgd', p.astype(v.dtype), vb)
    return o.reshape(bsz, t, hq, d)

def neighbourhood_attn(q, k, v, rpb):
    bsz, t, hq, d = q.shape
    hkv = k.shape[2]
    grp = hq // hkv
    rows = t // GRID_W
    kr = min(NA_ROWS_MAX, rows)
    ncb = GRID_W // NA_QCOLS
    r = np.arange(rows)
    key_rows = np.clip(r - kr // 2, 0, rows - kr)[:, None] + np.arange(kr)[None, :]
    key_cols = (np.clip(np.arange(ncb) * NA_QCOLS - NA_COLS // 2, 0, GRID_W - NA_KCOLS)[:, None]
                + np.arange(NA_KCOLS)[None, :])
    key_idx = (key_rows[:, None, :, None] * GRID_W + key_cols[None, :, None, :]).reshape(rows, ncb, kr * NA_KCOLS)
    kg = k[:, key_idx]
    vg = v[:, key_idx]
    qb = q.reshape(bsz, rows, ncb, NA_QCOLS, hkv, grp, d)
    s = jnp.einsum('brjqhgd,brjkhd->brjhgqk', qb, kg, preferred_element_type=F32) * (d ** -0.5)
    qcol = np.arange(ncb)[:, None] * NA_QCOLS + np.arange(NA_QCOLS)[None, :]
    col_start = np.clip(qcol - NA_COLS // 2, 0, GRID_W - NA_COLS)
    kcol = np.repeat(key_cols[:, None, :], kr, axis=1).reshape(ncb, -1)
    krow = np.repeat(key_rows[:, :, None], NA_KCOLS, axis=2).reshape(rows, -1)
    in_win = ((kcol[:, None, :] >= col_start[..., None])
              & (kcol[:, None, :] < col_start[..., None] + NA_COLS))
    dr = krow - r[:, None] + NA_ROWS_MAX - 1
    dc = np.clip(kcol[:, None, :] - qcol[..., None] + NA_COLS - 1, 0, 2 * NA_COLS - 2)
    bias = rpb.astype(F32)[:, dr[:, None, None, :], dc[None]]
    bias = jnp.where(in_win[None, None], bias, -jnp.inf)
    bias = bias.reshape(hkv, grp, rows, ncb, NA_QCOLS, -1).transpose(2, 3, 0, 1, 4, 5)
    p = jax.nn.softmax(s + bias[None], axis=-1)
    o = jnp.einsum('brjhgqk,brjkhd->brjqhgd', p.astype(v.dtype), vg)
    return o.reshape(bsz, t, hq, d)

def gla_chunked(q, k, v, log_f):
    bsz, t, h, dk = q.shape
    dv = v.shape[-1]
    n = t // HG_CHUNK
    q, k, log_f = (a.reshape(bsz, n, HG_CHUNK, h, dk) for a in (q, k, log_f))
    v = v.reshape(bsz, n, HG_CHUNK, h, dv)
    b = jnp.cumsum(log_f, axis=2)
    b_end = b[:, :, -1:]
    q_dec = q * jnp.exp(b)
    k_dec = k * jnp.exp(-b)
    k_end = k * jnp.exp(b_end - b)
    causal = np.tril(np.ones((HG_CHUNK, HG_CHUNK), dtype=bool))
    s = jnp.where(causal, jnp.einsum('bcthk,bcshk->bchts', q_dec, k_dec), 0.0)
    o_intra = jnp.einsum('bchts,bcshv->bcthv', s, v)

    def step(state, inp):
        qd, ke, vc, dec = inp
        o = jnp.einsum('bthk,bhkv->bthv', qd, state)
        state = dec[..., None] * state + jnp.einsum('bshk,bshv->bhkv', ke, vc)
        return state, o

    xs = tuple(jnp.moveaxis(a, 1, 0) for a in (q_dec, k_end, v, jnp.exp(b_end[:, :, 0])))
    _, o_inter = lax.scan(step, jnp.zeros((bsz, h, dk, dv), F32), xs)
    return (o_intra + jnp.moveaxis(o_inter, 0, 1)).reshape(bsz, t, h, dv)

def ssd_chunked(x, dt, a, bm, cm):
    bsz, t, g, j, p = x.shape
    nst = bm.shape[-1]
    n = t // SSM_CHUNK
    x = x.reshape(bsz, n, SSM_CHUNK, g, j, p)
    dt = dt.reshape(bsz, n, SSM_CHUNK, g, j)
    bm = bm.reshape(bsz, n, SSM_CHUNK, g, nst)
    cm = cm.reshape(bsz, n, SSM_CHUNK, g, nst)
    cs = jnp.cumsum(dt * a, axis=2)
    xdt = x * dt[..., None]
    cs_t = jnp.moveaxis(cs, 2, -1)
    causal = np.tril(np.ones((SSM_CHUNK, SSM_CHUNK), dtype=bool))
    decay = jnp.exp(jnp.where(causal, cs_t[..., :, None] - cs_t[..., None, :], -jnp.inf))
    cb = jnp.einsum('bctgn,bcsgn->bcgts', cm, bm)
    y_diag = jnp.einsum('bcgjts,bcsgjp->bctgjp', cb[:, :, :, None] * decay, xdt)

    def step(state, inp):
        cq, bk, xd, c = inp
        c_end = c[:, -1]
        y_off = jnp.einsum('btgn,bgjpn->btgjp', cq, state) * jnp.exp(c)[..., None]
        w = jnp.exp(c_end[:, None] - c)[..., None]
        state = jnp.exp(c_end)[..., None, None] * state + jnp.einsum('bsgn,bsgjp->bgjpn', bk, xd * w)
        return state, y_off

    xs = tuple(jnp.moveaxis(arr, 1, 0) for arr in (cm, bm, xdt, cs))
    _, y_off = lax.scan(step, jnp.zeros((bsz, g, j, p, nst), F32), xs)
    return (y_diag + jnp.moveaxis(y_off, 0, 1)).reshape(bsz, t, g, j, p)

def hgrn_lower_bounds(logits):
    p = jax.nn.softmax(logits.astype(F32), axis=1)
    return jnp.cumsum(p, axis=1) - p[:, :1]

def mixer_window_attn(u, mem_kv, w_in, sink, w_out, pos):
    bsz, t, _ = u.shape
    q, k, v, xq = jnp.split(u @ w_in, [ATT_Q_W, ATT_Q_W + ATT_KV_W, ATT_Q_W + 2 * ATT_KV_W], axis=-1)
    q = rope(q.reshape(bsz, t, ATT_HEADS, ATT_HEAD_DIM), pos)
    k = rope(k.reshape(bsz, t, ATT_KV_HEADS, ATT_HEAD_DIM), pos)
    v = v.reshape(bsz, t, ATT_KV_HEADS, ATT_HEAD_DIM)
    o = window_gqa_sink(q, k, v, sink).reshape(bsz, t, ATT_Q_W)
    return jnp.concatenate([o, memory_cross_attn(xq, mem_kv)], axis=-1) @ w_out

def mixer_hgrn2(u, mem_kv, w_in, lb_fwd, lb_bwd, norm_g, w_out):
    bsz, t, _ = u.shape
    q, i, zf, zb, gate, xq = jnp.split(u @ w_in, [HG_W, 2 * HG_W, 3 * HG_W, 4 * HG_W, 5 * HG_W], axis=-1)
    shp = (bsz, t, HG_HEADS, HG_KEY_DIM)
    q = jax.nn.silu(q.astype(F32)).reshape(shp)
    v = i.astype(F32).reshape(bsz, t, HG_HEADS, HG_VAL_DIM)

    def forget(z, lb):
        f = lb + (1.0 - lb) * jax.nn.sigmoid(z.astype(F32))
        return jnp.log(f).reshape(shp), (1.0 - f).reshape(shp)

    lf_f, k_f = forget(zf, lb_fwd)
    lf_b, k_b = forget(zb, lb_bwd)
    o = (gla_chunked(q, k_f, v, lf_f)
         + flip_t(gla_chunked(flip_t(q), flip_t(k_b), flip_t(v), flip_t(lf_b))))
    o = rmsnorm(o, norm_g.reshape(HG_HEADS, HG_VAL_DIM)).reshape(bsz, t, HG_W).astype(u.dtype)
    o = o * jax.nn.silu(gate)
    return jnp.concatenate([o, memory_cross_attn(xq, mem_kv)], axis=-1) @ w_out

def mixer_mamba2(u, mem_kv, w_in, conv_w, conv_b, dt_bias, a_log, d_skip, norm_g, w_out):
    bsz, t, _ = u.shape
    z, xbc, dt_raw, xq = jnp.split(
        u @ w_in, [SSM_INNER, SSM_INNER + SSM_CONV_DIM, SSM_INNER + SSM_CONV_DIM + 2 * SSM_HEADS], axis=-1)
    xbc = jax.nn.silu(dwconv_centred(xbc, conv_w, conv_b)).astype(F32)
    xs, bm, cm = jnp.split(xbc, [SSM_INNER, SSM_INNER + SSM_GROUPS * SSM_STATE], axis=-1)
    xs = xs.reshape(bsz, t, SSM_GROUPS, SSM_HEADS_PER_GROUP, SSM_HEAD_DIM)
    bm = bm.reshape(bsz, t, SSM_GROUPS, SSM_STATE)
    cm = cm.reshape(bsz, t, SSM_GROUPS, SSM_STATE)
    dt = jax.nn.softplus(dt_raw.astype(F32).reshape(bsz, t, 2, SSM_HEADS) + dt_bias.astype(F32))
    dt = dt.reshape(bsz, t, 2, SSM_GROUPS, SSM_HEADS_PER_GROUP)
    a = -jnp.exp(a_log.astype(F32)).reshape(2, SSM_GROUPS, SSM_HEADS_PER_GROUP)
    y = (ssd_chunked(xs, dt[:, :, 0], a[0], bm, cm)
         + flip_t(ssd_chunked(flip_t(xs), flip_t(dt[:, :, 1]), a[1], flip_t(bm), flip_t(cm))))
    y = y + d_skip.astype(F32).reshape(SSM_GROUPS, SSM_HEADS_PER_GROUP, 1) * xs
    y = y.reshape(bsz, t, SSM_INNER) * jax.nn.silu(z.astype(F32))
    y = rmsnorm(y.reshape(bsz, t, SSM_GROUPS, -1), norm_g.reshape(SSM_GROUPS, -1))
    y = y.reshape(bsz, t, SSM_INNER).astype(u.dtype)
    return jnp.concatenate([y, memory_cross_attn(xq, mem_kv)], axis=-1) @ w_out

def mixer_neighbourhood(u, mem_kv, w_in, rpb, w_out):
    bsz, t, _ = u.shape
    q, k, v, xq = jnp.split(u @ w_in, [ATT_Q_W, ATT_Q_W + ATT_KV_W, ATT_Q_W + 2 * ATT_KV_W], axis=-1)
    q = q.reshape(bsz, t, ATT_HEADS, ATT_HEAD_DIM)
    k = k.reshape(bsz, t, ATT_KV_HEADS, ATT_HEAD_DIM)
    v = v.reshape(bsz, t, ATT_KV_HEADS, ATT_HEAD_DIM)
    o = neighbourhood_attn(q, k, v, rpb).reshape(bsz, t, ATT_Q_W)
    return jnp.concatenate([o, memory_cross_attn(xq, mem_kv)], axis=-1) @ w_out

def conv_ffn(v, w_in, conv_w, conv_b, w_out):
    gate, up = jnp.split(v @ w_in, 2, axis=-1)
    hid = jax.nn.gelu(dwconv_centred(gate, conv_w, conv_b)) * up
    return hid @ w_out

def second_inputs(seed: int = 0) -> dict:
    key = jax.random.key(seed)
    ks = jax.random.split(key, 32)
    n_a, n_b, n_c, n_d = (_layers_of(m) for m in range(N_MIXERS))

    def nrm(k, shape, scale):
        return jax.random.normal(k, shape, F32) * scale

    def gain(k, shape):
        return 1.0 + 0.05 * jax.random.normal(k, shape, F32)

    dt0 = jnp.exp(jax.random.uniform(ks[16], (n_c, 2, SSM_HEADS), F32, math.log(1e-3), math.log(1e-1)))
    return {
        'x': nrm(ks[0], (BATCH, SEQ, D_MODEL), 1.0),
        'mem': nrm(ks[1], (BATCH, MEM_LEN, D_MODEL), 1.0),
        'norm_g': gain(ks[2], (DEPTH_2, 4, D_MODEL)),
        'mem_norm_g': gain(ks[3], (D_MODEL,)),
        'w_mem_kv': nrm(ks[4], (DEPTH_2, D_MODEL, 2 * X_W), D_MODEL ** -0.5),
        'a_w_in': nrm(ks[5], (n_a, D_MODEL, A_IN_W), D_MODEL ** -0.5),
        'a_sink': nrm(ks[6], (n_a, ATT_HEADS), 0.5),
        'a_w_out': nrm(ks[7], (n_a, ATT_Q_W + X_W, D_MODEL), (ATT_Q_W + X_W) ** -0.5),
        'b_w_in': nrm(ks[8], (n_b, D_MODEL, B_IN_W), D_MODEL ** -0.5),
        'b_lb_logits': nrm(ks[9], (2, DEPTH_2, HG_W), 0.1),
        'b_norm_g': gain(ks[10], (n_b, HG_W)),
        'b_w_out': nrm(ks[11], (n_b, HG_W + X_W, D_MODEL), (HG_W + X_W) ** -0.5),
        'c_w_in': nrm(ks[12], (n_c, D_MODEL, C_IN_W), D_MODEL ** -0.5),
        'c_conv_w': nrm(ks[13], (n_c, SSM_CONV, SSM_CONV_DIM), SSM_CONV ** -0.5),
        'c_conv_b': nrm(ks[14], (n_c, SSM_CONV_DIM), 0.02),
        'c_dt_bias': dt0 + jnp.log(-jnp.expm1(-dt0)),
        'c_a_log': jnp.log(jax.random.uniform(ks[15], (n_c, 2, SSM_HEADS), F32, 1.0, 16.0)),
        'c_d': 1.0 + 0.1 * jax.random.normal(ks[17], (n_c, SSM_HEADS), F32),
        'c_norm_g': gain(ks[18], (n_c, SSM_INNER)),
        'c_w_out': nrm(ks[19], (n_c, SSM_INNER + X_W, D_MODEL), (SSM_INNER + X_W) ** -0.5),
        'd_w_in': nrm(ks[20], (n_d, D_MODEL, D_IN_W), D_MODEL ** -0.5),
        'd_rpb': nrm(ks[21], (n_d, ATT_HEADS, 2 * NA_ROWS_MAX - 1, 2 * NA_COLS - 1), 0.1),
        'd_w_out': nrm(ks[22], (n_d, ATT_Q_W + X_W, D_MODEL), (ATT_Q_W + X_W) ** -0.5),
        'ffn_w_in': nrm(ks[23], (DEPTH_2, D_MODEL, 2 * D_FF_2), D_MODEL ** -0.5),
        'ffn_conv_w': nrm(ks[24], (DEPTH_2, FFN_CONV, D_FF_2), FFN_CONV ** -0.5),
        'ffn_conv_b': nrm(ks[25], (DEPTH_2, D_FF_2), 0.02),
        'ffn_w_out': nrm(ks[26], (DEPTH_2, D_FF_2, D_MODEL), D_FF_2 ** -0.5),
    }

def second_block(x, mem, norm_g, mem_norm_g, w_mem_kv, a_w_in, a_sink, a_w_out,
              b_w_in, b_lb_logits, b_norm_g, b_w_out,
              c_w_in, c_conv_w, c_conv_b, c_dt_bias, c_a_log, c_d, c_norm_g, c_w_out,
              d_w_in, d_rpb, d_w_out, ffn_w_in, ffn_conv_w, ffn_conv_b, ffn_w_out):
    t = x.shape[1]
    pos = jnp.arange(t)
    mem_n = rmsnorm(mem, mem_norm_g)
    lb = hgrn_lower_bounds(b_lb_logits)
    h = x
    for layer in range(DEPTH_2):
        kind, slot = layer % N_MIXERS, layer // N_MIXERS
        u = rmsnorm(h, norm_g[layer, 0])
        mem_kv = mem_n @ w_mem_kv[layer]
        if kind == 0:
            y = mixer_window_attn(u, mem_kv, a_w_in[slot], a_sink[slot], a_w_out[slot], pos)
        elif kind == 1:
            y = mixer_hgrn2(u, mem_kv, b_w_in[slot], lb[0, layer], lb[1, layer], b_norm_g[slot], b_w_out[slot])
        elif kind == 2:
            y = mixer_mamba2(u, mem_kv, c_w_in[slot], c_conv_w[slot], c_conv_b[slot], c_dt_bias[slot],
                             c_a_log[slot], c_d[slot], c_norm_g[slot], c_w_out[slot])
        else:
            y = mixer_neighbourhood(u, mem_kv, d_w_in[slot], d_rpb[slot], d_w_out[slot])
        h = h + rmsnorm(y, norm_g[layer, 1])
        f = conv_ffn(rmsnorm(h, norm_g[layer, 2]), ffn_w_in[layer], ffn_conv_w[layer],
                     ffn_conv_b[layer], ffn_w_out[layer])
        h = h + rmsnorm(f, norm_g[layer, 3])
    return h


def setup_inputs(seed=0):
    out = dict(first_inputs(seed))
    for name, value in second_inputs(seed + 1).items():
        if name != "x":
            out[name + "_2"] = value
    return out


def reference(
    x, norm1_g, w_in, q_norm_g, k_norm_g, rel_bias, conv_w, conv_b, w_attn_proj, w_conv_proj,
    w_gate, b_gate, w_out, norm2_g, w_up, w_down, mem_2, norm_g_2, mem_norm_g_2, w_mem_kv_2,
    a_w_in_2, a_sink_2, a_w_out_2, b_w_in_2, b_lb_logits_2, b_norm_g_2, b_w_out_2, c_w_in_2,
    c_conv_w_2, c_conv_b_2, c_dt_bias_2, c_a_log_2, c_d_2, c_norm_g_2, c_w_out_2, d_w_in_2,
    d_rpb_2, d_w_out_2, ffn_w_in_2, ffn_conv_w_2, ffn_conv_b_2, ffn_w_out_2,
):
    x = first_block(
        x, norm1_g, w_in, q_norm_g, k_norm_g, rel_bias, conv_w, conv_b, w_attn_proj,
        w_conv_proj, w_gate, b_gate, w_out, norm2_g, w_up, w_down,
    )
    return second_block(
        x, mem_2, norm_g_2, mem_norm_g_2, w_mem_kv_2, a_w_in_2, a_sink_2, a_w_out_2, b_w_in_2,
        b_lb_logits_2, b_norm_g_2, b_w_out_2, c_w_in_2, c_conv_w_2, c_conv_b_2, c_dt_bias_2,
        c_a_log_2, c_d_2, c_norm_g_2, c_w_out_2, d_w_in_2, d_rpb_2, d_w_out_2, ffn_w_in_2,
        ffn_conv_w_2, ffn_conv_b_2, ffn_w_out_2,
    )


_drawn_inputs = setup_inputs


def setup_inputs(seed=0):
    import zlib

    import numpy as np

    out = dict(_drawn_inputs(seed))
    spreads = {}
    factors = {'q_norm_g': 8.0,
     'k_norm_g': 8.0,
     'conv_b': 4.901,
     'b_gate': 8.0,
     'mem_norm_g_2': 4.602,
     'a_sink_2': 8.0,
     'b_lb_logits_2': 60.632,
     'ffn_conv_b_2': 4.283,
     'b_norm_g_2': 8.0}
    for name, (base, spread) in spreads.items():
        noise = np.random.default_rng([zlib.crc32(name.encode()), seed]).standard_normal(out[name].shape)
        drawn = base * np.exp(spread * noise) if base else spread * noise
        out[name] = jnp.asarray(drawn.astype(out[name].dtype))
    for name, factor in factors.items():
        out[name] = (out[name] * factor).astype(out[name].dtype)
    return out
```

```python
from contextlib import ExitStack, contextmanager

import numpy as np

import concourse.bass as bass
from concourse import mybir

F32 = mybir.dt.float32
F32R = mybir.dt.float32r
ALU = mybir.AluOpType
ACT = mybir.ActivationFunctionType

P = 128
T = 512
D = 1024
DT = D // P
BLOCKS = T // P
EPS = 1e-6
NEG = -1e30

RING = 4
SLOT_TILES = 8
BANKS = 4

HEADS, HEAD_DIM, CHUNK, MAX_REL = 16, 64, 64, 256
FF1 = 4 * D
HALF = FF1 // P // 2
EXT_W = 640
MEM = 256
KV_HEADS = 4
X_HEADS = 4
FF2 = 2816 // P
HG_HEADS, HG_CHUNK = 8, 16
CHUNKS = T // HG_CHUNK
GROUP = 4
BLOCK_CHUNKS = P // HG_CHUNK

STAGES = [
    ("qkv", 24, 8), ("conv", 24, 8), ("gate", 16, 8), ("proj", 16, 8), ("out", 8, 8),
    ("up0", HALF, 8), ("down0", 8, HALF), ("up1", HALF, 8), ("down1", 8, HALF),
    ("memkv", 16, 8),
    ("a_in", 16, 8), ("a_out", 8, 12), ("ffn_in0", 2 * FF2, 8), ("ffn_out0", 8, FF2),
    ("b_in", 44, 8), ("b_out", 8, 12), ("ffn_in1", 2 * FF2, 8), ("ffn_out1", 8, FF2),
]

PARAM_COLS = {}
_at = 0
for _name, _n in [
    ("norm1_g", 8), ("norm2_g", 8), ("q_g", 1), ("k_g", 1), ("conv_w", 24), ("conv_b", 8), ("b_gate", 16),
    ("norm_g", 64), ("mem_g", 8), ("lb_logits", 32), ("b_norm_g", 8), ("ffn_w", 2 * 3 * FF2), ("ffn_b", 2 * FF2),
    ("sink", 16),
]:
    PARAM_COLS[_name] = _at
    _at += _n
PARAM_W = _at

CONST_COLS = {}
_at = 0
for _name, _n in [
    ("ident", 128), ("rot", 128), ("pair_ones", 128), ("ones", 128), ("win_mask", 384), ("causal_f", 128),
    ("causal_b", 128), ("chunk_mask", BLOCK_CHUNKS), ("reset", 512), ("zeros", 512),
]:
    CONST_COLS[_name] = _at
    _at += _n
CONST_W = _at


class Stage:

    def __init__(self, name, cbs, kt, first_slot, first_cb, prev):
        self.name, self.cbs, self.kt = name, cbs, kt
        self.first_slot, self.first_cb, self.prev = first_slot, first_cb, prev
        self.slots = cbs * kt // SLOT_TILES
        self.free = None

    def made(self, c):
        if self.kt % SLOT_TILES == 0:
            return c * (self.kt // SLOT_TILES) + self.first_slot + self.kt // SLOT_TILES
        return self.first_slot + ((c + 1) * self.kt - 1) // SLOT_TILES + 1

    def bank(self, c):
        return (self.first_cb + c) % BANKS


class Order:

    def __init__(self, eng, own):
        self.eng, self.own, self.count, self.last = eng, own, {}, None
        self.it = self.lo = None
        self.per, self.base = {}, {}

    def wait(self):
        if self.last is not None:
            self.eng.wait_ge(*self.last)

    def __call__(self, ins, sem=None):
        sem = self.own if sem is None else sem
        ins.then_inc(sem, 1)
        self.count[sem] = self.count.get(sem, 0) + 1
        if self.it is None:
            self.last = (sem, self.count[sem])
        else:
            per = self.per[sem]
            self.last = (sem, self.it * per + (self.count[sem] - self.lo * per))

    @contextmanager
    def loop(self, lo, hi, per):
        self.wait()
        self.last = None
        before = dict(self.count)
        with self.eng.Fori(lo, hi, 1) as it:
            self.it, self.lo, self.per = it, lo, per
            yield it
            self.wait()
        added = {s: n - before.get(s, 0) for s, n in self.count.items() if n != before.get(s, 0)}
        assert added == per, {s.name: n for s, n in added.items()}
        for s, n in per.items():
            self.count[s] = before.get(s, 0) + n * (hi - lo)
        self.it = self.last = None


def tile_of(buf, i):
    if isinstance(i, int):
        return buf[:, i, :]
    return buf[:, bass.ds(i, 1), :].rearrange("p a n -> p (a n)")


def column(buf, i):
    if isinstance(i, int):
        return buf[:, i:i + 1]
    return buf[:, bass.ds(i, 1)]


def f32(ap):
    return ap.bitcast(F32)


class Unit:

    def __init__(self, q, k, width, bias, scale, sink, v, out_part, out_cols, last, dst, heads_bias=None):
        self.q, self.k, self.width, self.bias, self.scale, self.sink = q, k, width, bias, scale, sink
        self.v, self.out_part, self.out_cols, self.last, self.dst = v, out_part, out_cols, last, dst
        self.heads_bias = heads_bias


def build(nc, stream, x_in, mem_in, consts_in, rope_in, params_in, ext_in, out):
    stages = {}
    slot = cb = 0
    prev = None
    for name, cbs, kt in STAGES:
        prev = stages[name] = Stage(name, cbs, kt, slot, cb, prev)
        slot += prev.slots
        cb += cbs
        assert prev.cbs % BANKS == 0
    n_slots = slot
    assert n_slots % RING == 0

    with ExitStack() as ctx:
        def sem(name):
            return ctx.enter_context(nc.semaphore(name))

        KB = 1024
        base = (nc.sbuf_base + 63) // 64 * 64

        def sb(name, shape, offset, dtype=F32):
            return nc.alloc_sbuf_tensor_at(name, [P] + list(shape), dtype, offset=base + offset)

        w_raw = sb("w_raw", [RING, D], 0)
        w_hi = sb("w_hi", [RING, SLOT_TILES, P], 16 * KB, F32R)
        w_lo = sb("w_lo", [RING, SLOT_TILES, P], 32 * KB, F32R)
        x_res = sb("x_res", [DT, T], 48 * KB)
        h_hi = sb("h_hi", [DT, T], 64 * KB, F32R)
        h_lo = sb("h_lo", [DT, T], 80 * KB, F32R)
        consts = sb("consts", [CONST_W], 96 * KB)
        at = 96 * KB + 4 * CONST_W
        params = sb("params", [PARAM_W], at)
        at += -(-4 * PARAM_W // 32) * 32
        small = {}
        for name, n in [("zero", 1), ("k_g8", 1), ("half_gate_b", 16), ("lower", 16), ("one_less", 16), ("eps_d", 1), ("eps_q", 1),
                        ("eps_v", 1), ("row_max", 2), ("neg_max", 2), ("row_sum", 2), ("sink_exp", 2), ("inv_sum", 2),
                        ("end_f", CHUNKS), ("end_b", CHUNKS), ("decay_f", CHUNKS), ("decay_b", CHUNKS),
                        ("lb_exp", 32)]:
            small[name] = sb(name, [n], at)
            at += -(-4 * n // 32) * 32
        at = (at + 63) // 64 * 64
        rope = sb("rope", [2, T], at)
        ffn_tmp = sb("ffn_tmp", [2, T], at)
        at += 4 * KB
        arena = at
        assert base + arena + 96 * KB <= nc.sbuf_usable_end, (base + arena + 96 * KB, nc.sbuf_usable_end)

        def ar(name, shape, kb, dtype=F32):
            return sb(name, shape, arena + kb * KB, dtype)

        square = ar("square", [2, T], 68)
        rms = ar("rms", [T], 72)
        rstd = ar("rstd", [T], 74)
        normed = ar("normed", [2, T], 76)
        qk = ar("qk", [2 * DT, T], 0)
        v_tok1 = ar("v_tok1", [BLOCKS, D], 32)
        o_all = ar("o_all", [12, T], 48)
        o_hi1 = ar("o_hi1", [DT, T], 32, F32R)
        o_lo1 = ar("o_lo1", [DT, T], 48, F32R)
        v_feat = ar("v_feat", [2, T], 64)
        toeplitz = ar("toeplitz", [2, T], 80)
        probs = ar("probs", [2, T], 84)
        probs_t = ar("probs_t", [2, T], 88)
        y_hi = ar("y_hi", [DT, T], 0, F32R)
        y_lo = ar("y_lo", [DT, T], 16, F32R)
        conv_tmp = ar("conv_tmp", [3, T], 32)
        gates = ar("gates", [2 * DT, T], 64)
        u_hi = ar("u_hi", [HALF, T], 0, F32R)
        u_lo = ar("u_lo", [HALF, T], 32, F32R)
        u_tmp = ar("u_tmp", [2, T], 64)
        mem = ar("mem", [DT, MEM], 80)
        mem_k = [ar(f"mem_k{i}", [X_HEADS, MEM], 80 + 8 * i) for i in range(2)]
        mem_v = [ar(f"mem_v{i}", [MEM // P, X_HEADS * P], 84 + 8 * i) for i in range(2)]
        o2 = ar("o2", [12, T], 0)
        o_lo2 = ar("o_lo2", [12, T], 0, F32R)
        o_hi2 = ar("o_hi2", [12, T], 24, F32R)
        q_win = ar("q_win", [DT, T], 24)
        k_win = ar("k_win", [2, T], 40)
        v_win = ar("v_win", [BLOCKS, KV_HEADS * HEAD_DIM], 44)
        xq = ar("xq", [X_HEADS, T], 48)
        probs2 = ar("probs2", [2, T], 56)
        probs2_t = ar("probs2_t", [2, T], 60)
        y_all = sb("y_all", [DT, T], 64 * KB)
        hid_hi = ar("hid_hi", [FF2, T], 0, F32R)
        hid_lo = ar("hid_lo", [FF2, T], 44, F32R)
        (hg_q, hg_gate, hg_lf_f, hg_lf_b, hg_k_f, hg_k_b, hg_b_f, hg_b_b, hg_qd_f, hg_qd_b, hg_kd_f, hg_kd_b,
         hg_v_feat) = [ar(n, [T], 24 + 2 * i) for i, n in enumerate(
             ["hg_q", "hg_gate", "hg_lf_f", "hg_lf_b", "hg_k_f", "hg_k_b", "hg_b_f", "hg_b_b", "hg_qd_f", "hg_qd_b",
              "hg_kd_f", "hg_kd_b", "hg_v_feat"])]
        hg_v, hg_ke_f, hg_ke_b, hg_s_f, hg_s_b = [ar(n, [BLOCKS, P], 50 + 2 * i) for i, n in enumerate(
            ["hg_v", "hg_ke_f", "hg_ke_b", "hg_s_f", "hg_s_b"])]
        hg_state_f = ar("hg_state_f", [2 * GROUP, P], 60)
        hg_state_b = ar("hg_state_b", [2 * GROUP, P], 64)
        hg_vm = ar("hg_vm", [BLOCKS, BLOCK_CHUNKS, P], 80)

        def const(name, n=P):
            c = CONST_COLS[name]
            return consts[:, c:c + n]

        def param(name, i=0):
            c = PARAM_COLS[name]
            if isinstance(i, int):
                return params[:, c + i:c + i + 1]
            return params[:, bass.ds(i + c, 1)]

        acc = [ctx.enter_context(nc.psum_tensor(f"acc{i}", [P, T], F32)) for i in range(BANKS)]
        ps_s = [ctx.enter_context(nc.psum_tensor(f"ps_s{i}", [P, T], F32)) for i in range(2)]
        ps_t = ctx.enter_context(nc.psum_tensor("ps_t", [P, T], F32))
        ps_o = ctx.enter_context(nc.psum_tensor("ps_o", [P, T], F32))

        small_in = sem("small_in")
        mem_loaded = sem("mem_loaded")
        loaded = [sem(f"loaded{i}") for i in range(RING)]
        bias_in = [sem(f"bias_in{i}") for i in range(2)]
        hi_made = sem("hi_made")
        split_made = sem("split_made")
        slot_done = sem("slot_done")
        for s in stages.values():
            s.free = sem(f"free_{s.name}")
        dve_own = sem("dve_own")
        act_own = sem("act_own")
        setup_done = sem("setup_done")
        setup_act = sem("setup_act")
        h_ready = sem("h_ready")
        o_ready = sem("o_ready")
        y_ready = sem("y_ready")
        m_ready = sem("m_ready")
        u_ready = sem("u_ready")
        hid_ready = sem("hid_ready")
        x_ready = sem("x_ready")
        sq_ready = sem("sq_ready")
        sq_used = sem("sq_used")
        rms_ready = sem("rms_ready")
        rms_used = sem("rms_used")
        vt_done = sem("vt_done")
        v_ready = sem("v_ready")
        rope_rot = sem("rope_rot")
        rope_done = sem("rope_done")
        s_ready = sem("s_ready")
        s_used = sem("s_used")
        max_ready = sem("max_ready")
        p_ready = sem("p_ready")
        sink_ready = sem("sink_ready")
        pn_ready = sem("pn_ready")
        pt_made = sem("pt_made")
        pt_ready = sem("pt_ready")
        pv_done = sem("pv_done")
        o_taken = sem("o_taken")
        gate_ready = sem("gate_ready")
        gelu_ready = sem("gelu_ready")
        hg_f = sem("hg_f")
        hg_ln = sem("hg_ln")
        hg_cum = sem("hg_cum")
        hg_exp = sem("hg_exp")
        hg_rest = sem("hg_rest")
        hg_rest_exp = sem("hg_rest_exp")
        hg_dec = sem("hg_dec")
        hg_ket = sem("hg_ket")
        hg_ke = sem("hg_ke")
        hg_st = sem("hg_st")
        hg_s = sem("hg_s")
        hg_vmask = sem("hg_vmask")
        hg_u = sem("hg_u")
        hg_chain = sem("hg_chain")
        hg_inter = sem("hg_inter")
        stored = sem("stored")

        units1, units_win, units_x = [], [], [[], []]
        for h in range(HEADS):
            off = HEAD_DIM * (h % 2)
            for t in range(BLOCKS):
                units1.append(Unit(
                    q=qk[off:off + HEAD_DIM, h // 2, t * P:(t + 1) * P], k=qk[off:off + HEAD_DIM, DT + h // 2, 0:(t + 1) * P],
                    width=(t + 1) * P, bias=toeplitz[:, h % 2, T - (t + 1) * P:T], scale=1.0, sink=None,
                    v=[v_tok1[:, b, h * HEAD_DIM:(h + 1) * HEAD_DIM] for b in range(t + 1)],
                    out_part=off, out_cols=(t * P, (t + 1) * P), last=h % 2 == 1 and t == BLOCKS - 1,
                    dst=o_all[:, h // 2, :], heads_bias=(h, t == 0)))
            kv = 2 * (h // 8) + h % 2
            for t in range(BLOCKS):
                lo, hi = max(0, t - 1), min(BLOCKS, t + 2)
                m = CONST_COLS["win_mask"] + (lo - t + 1) * P
                units_win.append(Unit(
                    q=q_win[off:off + HEAD_DIM, h // 2, t * P:(t + 1) * P], k=k_win[off:off + HEAD_DIM, kv // 2, lo * P:hi * P],
                    width=(hi - lo) * P, bias=consts[:, m:m + (hi - lo) * P], scale=1.0, sink=param("sink", h),
                    v=[v_win[:, b, kv * HEAD_DIM:(kv + 1) * HEAD_DIM] for b in range(lo, hi)],
                    out_part=off, out_cols=(t * P, (t + 1) * P), last=h % 2 == 1 and t == BLOCKS - 1,
                    dst=o2[:, h // 2, :]))
        for layer in range(2):
            for h in range(X_HEADS):
                for t in range(BLOCKS):
                    units_x[layer].append(Unit(
                        q=xq[:, h, t * P:(t + 1) * P], k=mem_k[layer][:, h, :], width=MEM, bias=const("zeros", MEM),
                        scale=float(P) ** -0.5, sink=None, v=[mem_v[layer][:, b, h * P:(h + 1) * P] for b in range(MEM // P)],
                        out_part=0, out_cols=(t * P, (t + 1) * P), last=t == BLOCKS - 1, dst=o2[:, DT + h, :]))

        block = ctx.enter_context(nc.Block())

        @block.sync
        def _(sp):
            sp.dma_start(params[:], params_in).then_inc(small_in, 16)
            sp.dma_start(consts[:], consts_in).then_inc(small_in, 16)
            sp.dma_start(x_res[:], x_in).then_inc(small_in, 16)
            for s in range(RING):
                sp.dma_start(w_raw[:, s, :], stream[s]).then_inc(loaded[s], 16)
            sp.dma_start(rope[:], rope_in).then_inc(small_in, 16)
            with sp.Fori(1, n_slots // RING, 1) as it:
                for s in range(RING):
                    sp.wait_ge(split_made, it * RING + (s + 1 - RING))
                    sp.dma_start(w_raw[:, s, :], stream[bass.ds(it * RING + s, 1)].rearrange("a p n -> p (a n)"))\
                        .then_inc(loaded[s], 16)
            sp.wait_ge(x_ready, 4 * DT)
            sp.dma_start(out, x_res[:]).then_inc(stored, 16)
            sp.wait_ge(stored, 16)

        @block.gpsimd
        def _(pool):
            def split(it, s):
                pool.wait_ge(loaded[s], it * 16 + 16)
                if not isinstance(it, int):
                    pool.wait_ge(slot_done, it * RING + (s + 1 - RING))
                raw = w_raw[:, s, :]
                hi = w_hi[:, s, :, :].rearrange("p t n -> p (t n)")
                lo = w_lo[:, s, :, :].rearrange("p t n -> p (t n)")
                nc.gpsimd.tensor_tensor(hi, raw, small["zero"][:].to_broadcast([P, D]), ALU.add).then_inc(hi_made, 1)
                pool.wait_ge(hi_made, it * RING + (s + 2))
                nc.gpsimd.tensor_tensor(lo, raw, f32(hi), ALU.subtract).then_inc(split_made, 1)

            nc.gpsimd.memset(small["zero"][:], 0.0).then_inc(hi_made, 1)
            pool.wait_ge(hi_made, 1)
            for s in range(RING):
                split(0, s)
            with pool.Fori(1, n_slots // RING, 1) as it:
                for s in range(RING):
                    split(it, s)

        @block.tensor
        def _(pe):
            n = {"sq": 0, "rms": 0, "v": 0, "rope": 0, "unit": 0, "o": 0, "h": 0}
            t_free = []

            def take_t(sem_, value):
                if t_free:
                    pe.wait_ge(*t_free[0])
                t_free[:] = [(sem_, value)]

            def products(st, it, body, j, x_hi, x_lo, cols=T, ready=None):
                c = it * body + j
                if isinstance(c, int) and c < BANKS:
                    if st.prev is not None:
                        pe.wait_ge(st.prev.free, st.prev.cbs - BANKS + c + 1)
                else:
                    pe.wait_ge(st.free, c - (BANKS - 1))
                ps = acc[st.bank(j)][:, 0:cols]
                for k in range(st.kt):
                    tile = j * st.kt + k
                    s = (st.first_slot + tile // SLOT_TILES) % RING
                    if tile % SLOT_TILES == 0:
                        pe.wait_ge(split_made, it * (body * st.kt // SLOT_TILES) + (st.first_slot + tile // SLOT_TILES + 1))
                    if ready is not None:
                        ready(k)
                    hi, lo = w_hi[:, s, tile % SLOT_TILES, :], w_lo[:, s, tile % SLOT_TILES, :]
                    nc.tensor.matmul(ps, hi, x_hi[:, k, 0:cols], start=(k == 0), stop=False)
                    nc.tensor.matmul(ps, hi, x_lo[:, k, 0:cols], start=False, stop=False)
                    mm = nc.tensor.matmul(ps, lo, x_hi[:, k, 0:cols], start=False, stop=(k == st.kt - 1))
                    if tile % SLOT_TILES == SLOT_TILES - 1:
                        mm.then_inc(slot_done, 1)

            def block_at(st, c, x_hi, x_lo, ready=None, cols=T):
                products(st, 0, st.cbs, c, x_hi, x_lo, cols, ready if c == 0 else None)

            def whole(st, body, x_hi, x_lo, cols=T, ready=None):
                for j in range(body):
                    products(st, 0, body, j, x_hi, x_lo, cols, ready if j == 0 else None)
                if st.cbs > body:
                    assert body % BANKS == 0 and body * st.kt // SLOT_TILES % RING == 0
                    with pe.Fori(1, st.cbs // body, 1) as it:
                        for j in range(body):
                            products(st, it, body, j, x_hi, x_lo, cols)

            def waits_for(sem_, first):
                return lambda k: pe.wait_ge(sem_, first + k + 1)

            def sum_squares(tiles, ones, cols=T, sq=square):
                n["rms"] += 1
                take_t(rms_ready, n["rms"])
                for i in range(tiles):
                    pe.wait_ge(sq_ready, n["sq"] + 1)
                    nc.tensor.matmul(ps_t[:, 0:cols], ones, sq[:, n["sq"] % 2, 0:cols],
                                     start=(i == 0), stop=(i == tiles - 1)).then_inc(sq_used, 1)
                    n["sq"] += 1

            def norm(cols=T, sq=square):
                if n["rms"] == 0:
                    pe.wait_ge(small_in, 64)
                sum_squares(DT, const("ones"), cols, sq)

            def transpose_v(st, c, blocks=BLOCKS):
                n["v"] += 1
                take_t(v_ready, n["v"])
                pe.wait_ge(st.free, c + 1)
                src = v_feat[:, c % 2, :]
                for b in range(blocks):
                    mm = nc.tensor.transpose(ps_t[:, b * P:(b + 1) * P], src[:, b * P:(b + 1) * P], const("ident"))
                mm.then_inc(vt_done, 1)

            def rotate(st, i):
                n["rope"] += 1
                take_t(rope_done, i + 1)
                pe.wait_ge(st.free, i + 1)
                nc.tensor.matmul(ps_t[:], const("rot"), normed[:, i % 2, :], start=True, stop=True).then_inc(rope_rot, 1)

            def attention(units, p_t):
                u0 = n["unit"]

                def scores(i):
                    u = units[i]
                    if u0 + i >= 2:
                        pe.wait_ge(s_used, u0 + i - 1)
                    nc.tensor.matmul(ps_s[(u0 + i) % 2][:, 0:u.width], u.q, u.k, start=True, stop=True).then_inc(s_ready, 1)

                def turn(i):
                    u = units[i]
                    take_t(pt_ready, u0 + i + 1)
                    pe.wait_ge(pn_ready, u0 + i + 1)
                    src = (probs if units is units1 else probs2)[:, (u0 + i) % 2, :]
                    for b in range(u.width // P):
                        mm = nc.tensor.transpose(ps_t[:, b * P:(b + 1) * P], src[:, b * P:(b + 1) * P], const("ident"))
                    mm.then_inc(pt_made, 1)

                def weigh(i):
                    u = units[i]
                    if n["o"]:
                        pe.wait_ge(o_taken, n["o"])
                    pe.wait_ge(pt_ready, u0 + i + 1)
                    rows = u.v[0].shape[1]
                    for b in range(u.width // P):
                        mm = nc.tensor.matmul(ps_o[u.out_part:u.out_part + rows, u.out_cols[0]:u.out_cols[1]], u.v[b],
                                              p_t[:, (u0 + i) % 2, b * P:(b + 1) * P],
                                              start=(b == 0), stop=(b == u.width // P - 1))
                    mm.then_inc(pv_done, 1)
                    if u.last:
                        n["o"] += 1

                scores(0)
                for i in range(len(units)):
                    if i + 1 < len(units):
                        scores(i + 1)
                    turn(i)
                    if i:
                        weigh(i - 1)
                weigh(len(units) - 1)
                n["unit"] += len(units)

            norm()
            st = stages["qkv"]
            for c in range(st.cbs):
                block_at(st, c, h_hi, h_lo, waits_for(h_ready, n["h"]))
                if 1 <= c <= 2 * DT:
                    sum_squares(1, const("pair_ones"))
                if c > 2 * DT:
                    transpose_v(st, c - 1)
            transpose_v(st, st.cbs - 1)
            n["h"] += DT
            pe.wait_ge(v_ready, n["v"])
            attention(units1, probs_t)
            whole(stages["conv"], 12, h_hi, h_lo)
            whole(stages["gate"], 4, h_hi, h_lo)
            st = stages["proj"]

            def proj(it):
                for j in range(4):
                    if j % 2 == 0:
                        products(st, it, 4, j, o_hi1, o_lo1, ready=waits_for(o_ready, 0) if isinstance(it, int) and j == 0 else None)
                    else:
                        products(st, it, 4, j, y_hi, y_lo, ready=waits_for(y_ready, 0) if isinstance(it, int) and j == 1 else None)

            proj(0)
            with pe.Fori(1, st.cbs // 4, 1) as it:
                proj(it)
            whole(stages["out"], 4, h_hi, h_lo, ready=waits_for(m_ready, 0))
            norm()
            for half in range(2):
                whole(stages[f"up{half}"], 4, h_hi, h_lo, ready=waits_for(h_ready, n["h"]))
                whole(stages[f"down{half}"], 4, u_hi, u_lo, ready=waits_for(u_ready, half * HALF))
            n["h"] += DT
            norm(MEM)
            st = stages["memkv"]
            for c in range(st.cbs):
                block_at(st, c, h_hi, h_lo, waits_for(h_ready, n["h"]), MEM)
                if c and (c - 1) % 8 >= 4:
                    transpose_v(st, c - 1, MEM // P)
            transpose_v(st, st.cbs - 1, MEM // P)
            n["h"] += DT

            def conv_mlp(layer):
                norm()
                whole(stages[f"ffn_in{layer}"], 4, h_hi, h_lo, ready=waits_for(h_ready, n["h"]))
                n["h"] += DT
                st = stages[f"ffn_out{layer}"]
                for c in range(st.cbs):
                    block_at(st, c, hid_hi, hid_lo, waits_for(hid_ready, layer * FF2))
                norm(sq=ffn_tmp)

            def mixer_out(layer):
                st = stages["ab"[layer] + "_out"]
                for c in range(st.cbs):
                    block_at(st, c, o_hi2, o_lo2, waits_for(o_ready, DT + 12 * layer))
                norm()

            norm()
            st = stages["a_in"]
            for c in range(st.cbs):
                block_at(st, c, h_hi, h_lo, waits_for(h_ready, n["h"]))
                if 1 <= c <= 10:
                    rotate(st, c - 1)
                elif 11 <= c <= 12:
                    transpose_v(st, c - 1)
            n["h"] += DT
            pe.wait_ge(v_ready, n["v"])
            pe.wait_ge(rope_done, n["rope"])
            attention(units_win, probs2_t)
            pe.wait_ge(st.free, st.cbs)
            attention(units_x[0], probs2_t)
            mixer_out(0)
            conv_mlp(0)
            norm()
            st = stages["b_in"]
            for c in range(X_HEADS):
                block_at(st, c, h_hi, h_lo, waits_for(h_ready, n["h"]))
            n["h"] += DT
            pe.wait_ge(st.free, X_HEADS)
            attention(units_x[1], probs2_t)
            for h in range(HG_HEADS):
                for c in range(X_HEADS + 5 * h, X_HEADS + 5 * (h + 1)):
                    block_at(st, c, h_hi, h_lo)
                n["v"] += 1
                take_t(v_ready, n["v"])
                pe.wait_ge(st.free, X_HEADS + 5 * h + 2)
                for b in range(BLOCKS):
                    mm = nc.tensor.transpose(ps_t[:, b * P:(b + 1) * P], hg_v_feat[:, b * P:(b + 1) * P], const("ident"))
                mm.then_inc(vt_done, 1)
                for d, (kd, qd) in enumerate([(hg_kd_f, hg_qd_f), (hg_kd_b, hg_qd_b)]):
                    pe.wait_ge(hg_dec, 2 * h + d + 1)
                    if h:
                        pe.wait_ge(hg_chain, 8 * h)
                    else:
                        pe.wait_ge(s_used, n["unit"])
                    for b in range(BLOCKS):
                        mm = nc.tensor.matmul(ps_s[d][:, b * P:(b + 1) * P], kd[:, b * P:(b + 1) * P],
                                              qd[:, b * P:(b + 1) * P], start=True, stop=True)
                    mm.then_inc(hg_st, 1)
                for d, ke in enumerate([hg_b_f, hg_b_b]):
                    take_t(hg_ke, 2 * h + d + 1)
                    for b in range(BLOCKS):
                        mm = nc.tensor.transpose(ps_t[:, b * P:(b + 1) * P], ke[:, b * P:(b + 1) * P], const("ident"))
                    mm.then_inc(hg_ket, 1)
                pe.wait_ge(o_taken, n["o"])
                for d, s_ in enumerate([hg_s_f, hg_s_b]):
                    pe.wait_ge(hg_s, 2 * h + d + 1)
                    for b in range(BLOCKS):
                        nc.tensor.matmul(ps_o[:, b * P:(b + 1) * P], hg_v[:, b, :], s_[:, b, :],
                                         start=(d == 0 and b == 0), stop=False, skip_group_check=True)
                pe.wait_ge(hg_ke, 2 * h + 2)
                pe.wait_ge(hg_vmask, h + 1)

                def update(g):
                    if g:
                        pe.wait_ge(hg_chain, 8 * h + g)
                    for d, ke in enumerate([hg_ke_f, hg_ke_b]):
                        gg = g if d == 0 else CHUNKS // GROUP - 1 - g
                        mm = nc.tensor.matmul(ps_s[d][:], ke[:, gg // 2, :],
                                              hg_vm[:, gg // 2, GROUP * (gg % 2):GROUP * (gg % 2 + 1), :],
                                              start=True, stop=True)
                    mm.then_inc(hg_u, 1)

                def inter(g):
                    pe.wait_ge(hg_chain, 8 * h + g + 1)
                    for c in range(GROUP * g, GROUP * (g + 1)):
                        if c == 0:
                            continue
                        for d, (state, qd) in enumerate([(hg_state_f, hg_qd_f), (hg_state_b, hg_qd_b)]):
                            at_ = HG_CHUNK * (c if d == 0 else CHUNKS - 1 - c)
                            mm = nc.tensor.matmul(ps_o[:, at_:at_ + HG_CHUNK], state[:, c % (2 * GROUP), :],
                                                  qd[:, at_:at_ + HG_CHUNK], start=False,
                                                  stop=(c == CHUNKS - 1 and d == 1), skip_group_check=True)
                    mm.then_inc(hg_inter, 1)

                update(0)
                for g in range(CHUNKS // GROUP):
                    if g + 1 < CHUNKS // GROUP:
                        update(g + 1)
                    inter(g)
                n["o"] += 1
                sum_squares(1, const("ones"))
            mixer_out(1)
            conv_mlp(1)

        @block.scalar
        def _(act):
            n = {"sq": 0, "rms": 0, "unit": 0, "bias": 0, "gelu": 0}

            def sum_squares_root(srcs, scale, eps, cols=T, sq=square):
                for wait_src, src in srcs:
                    if n["sq"] >= 2:
                        act.wait_ge(sq_used, n["sq"] - 1)
                    wait_src()
                    nc.scalar.activation(sq[:, n["sq"] % 2, 0:cols], src, ACT.Square).then_inc(sq_ready, 1)
                    n["sq"] += 1
                act.wait_ge(sq_used, n["sq"])
                if n["rms"]:
                    act.wait_ge(rms_used, n["rms"])
                nc.scalar.activation(rms[:, 0:cols], ps_t[:, 0:cols], ACT.Sqrt, scale=scale, bias=eps)\
                    .then_inc(rms_ready, 1)
                n["rms"] += 1

            def norm(src, sem_, first, cols=T, sq=square):
                sum_squares_root([((lambda i=i: act.wait_ge(sem_, first + i + 1)), src[:, i, 0:cols]) for i in range(DT)],
                                 1.0 / D, small["eps_d"][:], cols, sq)

            def attention(units, p, p_t):
                u0 = n["unit"]

                def exps(i):
                    u, b = units[i], (u0 + i) % 2
                    act.wait_ge(max_ready, u0 + i + 1)
                    nc.scalar.activation(p[:, b, 0:u.width], p[:, b, 0:u.width], ACT.Exp, bias=small["neg_max"][:, b:b + 1],
                                         accum_out=small["row_sum"][:, b:b + 1]).then_inc(p_ready, 1)
                    if u.sink is not None:
                        nc.scalar.activation(small["sink_exp"][:, b:b + 1], u.sink, ACT.Exp,
                                             bias=small["neg_max"][:, b:b + 1]).then_inc(sink_ready, 1)

                def take(i):
                    u, b = units[i], (u0 + i) % 2
                    act.wait_ge(pt_made, u0 + i + 1)
                    if u0 + i >= 2:
                        act.wait_ge(pv_done, u0 + i - 1)
                    nc.scalar.activation(p_t[:, b, 0:u.width], ps_t[:, 0:u.width], ACT.Copy).then_inc(pt_ready, 1)

                def load_bias(i):
                    h, first = units[i].heads_bias
                    if not first:
                        return
                    if h >= 2:
                        act.wait_ge(s_used, u0 + i - BLOCKS)
                    act.dma_start(toeplitz[:, h % 2, :], ext_in[h])\
                        .then_inc(bias_in[h % 2], 16)

                biased = units[0].heads_bias is not None
                if biased:
                    load_bias(0)
                    load_bias(BLOCKS)
                exps(0)
                for i in range(len(units)):
                    if i + 1 < len(units):
                        exps(i + 1)
                    if biased and i + 1 + BLOCKS < len(units) and i + 1 >= BLOCKS:
                        load_bias(i + 1 + BLOCKS)
                    take(i)
                n["unit"] += len(units)

            act.wait_ge(setup_done, 1)
            nc.scalar.activation(small["lb_exp"][:], small["lb_exp"][:], ACT.Exp).then_inc(setup_act, 1)
            act.wait_ge(setup_done, 2)

            sum_squares_root([((lambda: act.wait_ge(small_in, 64)), x_res[:, i, :]) for i in range(DT)],
                             1.0 / D, small["eps_d"][:])
            st = stages["qkv"]
            for c in range(2 * DT):
                sum_squares_root([((lambda c=c: act.wait_ge(slot_done, st.made(c))), acc[st.bank(c)][:])], 1.0,
                                 small["eps_q"][:])
            attention(units1, probs, probs_t)
            st = stages["gate"]

            def gate(it, j):
                c = it * 4 + j
                act.wait_ge(slot_done, st.made(c))
                nc.scalar.activation(tile_of(gates, c), acc[st.bank(j)][:], ACT.Tanh, scale=0.5,
                                     bias=column(small["half_gate_b"], c)).then_inc(st.free, 1)

            act.wait_ge(y_ready, DT)
            for c in range(st.cbs):
                gate(0, c)
            norm(x_res, stages["out"].free, 0)
            act.dma_start(mem[:], mem_in).then_inc(mem_loaded, 16)
            act.wait_ge(mem_loaded, 16)
            sum_squares_root([((lambda: None), mem[:, i, :]) for i in range(DT)], 1.0 / D, small["eps_d"][:], MEM)

            def gelus(layer):
                g0 = layer * FF2
                for i in range(FF2):
                    act.wait_ge(stages[f"ffn_in{layer}"].free, 2 * i + 1)
                    t_ = ffn_tmp[:, i % 2, :]
                    nc.scalar.activation(t_, t_, ACT.Gelu_apprx_tanh).then_inc(gelu_ready, 1)

            norm(x_res, stages["down1"].free, 0)
            attention(units_win, probs2, probs2_t)
            attention(units_x[0], probs2, probs2_t)
            norm(y_all, stages["a_out"].free, 0)
            norm(x_res, x_ready, 0)
            gelus(0)
            norm(y_all, stages["ffn_out0"].free, 0, sq=ffn_tmp)
            norm(x_res, x_ready, DT)
            st = stages["b_in"]
            for c in range(X_HEADS):
                act.wait_ge(slot_done, st.made(c))
                nc.scalar.activation(xq[:, c, :], acc[st.bank(c)][:], ACT.Copy).then_inc(st.free, 1)
            attention(units_x[1], probs2, probs2_t)
            for h in range(HG_HEADS):
                c0 = X_HEADS + 5 * h
                act.wait_ge(o_taken, 8 + 8 + 4 + 4 + h)
                for j, (dst, func) in enumerate([(hg_q, ACT.Silu), (hg_v_feat, ACT.Copy), (hg_lf_f, ACT.Sigmoid),
                                                 (hg_lf_b, ACT.Sigmoid), (hg_gate, ACT.Silu)]):
                    act.wait_ge(slot_done, st.made(c0 + j))
                    nc.scalar.activation(dst[:], acc[st.bank(c0 + j)][:], func).then_inc(st.free, 1)
                for d, lf in enumerate([hg_lf_f, hg_lf_b]):
                    act.wait_ge(hg_f, 2 * h + d + 1)
                    nc.scalar.activation(lf[:], lf[:], ACT.Ln).then_inc(hg_ln, 1)
                for d, (b_, qd, kd) in enumerate([(hg_b_f, hg_qd_f, hg_kd_f), (hg_b_b, hg_qd_b, hg_kd_b)]):
                    act.wait_ge(hg_cum, 2 * h + d + 1)
                    nc.scalar.activation(qd[:], b_[:], ACT.Exp).then_inc(hg_exp, 1)
                    nc.scalar.activation(kd[:], b_[:], ACT.Exp, scale=-1.0).then_inc(hg_exp, 1)
                for d, (ke, end, decay) in enumerate([(hg_b_f, "end_f", "decay_f"), (hg_b_b, "end_b", "decay_b")]):
                    act.wait_ge(hg_rest, 2 * h + d + 1)
                    nc.scalar.activation(small[decay][:], small[end][:], ACT.Exp).then_inc(act_own, 1)
                    nc.scalar.activation(ke[:], ke[:], ACT.Exp).then_inc(hg_rest_exp, 1)
                sum_squares_root([((lambda h=h: act.wait_ge(hg_inter, 8 * h + 8)), ps_o[:])], 1.0 / P, small["eps_v"][:])
            norm(y_all, stages["b_out"].free, 0)
            norm(x_res, x_ready, 2 * DT)
            gelus(1)
            norm(y_all, stages["ffn_out1"].free, 0, sq=ffn_tmp)

        @block.vector
        def _(dve):
            step = Order(dve, dve_own)
            n = {"rms": 0, "v": 0, "rope": 0, "unit": 0, "o": 0, "pv": 0, "sink": 0}

            def split(src, hi, lo, sem_):
                step.wait()
                step(nc.vector.tensor_copy(hi, src))
                step.wait()
                step(nc.vector.tensor_tensor(lo, src, f32(hi), ALU.subtract), sem_)

            def invert_rms(cols=T):
                n["rms"] += 1
                dve.wait_ge(rms_ready, n["rms"])
                step.wait()
                step(nc.vector.reciprocal(rstd[:, 0:cols], rms[:, 0:cols]), rms_used)

            def norm(src, gain, cols=T):
                invert_rms(cols)
                for i in range(DT):
                    step.wait()
                    t_ = normed[:, i % 2, 0:cols]
                    step(nc.vector.scalar_tensor_tensor(t_, src[:, i, 0:cols], gain(i), rstd[:, 0:cols], ALU.mult, ALU.mult))
                    split(t_, h_hi[:, i, 0:cols], h_lo[:, i, 0:cols], h_ready)

            def add_norm(gain):
                invert_rms()
                for i in range(DT):
                    step.wait()
                    t_ = normed[:, i % 2, :]
                    step(nc.vector.scalar_tensor_tensor(t_, y_all[:, i, :], gain(i), rstd[:], ALU.mult, ALU.mult))
                    step.wait()
                    step(nc.vector.tensor_tensor(x_res[:, i, :], x_res[:, i, :], t_, ALU.add), x_ready)

            def take(st, c, dst, scale=None):
                dve.wait_ge(slot_done, st.made(c))
                step.wait()
                src = acc[st.bank(c)][:, 0:dst.shape[-1]]
                if scale is None:
                    step(nc.vector.tensor_copy(dst, src), st.free)
                else:
                    step(nc.vector.tensor_scalar(dst, src, scale, None, ALU.mult), st.free)

            def feat_v(st, c, cols=T):
                if n["v"] >= 1:
                    dve.wait_ge(vt_done, n["v"])
                take(st, c, v_feat[:, c % 2, 0:cols])

            def tok_v(dst):
                n["v"] += 1
                dve.wait_ge(vt_done, n["v"])
                step.wait()
                blocks = dst.shape[1]
                step(nc.vector.tensor_copy(dst, ps_t[:, 0:blocks * P].rearrange("p (b n) -> p b n", n=P)), v_ready)

            def attention(units, p):
                u0 = n["unit"]

                def top(i):
                    u, b = units[i], (u0 + i) % 2
                    dve.wait_ge(s_ready, u0 + i + 1)
                    if u.heads_bias is not None and u.heads_bias[1]:
                        dve.wait_ge(bias_in[u.heads_bias[0] % 2], 16 * (u.heads_bias[0] // 2 + 1))
                        if i == 0 or units is units1:
                            step.wait()
                            step(nc.vector.memset(toeplitz[0:CHUNK, u.heads_bias[0] % 2, T - CHUNK:T], NEG))
                    if u0 + i >= 2:
                        dve.wait_ge(pt_made, u0 + i - 1)
                    step.wait()
                    step(nc.vector.tensor_tensor_reduce(p[:, b, 0:u.width], ps_s[b][:, 0:u.width], u.bias, u.scale, -3e38,
                                                        ALU.add, ALU.max, small["row_max"][:, b:b + 1]), s_used)
                    step.wait()
                    if u.sink is None:
                        step(nc.vector.tensor_scalar(small["neg_max"][:, b:b + 1], small["row_max"][:, b:b + 1], -1.0, None,
                                                     ALU.mult), max_ready)
                    else:
                        step(nc.vector.tensor_scalar(small["neg_max"][:, b:b + 1], small["row_max"][:, b:b + 1], u.sink, -1.0,
                                                     ALU.max, ALU.mult), max_ready)

                def scale(i):
                    u, b = units[i], (u0 + i) % 2
                    total = small["row_sum"][:, b:b + 1]
                    dve.wait_ge(p_ready, u0 + i + 1)
                    if u.sink is not None:
                        n["sink"] += 1
                        dve.wait_ge(sink_ready, n["sink"])
                        step.wait()
                        step(nc.vector.tensor_scalar(total, total, small["sink_exp"][:, b:b + 1], None, ALU.add))
                    step.wait()
                    step(nc.vector.reciprocal(small["inv_sum"][:, b:b + 1], total))
                    step.wait()
                    step(nc.vector.tensor_scalar(p[:, b, 0:u.width], p[:, b, 0:u.width], small["inv_sum"][:, b:b + 1], None,
                                                 ALU.mult), pn_ready)

                def out_of(i):
                    if units[i].last:
                        dve.wait_ge(pv_done, u0 + i + 1)
                        step.wait()
                        step(nc.vector.tensor_copy(units[i].dst, ps_o[:]), o_taken)

                top(0)
                for i in range(len(units)):
                    if i + 1 < len(units):
                        top(i + 1)
                    scale(i)
                    if i:
                        out_of(i - 1)
                out_of(len(units) - 1)
                n["unit"] += len(units)

            dve.wait_ge(small_in, 64)
            lb = lambda d, l: params[:, PARAM_COLS["lb_logits"] + 16 * d + 8 * l:PARAM_COLS["lb_logits"] + 16 * d + 8 * l + 8]
            ex = lambda d, l: small["lb_exp"][:, 16 * d + 8 * l:16 * d + 8 * l + 8]
            for d in range(2):
                step.wait()
                step(nc.vector.tensor_tensor(small["lower"][:, 8 * d:8 * d + 8], lb(d, 0), lb(d, 1), ALU.max))
                for l in range(2):
                    step.wait()
                    step(nc.vector.tensor_tensor(ex(d, l), lb(d, l), small["lower"][:, 8 * d:8 * d + 8], ALU.subtract),
                         setup_done if d == 1 and l == 1 else None)
            for dst, value in [("eps_d", EPS), ("eps_q", HEAD_DIM * EPS), ("eps_v", EPS)]:
                step.wait()
                step(nc.vector.memset(small[dst][:], value))
            step.wait()
            step(nc.vector.tensor_scalar(small["k_g8"][:], param("k_g"), float(HEAD_DIM) ** 0.5, None, ALU.mult))
            step.wait()
            c = PARAM_COLS["b_gate"]
            step(nc.vector.tensor_scalar(small["half_gate_b"][:], params[:, c:c + 16], 0.5, None, ALU.mult), setup_done)
            dve.wait_ge(setup_act, 1)
            for d in range(2):
                low, one = small["lower"][:, 8 * d:8 * d + 8], small["one_less"][:, 8 * d:8 * d + 8]
                step.wait()
                step(nc.vector.tensor_tensor(low, ex(d, 0), ex(d, 1), ALU.add))
                step.wait()
                step(nc.vector.reciprocal(one, low))
                step.wait()
                step(nc.vector.tensor_tensor(low, ex(d, 1), one, ALU.mult))
                step.wait()
                step(nc.vector.tensor_scalar(one, low, -1.0, 1.0, ALU.mult, ALU.add))

            norm(x_res, lambda i: param("norm1_g", i))
            st = stages["qkv"]
            for c in range(2 * DT):
                invert_rms()
                step.wait()
                step(nc.vector.scalar_tensor_tensor(qk[:, c, :], acc[st.bank(c)][:], param("q_g") if c < DT else
                                                    small["k_g8"][:], rstd[:], ALU.mult, ALU.mult), st.free)
            for c in range(2 * DT, st.cbs):
                feat_v(st, c)
                tok_v(v_tok1[:, :, (c - 2 * DT) * P:(c - 2 * DT + 1) * P])
            attention(units1, probs)

            st = stages["conv"]
            cg, u, t_ = conv_tmp[:, 0, :], conv_tmp[:, 1, :], conv_tmp[:, 2, :]
            for i in range(DT):
                w = [param("conv_w", 8 * k + i) for k in range(3)]
                take(st, 3 * i, cg)
                dve.wait_ge(slot_done, st.made(3 * i + 1))
                step.wait()
                step(nc.vector.tensor_tensor(u, acc[st.bank(3 * i + 1)][:], cg, ALU.mult), st.free)
                step.wait()
                step(nc.vector.tensor_scalar(t_, u, w[2], param("conv_b", i), ALU.mult, ALU.add))
                step.wait()
                step(nc.vector.scalar_tensor_tensor(t_[:, 1:T], u[:, 0:T - 1], w[1], t_[:, 1:T], ALU.mult, ALU.add))
                step.wait()
                step(nc.vector.scalar_tensor_tensor(t_[:, 2:T], u[:, 0:T - 2], w[0], t_[:, 2:T], ALU.mult, ALU.add))
                dve.wait_ge(slot_done, st.made(3 * i + 2))
                step.wait()
                step(nc.vector.tensor_tensor(t_, acc[st.bank(3 * i + 2)][:], t_, ALU.mult), st.free)
                split(t_, y_hi[:, i, :], y_lo[:, i, :], y_ready)
            for i in range(DT):
                split(o_all[:, i, :], o_hi1[:, i, :], o_lo1[:, i, :], o_ready)
            st = stages["proj"]
            dve.wait_ge(stages["gate"].free, 2 * DT)
            for i in range(DT):
                for b in range(2):
                    g = gates[:, DT * b + i, :]
                    dve.wait_ge(slot_done, st.made(2 * i + b))
                    step.wait()
                    step(nc.vector.scalar_tensor_tensor(g, g, 1.0, acc[st.bank(2 * i + b)][:], ALU.add, ALU.mult), st.free)
                step.wait()
                step(nc.vector.tensor_tensor(gates[:, i, :], gates[:, i, :], gates[:, DT + i, :], ALU.add))
                split(gates[:, i, :], h_hi[:, i, :], h_lo[:, i, :], m_ready)
            st = stages["out"]
            for i in range(DT):
                dve.wait_ge(slot_done, st.made(i))
                step.wait()
                step(nc.vector.scalar_tensor_tensor(x_res[:, i, :], acc[st.bank(i)][:], 0.5, x_res[:, i, :], ALU.mult, ALU.add),
                     st.free)
            norm(x_res, lambda i: param("norm2_g", i))
            for half in range(2):
                st = stages[f"up{half}"]
                for i in range(HALF):
                    r, t_ = u_tmp[:, 0, :], u_tmp[:, 1, :]
                    ps = acc[st.bank(i)][:]
                    dve.wait_ge(slot_done, st.made(i))
                    step.wait()
                    step(nc.vector.tensor_scalar(r, ps, 0.0, None, ALU.max))
                    step.wait()
                    step(nc.vector.scalar_tensor_tensor(t_, ps, 0.0, r, ALU.max, ALU.mult), st.free)
                    split(t_, u_hi[:, i, :], u_lo[:, i, :], u_ready)
                st = stages[f"down{half}"]
                for i in range(DT):
                    dve.wait_ge(slot_done, st.made(i))
                    step.wait()
                    step(nc.vector.tensor_tensor(x_res[:, i, :], acc[st.bank(i)][:], x_res[:, i, :], ALU.add), st.free)

            dve.wait_ge(mem_loaded, 16)
            norm(mem, lambda i: param("mem_g", i), MEM)
            st = stages["memkv"]
            for layer in range(2):
                for j in range(4):
                    take(st, 8 * layer + j, mem_k[layer][:, j, :])
                for j in range(4):
                    feat_v(st, 8 * layer + 4 + j, MEM)
                    tok_v(mem_v[layer][:, :, j * P:(j + 1) * P])

            def conv_mlp(layer):
                norm(x_res, lambda i: param("norm_g", 32 * layer + 16 + i))
                st = stages[f"ffn_in{layer}"]

                def conv(i):
                    ps, t_ = acc[st.bank(2 * i)], ffn_tmp[:, i % 2, :]
                    w = [param("ffn_w", (3 * layer + k) * FF2 + i) for k in range(3)]
                    dve.wait_ge(slot_done, st.made(2 * i))
                    step.wait()
                    step(nc.vector.tensor_scalar(t_, ps[:], w[1], param("ffn_b", layer * FF2 + i), ALU.mult, ALU.add))
                    step.wait()
                    step(nc.vector.scalar_tensor_tensor(t_[:, 1:T], ps[:, 0:T - 1], w[0], t_[:, 1:T], ALU.mult, ALU.add))
                    step.wait()
                    step(nc.vector.scalar_tensor_tensor(t_[:, 0:T - 1], ps[:, 1:T], w[2], t_[:, 0:T - 1], ALU.mult, ALU.add),
                         st.free)

                def hidden(i):
                    t_ = ffn_tmp[:, i % 2, :]
                    dve.wait_ge(gelu_ready, layer * FF2 + i + 1)
                    dve.wait_ge(slot_done, st.made(2 * i + 1))
                    step.wait()
                    step(nc.vector.tensor_tensor(t_, acc[st.bank(2 * i + 1)][:], t_, ALU.mult), st.free)
                    split(t_, hid_hi[:, i, :], hid_lo[:, i, :], hid_ready)

                for i in range(FF2):
                    conv(i)
                    hidden(i)
                st = stages[f"ffn_out{layer}"]
                for i in range(DT):
                    take(st, i, y_all[:, i, :])
                add_norm(lambda i: param("norm_g", 32 * layer + 24 + i))

            def mixer_out(layer):
                for i in range(12):
                    split(o2[:, i, :], o_hi2[:, i, :], o_lo2[:, i, :], o_ready)
                st = stages["ab"[layer] + "_out"]
                for i in range(DT):
                    take(st, i, y_all[:, i, :])
                add_norm(lambda i: param("norm_g", 32 * layer + 8 + i))

            norm(x_res, lambda i: param("norm_g", i))
            st = stages["a_in"]
            for c in range(10):
                i = n["rope"]
                n["rope"] += 1
                t_, dst = normed[:, i % 2, :], (q_win[:, c, :] if c < DT else k_win[:, c - DT, :])
                take(st, c, t_, float(HEAD_DIM) ** -0.5 if c < DT else None)
                step.wait()
                step(nc.vector.tensor_tensor(dst, t_, rope[:, 0, :], ALU.mult))
                dve.wait_ge(rope_rot, i + 1)
                step.wait()
                step(nc.vector.tensor_tensor(square[:, 0, :], ps_t[:], rope[:, 1, :], ALU.mult))
                step.wait()
                step(nc.vector.tensor_tensor(dst, dst, square[:, 0, :], ALU.add), rope_done)
            for j in range(2):
                feat_v(st, 10 + j)
                tok_v(v_win[:, :, j * P:(j + 1) * P])
            for j in range(X_HEADS):
                take(st, 12 + j, xq[:, j, :])
            attention(units_win, probs2)
            attention(units_x[0], probs2)
            mixer_out(0)
            conv_mlp(0)

            norm(x_res, lambda i: param("norm_g", 32 + i))
            st = stages["b_in"]
            attention(units_x[1], probs2)
            by_chunk = lambda ap: ap.rearrange("p (c t) -> p c t", t=HG_CHUNK)
            for h in range(HG_HEADS):
                tok_v(hg_v[:])
                for b in range(BLOCKS):
                    step.wait()
                    step(nc.vector.tensor_tensor(
                        hg_vm[:, b, :, :], hg_v[:, b:b + 1, :].to_broadcast([P, BLOCK_CHUNKS, P]),
                        const("chunk_mask", BLOCK_CHUNKS).unsqueeze(2).to_broadcast([P, BLOCK_CHUNKS, P]), ALU.mult),
                        hg_vmask if b == BLOCKS - 1 else None)
                for d, (f, k) in enumerate([(hg_lf_f, hg_k_f), (hg_lf_b, hg_k_b)]):
                    dve.wait_ge(st.free, X_HEADS + 5 * h + 3 + d)
                    i = 8 * d + h
                    step.wait()
                    step(nc.vector.tensor_scalar(f[:], f[:], small["one_less"][:, i:i + 1], small["lower"][:, i:i + 1],
                                                 ALU.mult, ALU.add))
                    step.wait()
                    step(nc.vector.tensor_scalar(k[:], f[:], -1.0, 1.0, ALU.mult, ALU.add), hg_f)
                for d, (lf, b_) in enumerate([(hg_lf_f, hg_b_f), (hg_lf_b, hg_b_b)]):
                    dve.wait_ge(hg_ln, 2 * h + d + 1)
                    step.wait()
                    way = slice(None) if d == 0 else slice(None, None, -1)
                    step(nc.vector.tensor_tensor_scan(b_[:, way], const("reset", T), lf[:, way], 0.0, ALU.mult, ALU.add),
                         hg_cum)
                for d, (b_, end) in enumerate([(hg_b_f, "end_f"), (hg_b_b, "end_b")]):
                    at_ = HG_CHUNK - 1 if d == 0 else 0
                    dve.wait_ge(hg_exp, 4 * h + 2 * d + 2)
                    step.wait()
                    step(nc.vector.tensor_copy(small[end][:], by_chunk(b_[:])[:, :, at_]))
                    step.wait()
                    step(nc.vector.tensor_tensor(by_chunk(b_[:]), small[end][:].unsqueeze(2).to_broadcast([P, CHUNKS, HG_CHUNK]),
                                                 by_chunk(b_[:]), ALU.subtract), hg_rest)
                for d, (ke, k, qd, kd) in enumerate([(hg_b_f, hg_k_f, hg_qd_f, hg_kd_f), (hg_b_b, hg_k_b, hg_qd_b, hg_kd_b)]):
                    step.wait()
                    step(nc.vector.tensor_tensor(qd[:], qd[:], hg_q[:], ALU.mult))
                    step.wait()
                    step(nc.vector.tensor_tensor(kd[:], kd[:], k[:], ALU.mult))
                    dve.wait_ge(hg_rest_exp, 2 * h + d + 1)
                    step.wait()
                    step(nc.vector.tensor_tensor(ke[:], ke[:], k[:], ALU.mult), hg_dec)
                for d, (s_, mask) in enumerate([(hg_s_f, "causal_f"), (hg_s_b, "causal_b")]):
                    dve.wait_ge(hg_st, 2 * h + d + 1)
                    step.wait()
                    step(nc.vector.tensor_tensor(s_[:], ps_s[d][:].rearrange("p (b n) -> p b n", n=P),
                                                 const(mask).unsqueeze(1).to_broadcast([P, BLOCKS, P]), ALU.mult), hg_s)
                for d, ke in enumerate([hg_ke_f, hg_ke_b]):
                    dve.wait_ge(hg_ket, 2 * h + d + 1)
                    step.wait()
                    step(nc.vector.tensor_copy(ke[:], ps_t[:].rearrange("p (b n) -> p b n", n=P)), hg_ke)
                for g in range(CHUNKS // GROUP):
                    dve.wait_ge(hg_u, 8 * h + g + 1)
                    for c in range(GROUP * g, GROUP * (g + 1)):
                        for d, (state, decay) in enumerate([(hg_state_f, "decay_f"), (hg_state_b, "decay_b")]):
                            chunk = c if d == 0 else CHUNKS - 1 - c
                            u_ = ps_s[d][:, P * (chunk % GROUP):P * (chunk % GROUP + 1)]
                            new, old = state[:, (c + 1) % (2 * GROUP), :], state[:, c % (2 * GROUP), :]
                            if c >= 2 * GROUP and d == 0:
                                dve.wait_ge(hg_inter, 8 * h + (c + 1 - 2 * GROUP) // GROUP + 1)
                            step.wait()
                            done = hg_chain if c % GROUP == GROUP - 1 and d == 1 else None
                            if c == 0:
                                step(nc.vector.tensor_copy(new, u_), done)
                            else:
                                step(nc.vector.scalar_tensor_tensor(new, old, small[decay][:, chunk:chunk + 1], u_, ALU.mult,
                                                                    ALU.add), done)
                invert_rms()
                step.wait()
                step(nc.vector.scalar_tensor_tensor(o2[:, h, :], ps_o[:], param("b_norm_g", h), rstd[:], ALU.mult, ALU.mult))
                dve.wait_ge(st.free, X_HEADS + 5 * h + 5)
                step.wait()
                step(nc.vector.tensor_tensor(o2[:, h, :], o2[:, h, :], hg_gate[:], ALU.mult), o_taken)
            mixer_out(1)
            conv_mlp(1)


def weight_tiles(w):
    k, n = w.shape
    return w.reshape(k // P, P, n // P, P).transpose(2, 0, 1, 3).reshape(-1, P, P)


def columns(a):
    return np.ascontiguousarray(a.reshape(-1, P).T)


def shape_constants():
    i = np.arange(P)
    q, k = i[:, None], i[None, :]
    rot = np.zeros((P, P), np.float32)
    half = HEAD_DIM // 2
    for m in range(P):
        if m % HEAD_DIM < half:
            rot[m + half, m] = -1.0
        else:
            rot[m - half, m] = 1.0
    mask = lambda keep: np.where(keep, 0.0, NEG)
    same = q // HG_CHUNK == k // HG_CHUNK
    parts = {
        "ident": np.eye(P), "rot": rot, "pair_ones": q // HEAD_DIM == k // HEAD_DIM, "ones": np.ones((P, P)),
        "win_mask": np.concatenate([mask(k >= q), np.zeros((P, P)), mask(k <= q)], 1),
        "causal_f": same & (q <= k), "causal_b": same & (q >= k),
        "chunk_mask": q // HG_CHUNK == np.arange(BLOCK_CHUNKS)[None, :],
        "reset": np.broadcast_to(np.arange(T) % HG_CHUNK != 0, (P, T)), "zeros": np.zeros((P, T)),
    }
    consts = np.concatenate([np.asarray(parts[c], np.float32) for c in CONST_COLS], 1)
    inv = np.float32(10000.0) ** (-np.arange(half, dtype=np.float32) / np.float32(half))
    angle = (np.arange(T, dtype=np.float32)[None, :] * inv[i % half][:, None]).astype(np.float64)
    rope = np.stack([np.cos(angle), np.sin(angle)], 1).astype(np.float32)
    return consts, rope


def layout(a):
    by_tile = lambda x: np.ascontiguousarray(x[0].T.reshape(DT, P, -1).transpose(1, 0, 2))
    blocks = {}
    for name in ["w_in", "w_gate", "w_attn_proj", "w_conv_proj", "w_out", "w_up", "w_down"]:
        blocks[name] = weight_tiles(a[name]).reshape(a[name].shape[1] // P, -1, P, P)
    win = blocks["w_in"]
    conv = [win[24 + 8 * part + i] for i in range(DT) for part in (1, 2, 0)]
    proj = [blocks[w][i] for i in range(DT) for w in ("w_attn_proj", "w_conv_proj")]
    perm = [4 * (2 * (s // 8) + s % 2) + (s % 8) // 2 for s in range(HEADS)]
    cols = np.concatenate([np.arange(h * HEAD_DIM, (h + 1) * HEAD_DIM) for h in perm])
    a_in, a_out = a["a_w_in_2"][0], a["a_w_out_2"][0]
    a_in = np.concatenate([a_in[:, cols], a_in[:, D:]], 1)
    a_out = np.concatenate([a_out[cols], a_out[D:]], 0)
    b_in = weight_tiles(a["b_w_in_2"][0]).reshape(-1, DT, P, P)
    b_in = [b_in[40 + i] for i in range(X_HEADS)] + [b_in[8 * part + h] for h in range(HG_HEADS) for part in range(5)]

    def ffn_in(layer):
        return weight_tiles(a["ffn_w_in_2"][layer]).reshape(2, FF2, DT, P, P).transpose(1, 0, 2, 3, 4)

    up, down = blocks["w_up"], blocks["w_down"]
    order = [win[:24], conv, blocks["w_gate"], proj, blocks["w_out"],
             up[:HALF], down[:, :HALF], up[HALF:], down[:, HALF:],
             weight_tiles(a["w_mem_kv_2"][0]), weight_tiles(a["w_mem_kv_2"][1]),
             weight_tiles(a_in), weight_tiles(a_out), ffn_in(0), weight_tiles(a["ffn_w_out_2"][0]),
             b_in, weight_tiles(a["b_w_out_2"][0]), ffn_in(1), weight_tiles(a["ffn_w_out_2"][1])]
    tiles = np.concatenate([np.asarray(o).reshape(-1, P, P) for o in order])
    stream = np.ascontiguousarray(tiles.reshape(-1, SLOT_TILES, P, P).transpose(0, 2, 1, 3)).reshape(-1, P, SLOT_TILES * P)
    pair = lambda g: np.concatenate([g, g])
    params = np.concatenate([
        columns(a["norm1_g"]), columns(a["norm2_g"]), columns(pair(a["q_norm_g"])), columns(pair(a["k_norm_g"])),
        columns(a["conv_w"]), columns(a["conv_b"]), columns(a["b_gate"]), columns(a["norm_g_2"]), columns(a["mem_norm_g_2"]),
        columns(a["b_lb_logits_2"]), columns(a["b_norm_g_2"]), columns(a["ffn_conv_w_2"]), columns(a["ffn_conv_b_2"]),
        np.broadcast_to(a["a_sink_2"][0][perm][None, :], (P, HEADS))], 1)
    flipped = a["rel_bias"][:, ::-1]
    ext = np.concatenate([np.repeat(flipped[:, :1], T // 2 - 1, 1), flipped[:, :EXT_W - T // 2 + 1]], 1)
    consts, rope = shape_constants()
    return {"stream": stream, "x_in": by_tile(a["x"]), "mem_in": by_tile(a["mem_2"]), "consts_in": consts, "rope_in": rope,
            "params_in": np.ascontiguousarray(params), "ext_in": np.stack([ext[:, P - 1 - q:P - 1 - q + T] for q in range(P)], 1)}


def kernel(**inputs):
    import concourse.bacc as bacc
    from concourse.bass_utils import run_bass_kernel_spmd

    arrays = layout({k: np.asarray(v) for k, v in inputs.items()})
    nc = bacc.Bacc("TRN2", target_bir_lowering=False, num_devices=1)
    args = [nc.dram_tensor(k, v.shape, mybir.dt.from_np(v.dtype), kind="ExternalInput").ap() for k, v in arrays.items()]
    out = nc.dram_tensor("out", (P, DT, T), F32, kind="ExternalOutput").ap()
    build(nc, *args, out)
    result = run_bass_kernel_spmd(nc, [arrays], core_ids=[0]).results[0]["out"]
    return np.ascontiguousarray(result.transpose(1, 0, 2).reshape(1, D, T).transpose(0, 2, 1))
```

```python
from contextlib import ExitStack, contextmanager

import numpy as np

import concourse.bass as bass
from concourse import mybir

F32 = mybir.dt.float32
F32R = mybir.dt.float32r
ALU = mybir.AluOpType
ACT = mybir.ActivationFunctionType

P = 128
T = 512
D = 1024
DT = D // P
BLOCKS = T // P
EPS = 1e-6
NEG = -1e30

RING = 4
SLOT_TILES = 8
BANKS = 4

HEADS, HEAD_DIM, CHUNK, MAX_REL = 16, 64, 64, 256
FF1 = 4 * D
HALF = FF1 // P // 2
EXT_W = 640
MEM = 256
KV_HEADS = 4
X_HEADS = 4
FF2 = 2816 // P
HG_HEADS, HG_CHUNK = 8, 16
CHUNKS = T // HG_CHUNK
BLOCK_CHUNKS = P // HG_CHUNK

LEAD = {"qkv", "up0", "memkv", "a_in", "a_out", "ffn_in0", "b_in", "b_out", "ffn_in1"}
STAGES = [
    ("qkv", 24, 8), ("conv", 24, 8), ("gate", 16, 8), ("proj", 16, 8), ("out", 8, 8),
    ("up0", HALF, 8), ("down0", 8, HALF), ("up1", HALF, 8), ("down1", 8, HALF),
    ("memkv", 16, 8),
    ("a_in", 16, 8), ("a_out", 8, 12), ("ffn_in0", 2 * FF2, 8), ("ffn_out0", 8, FF2),
    ("b_in", 44, 8), ("b_out", 8, 12), ("ffn_in1", 2 * FF2, 8), ("ffn_out1", 8, FF2),
]

PARAM_COLS = {}
_at = 0
for _name, _n in [
    ("norm1_g", 8), ("norm2_g", 8), ("q_g", 1), ("k_g", 1), ("conv_w", 24), ("conv_b", 8), ("b_gate", 16),
    ("norm_g", 64), ("mem_g", 8), ("lb_logits", 32), ("b_norm_g", 8), ("ffn_w", 2 * 3 * FF2), ("ffn_b", 2 * FF2),
    ("sink", 16),
]:
    PARAM_COLS[_name] = _at
    _at += _n
PARAM_W = _at

CONST_COLS = {}
_at = 0
for _name, _n in [
    ("ident", 128), ("rot", 128), ("pair_ones", 128), ("ones", 128), ("win_mask", 384), ("reset", 512), ("span_reset", 5 * CHUNKS),
]:
    CONST_COLS[_name] = _at
    _at += _n
CONST_W = _at

MASK_COLS = {}
_at = 0
for _name, _n in [(f"{d}{level}", P if level == 0 else P // 2) for d in "fb" for level in range(4)]:
    MASK_COLS[_name] = _at
    _at += _n
MASK_W = _at


class Stage:

    def __init__(self, name, cbs, kt, first_slot, first_cb, prev):
        self.name, self.cbs, self.kt = name, cbs, kt
        self.first_slot, self.first_cb, self.prev = first_slot, first_cb, prev
        self.slots = cbs * kt // SLOT_TILES
        self.lead = name in LEAD
        self.free = None

    def made(self, c):
        if self.lead and isinstance(c, int) and c < BANKS:
            return self.first_slot + BANKS * self.kt // SLOT_TILES
        if self.kt % SLOT_TILES == 0:
            return c * (self.kt // SLOT_TILES) + self.first_slot + self.kt // SLOT_TILES
        return self.first_slot + ((c + 1) * self.kt - 1) // SLOT_TILES + 1

    def bank(self, c):
        return (self.first_cb + c) % BANKS


class Order:

    def __init__(self, eng, own):
        self.eng, self.own, self.count, self.last = eng, own, {}, None
        self.it = self.lo = None
        self.per, self.base = {}, {}

    def wait(self):
        if self.last is not None:
            self.eng.wait_ge(*self.last)

    def __call__(self, ins, sem=None):
        sem = self.own if sem is None else sem
        ins.then_inc(sem, 1)
        self.count[sem] = self.count.get(sem, 0) + 1
        if self.it is None:
            self.last = (sem, self.count[sem])
        else:
            per = self.per[sem]
            self.last = (sem, self.it * per + (self.count[sem] - self.lo * per))

    @contextmanager
    def loop(self, lo, hi, per):
        self.wait()
        self.last = None
        before = dict(self.count)
        with self.eng.Fori(lo, hi, 1) as it:
            self.it, self.lo, self.per = it, lo, per
            yield it
            self.wait()
        added = {s: n - before.get(s, 0) for s, n in self.count.items() if n != before.get(s, 0)}
        assert added == per, {s.name: n for s, n in added.items()}
        for s, n in per.items():
            self.count[s] = before.get(s, 0) + n * (hi - lo)
        self.it = self.last = None


def tile_of(buf, i):
    if isinstance(i, int):
        return buf[:, i, :]
    return buf[:, bass.ds(i, 1), :].rearrange("p a n -> p (a n)")


def column(buf, i):
    if isinstance(i, int):
        return buf[:, i:i + 1]
    return buf[:, bass.ds(i, 1)]


def f32(ap):
    return ap.bitcast(F32)


class Unit:

    def __init__(self, q, k, width, bias, scale, sink, v, out_part, out_cols, last, dst, heads_bias=None):
        self.q, self.k, self.width, self.bias, self.scale, self.sink = q, k, width, bias, scale, sink
        self.v, self.out_part, self.out_cols, self.last, self.dst = v, out_part, out_cols, last, dst
        self.heads_bias = heads_bias


def build(nc, stream, x_in, mem_in, consts_in, rope_in, params_in, masks_in, ext_in, out):
    stages = {}
    slot = cb = 0
    prev = None
    for name, cbs, kt in STAGES:
        prev = stages[name] = Stage(name, cbs, kt, slot, cb, prev)
        slot += prev.slots
        cb += cbs
        assert prev.cbs % BANKS == 0
    n_slots = slot
    assert n_slots % RING == 0

    with ExitStack() as ctx:
        def sem(name):
            return ctx.enter_context(nc.semaphore(name))

        KB = 1024
        base = (nc.sbuf_base + 63) // 64 * 64

        def sb(name, shape, offset, dtype=F32):
            return nc.alloc_sbuf_tensor_at(name, [P] + list(shape), dtype, offset=base + offset)

        w_raw = sb("w_raw", [RING, D], 0)
        w_hi = sb("w_hi", [RING, SLOT_TILES, P], 16 * KB, F32R)
        w_lo = sb("w_lo", [RING, SLOT_TILES, P], 32 * KB, F32R)
        x_res = sb("x_res", [DT, T], 48 * KB)
        h_hi = sb("h_hi", [DT, T], 64 * KB, F32R)
        h_lo = sb("h_lo", [DT, T], 80 * KB, F32R)
        consts = sb("consts", [CONST_W], 96 * KB)
        at = 96 * KB + -(-4 * CONST_W // 32) * 32
        masks = sb("masks", [MASK_W], at, mybir.dt.uint8)
        at += -(-MASK_W // 32) * 32
        params = sb("params", [PARAM_W], at)
        at += -(-4 * PARAM_W // 32) * 32
        small = {}
        for name, n in [("zero", 1), ("k_g8", 1), ("half_gate_b", 16), ("lower", 16), ("one_less", 16), ("eps_d", 1), ("eps_q", 1),
                        ("eps_v", 1), ("row_max", 3), ("neg_max", 3), ("row_sum", 3), ("sink_exp", 3), ("inv_sum", 3),
                        ("decay_f", CHUNKS), ("decay_b", CHUNKS),
                        ("block_f", BLOCKS), ("block_b", BLOCKS),
                        ("lb_exp", 32)]:
            small[name] = sb(name, [n], at)
            at += -(-4 * n // 32) * 32
        at = (at + 63) // 64 * 64
        rope = sb("rope", [2, T], at)
        ffn_tmp = sb("ffn_tmp", [2, T], at)
        at += 4 * KB
        rstd_in = sb("rstd_in", [T], at)
        at += 2 * KB
        arena = at
        assert base + arena + 96 * KB <= nc.sbuf_usable_end, (base + arena + 96 * KB, nc.sbuf_usable_end)

        def ar(name, shape, kb, dtype=F32):
            return sb(name, shape, arena + int(kb * KB), dtype)

        square = ar("square", [2, T], 68)
        rms = ar("rms", [T], 72)
        rstd = ar("rstd", [T], 74)
        normed = ar("normed", [2, T], 76)
        qk = ar("qk", [2 * DT, T], 0)
        v_tok1 = ar("v_tok1", [BLOCKS, D], 32)
        o_all = ar("o_all", [12, T], 48)
        o_hi1 = ar("o_hi1", [DT, T], 32, F32R)
        o_lo1 = ar("o_lo1", [DT, T], 48, F32R)
        v_feat = ar("v_feat", [2, T], 64)
        toeplitz = ar("toeplitz", [2, T], 80)
        probs = ar("probs", [3, T], 84)
        probs_t = ar("probs_t", [2, T], 90)
        y_hi = ar("y_hi", [DT, T], 0, F32R)
        y_lo = ar("y_lo", [DT, T], 16, F32R)
        conv_tmp = ar("conv_tmp", [3, T], 32)
        gates = ar("gates", [2 * DT, T], 64)
        u_hi = ar("u_hi", [HALF, T], 0, F32R)
        u_lo = ar("u_lo", [HALF, T], 32, F32R)
        u_tmp = ar("u_tmp", [2, T], 64)
        mem = ar("mem", [DT, MEM], 80)
        mem_k = [ar(f"mem_k{i}", [X_HEADS, MEM], 80 + 8 * i) for i in range(2)]
        mem_v = [ar(f"mem_v{i}", [MEM // P, X_HEADS * P], 84 + 8 * i) for i in range(2)]
        o2 = ar("o2", [12, T], 0)
        o_lo2 = ar("o_lo2", [12, T], 0, F32R)
        o_hi2 = ar("o_hi2", [12, T], 24, F32R)
        q_win = ar("q_win", [DT, T], 24)
        k_win = ar("k_win", [2, T], 40)
        v_win = ar("v_win", [BLOCKS, KV_HEADS * HEAD_DIM], 44)
        xq = ar("xq", [X_HEADS, T], 48)
        probs2 = ar("probs2", [3, T], 56)
        probs2_t = ar("probs2_t", [2, T], 62)
        y_all = sb("y_all", [DT, T], 64 * KB)
        hid_hi = ar("hid_hi", [FF2, T], 0, F32R)
        hid_lo = ar("hid_lo", [FF2, T], 44, F32R)
        hid_tmp = ar("hid_tmp", [FF2, T], 44)
        masks_f32 = ar("masks_f32", [MASK_W], 0)
        hg_in = [ar(f"hg_in{i}", [5, T], 24 + 10 * i) for i in range(2)]
        hg_v = ar("hg_v", [BLOCKS, P], 44)
        (hg_key_f, hg_key_b, hg_qd_f, hg_qd_b, hg_grow_f, hg_grow_b, hg_qb_f, hg_qb_b) = [
            ar(n, [T], 46 + 2 * i) for i, n in enumerate(
                ["hg_key_f", "hg_key_b", "hg_qd_f", "hg_qd_b", "hg_grow_f", "hg_grow_b", "hg_qb_f", "hg_qb_b"])]
        hg_s_f, hg_s_b, hg_ke_f, hg_ke_b = [ar(n, [BLOCKS, P], 62 + 2 * i) for i, n in enumerate(
            ["hg_s_f", "hg_s_b", "hg_ke_f", "hg_ke_b"])]
        hg_level_q = [ar(f"hg_level_q{d}", [2, T // 2], 70 + 2 * d) for d in range(2)]
        hg_level_k = [ar(f"hg_level_k{d}", [2, T], 74 + 4 * d) for d in range(2)]
        hg_block_k = [ar(f"hg_block_k{d}", [T], 82 + 2 * d) for d in range(2)]
        rstd_head = ar("rstd_head", [T], 88)
        hg_state_f = ar("hg_state_f", [BLOCKS - 1, P], 90)
        hg_state_b = ar("hg_state_b", [BLOCKS - 1, P], 92)
        near_f, near_b = ar("near_f", [6 * CHUNKS], 94), ar("near_b", [6 * CHUNKS], 94.75)
        end_f, end_b = ar("end_f", [3 * CHUNKS + 2], 93.5), ar("end_b", [3 * CHUNKS + 2], 95.5)

        def const(name, n=P):
            c = CONST_COLS[name]
            return consts[:, c:c + n]

        def param(name, i=0):
            c = PARAM_COLS[name]
            if isinstance(i, int):
                return params[:, c + i:c + i + 1]
            return params[:, bass.ds(i + c, 1)]

        acc = [ctx.enter_context(nc.psum_tensor(f"acc{i}", [P, T], F32)) for i in range(BANKS)]
        ps_s = [ctx.enter_context(nc.psum_tensor(f"ps_s{i}", [P, T], F32)) for i in range(2)]
        ps_t = ctx.enter_context(nc.psum_tensor("ps_t", [P, T], F32))
        ps_o = ctx.enter_context(nc.psum_tensor("ps_o", [P, T], F32))

        small_in = sem("small_in")
        mem_loaded = sem("mem_loaded")
        loaded = [sem(f"loaded{i}") for i in range(RING)]
        bias_in = [sem(f"bias_in{i}") for i in range(2)]
        hi_made = sem("hi_made")
        split_made = sem("split_made")
        slot_done = sem("slot_done")
        for s in stages.values():
            s.free = sem(f"free_{s.name}")
        dve_own = sem("dve_own")
        setup_done = sem("setup_done")
        setup_act = sem("setup_act")
        h_ready = sem("h_ready")
        o_ready = sem("o_ready")
        y_ready = sem("y_ready")
        m_ready = sem("m_ready")
        u_ready = sem("u_ready")
        hid_ready = sem("hid_ready")
        x_ready = sem("x_ready")
        sq_ready = sem("sq_ready")
        sq_used = sem("sq_used")
        rms_ready = sem("rms_ready")
        rms_used = sem("rms_used")
        vt_done = sem("vt_done")
        v_ready = sem("v_ready")
        rope_rot = sem("rope_rot")
        rope_done = sem("rope_done")
        s_ready = sem("s_ready")
        s_used = sem("s_used")
        max_ready = sem("max_ready")
        p_ready = sem("p_ready")
        sink_ready = sem("sink_ready")
        pn_ready = sem("pn_ready")
        pt_made = sem("pt_made")
        pt_ready = sem("pt_ready")
        pv_done = sem("pv_done")
        o_taken = sem("o_taken")
        gate_ready = sem("gate_ready")
        conv_ready = sem("conv_ready")
        qk_ready = sem("qk_ready")
        rope_ready = sem("rope_ready")
        gelu_ready = sem("gelu_ready")
        hg_sig = sem("hg_sig")
        hg_silu_q = sem("hg_silu_q")
        hg_silu_g = sem("hg_silu_g")
        hg_f = sem("hg_f")
        hg_ln = sem("hg_ln")
        hg_cum = sem("hg_cum")
        hg_exp = sem("hg_exp")
        hg_rest = sem("hg_rest")
        hg_rest_exp = sem("hg_rest_exp")
        hg_k = sem("hg_k")
        hg_st = sem("hg_st")
        hg_ket = sem("hg_ket")
        hg_s = sem("hg_s")
        hg_ke = sem("hg_ke")
        hg_u = sem("hg_u")
        hg_chain = sem("hg_chain")
        hg_o = sem("hg_o")
        stored = sem("stored")

        units1, units_win, units_x = [], [], [[], []]
        for h in range(HEADS):
            off = HEAD_DIM * (h % 2)
            for t in range(BLOCKS):
                units1.append(Unit(
                    q=qk[off:off + HEAD_DIM, h // 2, t * P:(t + 1) * P], k=qk[off:off + HEAD_DIM, DT + h // 2, 0:(t + 1) * P],
                    width=(t + 1) * P, bias=toeplitz[:, h % 2, T - (t + 1) * P:T], scale=1.0, sink=None,
                    v=[v_tok1[:, b, h * HEAD_DIM:(h + 1) * HEAD_DIM] for b in range(t + 1)],
                    out_part=off, out_cols=(t * P, (t + 1) * P), last=h % 2 == 1 and t == BLOCKS - 1,
                    dst=o_all[:, h // 2, :], heads_bias=(h, t == 0)))
            kv = 2 * (h // 8) + h % 2
            for t in range(BLOCKS):
                lo, hi = max(0, t - 1), min(BLOCKS, t + 2)
                m = CONST_COLS["win_mask"] + (lo - t + 1) * P
                units_win.append(Unit(
                    q=q_win[off:off + HEAD_DIM, h // 2, t * P:(t + 1) * P], k=k_win[off:off + HEAD_DIM, kv // 2, lo * P:hi * P],
                    width=(hi - lo) * P, bias=consts[:, m:m + (hi - lo) * P], scale=1.0, sink=param("sink", h),
                    v=[v_win[:, b, kv * HEAD_DIM:(kv + 1) * HEAD_DIM] for b in range(lo, hi)],
                    out_part=off, out_cols=(t * P, (t + 1) * P), last=h % 2 == 1 and t == BLOCKS - 1,
                    dst=o2[:, h // 2, :]))
        for layer in range(2):
            for h in range(X_HEADS):
                for t in range(BLOCKS):
                    units_x[layer].append(Unit(
                        q=xq[:, h, t * P:(t + 1) * P], k=mem_k[layer][:, h, :], width=MEM, bias=small["zero"][:].to_broadcast([P, MEM]),
                        scale=float(P) ** -0.5, sink=None, v=[mem_v[layer][:, b, h * P:(h + 1) * P] for b in range(MEM // P)],
                        out_part=0, out_cols=(t * P, (t + 1) * P), last=t == BLOCKS - 1, dst=o2[:, DT + h, :]))

        block = ctx.enter_context(nc.Block())

        @block.sync
        def _(sp):
            sp.dma_start(params[:], params_in).then_inc(small_in, 16)
            sp.dma_start(consts[:], consts_in).then_inc(small_in, 16)
            sp.dma_start(masks_f32[:], masks_in).then_inc(small_in, 16)
            sp.dma_start(x_res[:], x_in).then_inc(small_in, 16)
            for s in range(RING):
                sp.dma_start(w_raw[:, s, :], stream[s]).then_inc(loaded[s], 16)
            sp.dma_start(rope[:], rope_in).then_inc(small_in, 16)
            with sp.Fori(1, n_slots // RING, 1) as it:
                for s in range(RING):
                    sp.wait_ge(split_made, it * RING + (s + 1 - RING))
                    sp.dma_start(w_raw[:, s, :], stream[bass.ds(it * RING + s, 1)].rearrange("a p n -> p (a n)"))\
                        .then_inc(loaded[s], 16)
            sp.wait_ge(x_ready, 4 * DT)
            sp.dma_start(out, x_res[:]).then_inc(stored, 16)
            sp.wait_ge(stored, 16)

        @block.gpsimd
        def _(pool):
            def split(it, s):
                pool.wait_ge(loaded[s], it * 16 + 16)
                if not isinstance(it, int):
                    pool.wait_ge(slot_done, it * RING + (s + 1 - RING))
                raw = w_raw[:, s, :]
                hi = w_hi[:, s, :, :].rearrange("p t n -> p (t n)")
                lo = w_lo[:, s, :, :].rearrange("p t n -> p (t n)")
                nc.gpsimd.tensor_tensor(hi, raw, small["zero"][:].to_broadcast([P, D]), ALU.add).then_inc(hi_made, 1)
                pool.wait_ge(hi_made, it * RING + (s + 2))
                nc.gpsimd.tensor_tensor(lo, raw, f32(hi), ALU.subtract).then_inc(split_made, 1)

            nc.gpsimd.memset(small["zero"][:], 0.0).then_inc(hi_made, 1)
            pool.wait_ge(hi_made, 1)
            for s in range(RING):
                split(0, s)
            with pool.Fori(1, n_slots // RING, 1) as it:
                for s in range(RING):
                    split(it, s)

        def lagged(cbs, first, upto):
            plan, nxt = {}, 0
            for c in range(first, cbs + 1):
                n_ = min(upto - nxt, upto if c == cbs else min(2, c - nxt))
                plan[c] = list(range(nxt, nxt + n_))
                nxt += n_
            return plan

        @block.tensor
        def _(pe):
            n = {"sq": 0, "rms": 0, "v": 0, "rope": 0, "unit": 0, "o": 0, "h": 0}
            t_free = []

            def take_t(sem_, value):
                if t_free:
                    pe.wait_ge(*t_free[0])
                t_free[:] = [(sem_, value)]

            def three_passes(st, ps, s, t, x_hi, x_lo, k, cols):
                hi, lo = w_hi[:, s, t, :], w_lo[:, s, t, :]
                nc.tensor.matmul(ps, hi, x_hi[:, k, 0:cols], start=(k == 0), stop=False)
                nc.tensor.matmul(ps, hi, x_lo[:, k, 0:cols], start=False, stop=False)
                mm = nc.tensor.matmul(ps, lo, x_hi[:, k, 0:cols], start=False, stop=(k == st.kt - 1))
                if t == SLOT_TILES - 1:
                    mm.then_inc(slot_done, 1)

            def bank_free(st, c):
                if isinstance(c, int) and c < BANKS:
                    if st.prev is not None:
                        pe.wait_ge(st.prev.free, st.prev.cbs - BANKS + c + 1)
                else:
                    pe.wait_ge(st.free, c - (BANKS - 1))

            def products(st, it, body, j, x_hi, x_lo, cols=T, ready=None):
                bank_free(st, it * body + j)
                for k in range(st.kt):
                    tile = j * st.kt + k
                    if tile % SLOT_TILES == 0:
                        pe.wait_ge(split_made, it * (body * st.kt // SLOT_TILES) + (st.first_slot + tile // SLOT_TILES + 1))
                    if ready is not None:
                        ready(k)
                    three_passes(st, acc[st.bank(j)][:, 0:cols], (st.first_slot + tile // SLOT_TILES) % RING,
                                 tile % SLOT_TILES, x_hi, x_lo, k, cols)

            def lead(st, x_hi, x_lo, ready, then=None, cols=T):
                for k in range(st.kt):
                    ready(k)
                    for c in range(BANKS):
                        tile = k * BANKS + c
                        if k == 0:
                            bank_free(st, c)
                        if tile % SLOT_TILES == 0:
                            pe.wait_ge(split_made, st.first_slot + tile // SLOT_TILES + 1)
                        three_passes(st, acc[st.bank(c)][:, 0:cols], (st.first_slot + tile // SLOT_TILES) % RING,
                                     tile % SLOT_TILES, x_hi, x_lo, k, cols)
                    if then is not None:
                        then(k)

            def block_at(st, c, x_hi, x_lo, ready=None, cols=T):
                products(st, 0, st.cbs, c, x_hi, x_lo, cols, ready)

            def looped(st, body, x_hi, x_lo, ready=None, then=None):
                if st.lead:
                    lead(st, x_hi, x_lo, ready, then)
                else:
                    for j in range(body):
                        products(st, 0, body, j, x_hi, x_lo, T, ready if j == 0 else None)
                assert body % BANKS == 0 and body * st.kt // SLOT_TILES % RING == 0 and (body == BANKS or not st.lead)
                with pe.Fori(1, st.cbs // body, 1) as it:
                    for j in range(body):
                        products(st, it, body, j, x_hi, x_lo)

            def waits_for(sem_, first):
                return lambda k: pe.wait_ge(sem_, first + k + 1)

            def sum_square(i, tiles, ones, cols=T, sq=square):
                if i == 0:
                    n["rms"] += 1
                    take_t(rms_ready, n["rms"])
                pe.wait_ge(sq_ready, n["sq"] + 1)
                nc.tensor.matmul(ps_t[:, 0:cols], ones, sq[:, n["sq"] % sq.shape[1], 0:cols],
                                 start=(i == 0), stop=(i == tiles - 1)).then_inc(sq_used, 1)
                n["sq"] += 1

            def input_norm(cols=T):
                def then(k):
                    for i in [k] if k < 5 else range(5, DT) if k == 5 else []:
                        sum_square(i, DT, const("ones"), cols)
                return then

            def transpose_v(st, c, src, blocks=BLOCKS):
                n["v"] += 1
                take_t(v_ready, n["v"])
                pe.wait_ge(st.free, c + 1)
                for b in range(blocks):
                    mm = nc.tensor.transpose(ps_t[:, b * P:(b + 1) * P], src[:, b * P:(b + 1) * P], const("ident"))
                mm.then_inc(vt_done, 1)

            def rotate(st, i):
                take_t(rope_done, i + 1)
                pe.wait_ge(st.free, i + 1)
                src = q_win[:, i, :] if i < DT else k_win[:, i - DT, :]
                nc.tensor.matmul(ps_t[:], const("rot"), src, start=True, stop=True).then_inc(rope_rot, 1)

            def attention(units, p, p_t):
                u0 = n["unit"]

                def scores(i):
                    if i >= len(units):
                        return
                    u = units[i]
                    if u0 + i >= 2:
                        pe.wait_ge(s_used, u0 + i - 1)
                    nc.tensor.matmul(ps_s[(u0 + i) % 2][:, 0:u.width], u.q, u.k, start=True, stop=True).then_inc(s_ready, 1)

                def turn(i):
                    u = units[i]
                    take_t(pt_ready, u0 + i + 1)
                    pe.wait_ge(pn_ready, u0 + i + 1)
                    src = p[:, (u0 + i) % 3, :]
                    for b in range(u.width // P):
                        mm = nc.tensor.transpose(ps_t[:, b * P:(b + 1) * P], src[:, b * P:(b + 1) * P], const("ident"))
                    mm.then_inc(pt_made, 1)

                def weigh(i):
                    u = units[i]
                    if n["o"]:
                        pe.wait_ge(o_taken, n["o"])
                    pe.wait_ge(pt_ready, u0 + i + 1)
                    rows = u.v[0].shape[1]
                    for b in range(u.width // P):
                        mm = nc.tensor.matmul(ps_o[u.out_part:u.out_part + rows, u.out_cols[0]:u.out_cols[1]], u.v[b],
                                              p_t[:, (u0 + i) % 2, b * P:(b + 1) * P],
                                              start=(b == 0), stop=(b == u.width // P - 1))
                    mm.then_inc(pv_done, 1)
                    if u.last:
                        n["o"] += 1

                scores(0)
                scores(1)
                for i in range(len(units)):
                    scores(i + 2)
                    turn(i)
                    if i:
                        weigh(i - 1)
                weigh(len(units) - 1)
                n["unit"] += len(units)

            st = stages["qkv"]
            pe.wait_ge(small_in, 80)
            lead(st, h_hi, h_lo, waits_for(h_ready, 0), input_norm())
            n["h"] += DT
            plan = lagged(st.cbs, BANKS, 2 * DT)
            for c in range(BANKS, st.cbs):
                block_at(st, c, h_hi, h_lo)
                for i in plan[c]:
                    sum_square(0, 1, const("pair_ones"))
                if c > 2 * DT:
                    transpose_v(st, c - 1, v_feat[:, (c - 1) % 2, :])
            transpose_v(st, st.cbs - 1, v_feat[:, (st.cbs - 1) % 2, :])
            pe.wait_ge(v_ready, n["v"])
            pe.wait_ge(qk_ready, 2 * DT)
            attention(units1, probs, probs_t)
            looped(stages["conv"], 12, h_hi, h_lo)
            looped(stages["gate"], 4, h_hi, h_lo)
            st = stages["proj"]

            def proj(it):
                first = isinstance(it, int)
                for j in range(4):
                    if j % 2 == 0:
                        products(st, it, 4, j, o_hi1, o_lo1, ready=waits_for(o_ready, 0) if first and j == 0 else None)
                    else:
                        products(st, it, 4, j, y_hi, y_lo, ready=waits_for(y_ready, 0) if first and j == 1 else None)

            proj(0)
            with pe.Fori(1, st.cbs // 4, 1) as it:
                proj(it)
            looped(stages["out"], 4, h_hi, h_lo, ready=waits_for(m_ready, 0))
            for half in range(2):
                looped(stages[f"up{half}"], 4, h_hi, h_lo, ready=waits_for(h_ready, n["h"]),
                       then=input_norm() if half == 0 else None)
                looped(stages[f"down{half}"], 4, u_hi, u_lo, ready=waits_for(u_ready, half * HALF))
            n["h"] += DT
            st = stages["memkv"]
            lead(st, h_hi, h_lo, waits_for(h_ready, n["h"]), input_norm(MEM), MEM)
            n["h"] += DT
            for c in range(BANKS, st.cbs):
                block_at(st, c, h_hi, h_lo, cols=MEM)
                if (c - 1) % 8 >= 4:
                    transpose_v(st, c - 1, v_feat[:, (c - 1) % 2, :], MEM // P)
            transpose_v(st, st.cbs - 1, v_feat[:, (st.cbs - 1) % 2, :], MEM // P)

            def post_norm(st, c, sq):
                for i in lagged(st.cbs, BANKS if st.lead else 1, DT).get(c, []):
                    sum_square(i, DT, const("ones"), sq=sq)

            def conv_mlp(layer):
                looped(stages[f"ffn_in{layer}"], 4, h_hi, h_lo, ready=waits_for(h_ready, n["h"]), then=input_norm())
                n["h"] += DT
                st = stages[f"ffn_out{layer}"]
                for c in range(st.cbs):
                    block_at(st, c, hid_hi, hid_lo, waits_for(hid_ready, layer * FF2) if c == 0 else None)
                    post_norm(st, c, ffn_tmp)
                post_norm(st, st.cbs, ffn_tmp)

            def mixer_out(layer):
                st = stages["ab"[layer] + "_out"]
                lead(st, o_hi2, o_lo2, waits_for(o_ready, DT + 12 * layer))
                for c in range(BANKS, st.cbs):
                    block_at(st, c, o_hi2, o_lo2)
                    post_norm(st, c, square)
                post_norm(st, st.cbs, square)

            st = stages["a_in"]
            lead(st, h_hi, h_lo, waits_for(h_ready, n["h"]), input_norm())
            n["h"] += DT
            plan = lagged(st.cbs, BANKS, 10)
            for c in range(BANKS, st.cbs):
                block_at(st, c, h_hi, h_lo)
                for i in plan[c]:
                    rotate(st, i)
                if 11 <= c <= 12:
                    transpose_v(st, c - 1, v_feat[:, (c - 1) % 2, :])
            pe.wait_ge(v_ready, n["v"])
            pe.wait_ge(rope_ready, 10)
            attention(units_win, probs2, probs2_t)
            pe.wait_ge(st.free, st.cbs)
            attention(units_x[0], probs2, probs2_t)
            mixer_out(0)
            conv_mlp(0)
            st = stages["b_in"]
            lead(st, h_hi, h_lo, waits_for(h_ready, n["h"]), input_norm())
            n["h"] += DT
            pe.wait_ge(st.free, X_HEADS)
            attention(units_x[1], probs2, probs2_t)

            def head_in(h, j):
                if h < HG_HEADS:
                    block_at(st, X_HEADS + 5 * h + j, h_hi, h_lo)

            def head_scores(h, part):
                pe.wait_ge(hg_k, h + 1)
                qd, key, rest = (hg_qd_f, hg_qd_b), (hg_grow_f, hg_grow_b), hg_in[h % 2][:, 2:4, :]

                def own(d, bank, at):
                    for b in range(BLOCKS):
                        mm = nc.tensor.matmul(bank[:, at + b * P:at + (b + 1) * P], key[d][:, b * P:(b + 1) * P],
                                              qd[d][:, b * P:(b + 1) * P], start=True, stop=True)
                    return mm

                def level(d, i, bank, at):
                    half = HG_CHUNK << i
                    for b in range(BLOCKS):
                        cols = slice(b * P, (b + 1) * P)
                        if i == 0:
                            k_ = rest[:, d, cols]
                            q_ = qd[d][:, cols].rearrange("p (s x t) -> p s x t", x=2, t=half)[:, :, 1 - d, :]
                        else:
                            k_, q_ = hg_level_k[d][:, i - 1, cols], hg_level_q[d][:, i - 1, b * P // 2:(b + 1) * P // 2]
                        mm = nc.tensor.matmul(bank[:, at + b * P // 2:at + (b + 1) * P // 2], k_, q_, start=True, stop=True)
                    return mm

                if part == 0:
                    if h:
                        pe.wait_ge(hg_chain, h)
                    else:
                        pe.wait_ge(s_used, n["unit"])
                    own(0, ps_s[0], 0)
                    level(0, 0, ps_s[1], 0)
                    mm = level(0, 1, ps_s[1], T // 2)
                else:
                    pe.wait_ge(hg_s, 3 * h + part)
                    if part == 1:
                        level(0, 2, ps_s[0], 0)
                        level(1, 2, ps_s[0], T // 2)
                        level(1, 0, ps_s[1], 0)
                        mm = level(1, 1, ps_s[1], T // 2)
                    else:
                        mm = own(1, ps_s[0], 0)
                mm.then_inc(hg_st, 1)

            def head_keys(h, d):
                take_t(hg_ke, 2 * h + d + 1)
                for b in range(BLOCKS):
                    mm = nc.tensor.transpose(ps_t[:, b * P:(b + 1) * P], hg_block_k[d][:, b * P:(b + 1) * P], const("ident"))
                mm.then_inc(hg_ket, 1)

            def head_updates(h, d):
                bank = ps_s[1 - d]
                pe.wait_ge(v_ready, v0 + h + 1)
                pe.wait_ge(hg_s, 3 * h + 2 + d)
                pe.wait_ge(hg_ke, 2 * h + d + 1)
                for b in range(BLOCKS - 1):
                    src = b + d
                    mm = nc.tensor.matmul(bank[:, b * P:(b + 1) * P], [hg_ke_f, hg_ke_b][d][:, src, :], hg_v[:, src, :],
                                          start=True, stop=True)
                mm.then_inc(hg_u, 1)

            def head_out(h):
                pe.wait_ge(hg_chain, h + 1)
                pe.wait_ge(o_taken, n["o"])
                for b in range(BLOCKS):
                    cols = slice(b * P, (b + 1) * P)
                    parts = [(hg_v[:, b, :], hg_s_f[:, b, :]), (hg_v[:, b, :], hg_s_b[:, b, :])]
                    if b:
                        parts.append((hg_state_f[:, b - 1, :], hg_qb_f[:, cols]))
                    if b < BLOCKS - 1:
                        parts.append((hg_state_b[:, b, :], hg_qb_b[:, cols]))
                    for i, (left, right) in enumerate(parts):
                        mm = nc.tensor.matmul(ps_o[:, cols], left, right, start=(i == 0), stop=(i == len(parts) - 1))
                mm.then_inc(hg_o, 1)
                n["o"] += 1

            v0 = n["v"]
            for j in range(5):
                head_in(0, j)
            for h in range(HG_HEADS):
                head_in(h + 1, 0)
                if h:
                    head_updates(h - 1, 1)
                head_in(h + 1, 1)
                if h:
                    head_out(h - 1)
                transpose_v(st, X_HEADS + 5 * h + 1, hg_in[h % 2][:, 1, :])
                head_in(h + 1, 2)
                if h:
                    sum_square(0, 1, const("ones"), sq=ffn_tmp[:, 0:1, :])
                head_scores(h, 0)
                head_keys(h, 0)
                head_in(h + 1, 3)
                head_scores(h, 1)
                head_keys(h, 1)
                head_in(h + 1, 4)
                head_scores(h, 2)
                head_updates(h, 0)
            head_updates(HG_HEADS - 1, 1)
            head_out(HG_HEADS - 1)
            sum_square(0, 1, const("ones"), sq=ffn_tmp[:, 0:1, :])
            mixer_out(1)
            conv_mlp(1)

        @block.scalar
        def _(act):
            n = {"sq": 0, "rms": 0, "unit": 0}

            def squared(src, cols=T, sq=square):
                bufs = sq.shape[1]
                if n["sq"] >= bufs:
                    act.wait_ge(sq_used, n["sq"] - bufs + 1)
                nc.scalar.activation(sq[:, n["sq"] % bufs, 0:cols], src, ACT.Square).then_inc(sq_ready, 1)
                n["sq"] += 1

            def root(sums, scale, eps, cols=T, dst=rms):
                act.wait_ge(sq_used, sums)
                if n["rms"]:
                    act.wait_ge(rms_used, n["rms"])
                nc.scalar.activation(dst[:, 0:cols], ps_t[:, 0:cols], ACT.Sqrt, scale=scale, bias=eps).then_inc(rms_ready, 1)
                n["rms"] += 1

            def norm(src, sem_, first, cols=T, sq=square):
                for i in range(DT):
                    act.wait_ge(sem_, first + i + 1)
                    squared(src[:, i, 0:cols], cols, sq)
                root(n["sq"], 1.0 / D, small["eps_d"][:], cols)

            def attention(units, p, p_t):
                u0 = n["unit"]

                def exps(i):
                    if i >= len(units):
                        return
                    u, b = units[i], (u0 + i) % 3
                    act.wait_ge(max_ready, u0 + i + 1)
                    nc.scalar.activation(p[:, b, 0:u.width], p[:, b, 0:u.width], ACT.Exp, bias=small["neg_max"][:, b:b + 1],
                                         accum_out=small["row_sum"][:, b:b + 1]).then_inc(p_ready, 1)
                    if u.sink is not None:
                        nc.scalar.activation(small["sink_exp"][:, b:b + 1], u.sink, ACT.Exp,
                                             bias=small["neg_max"][:, b:b + 1]).then_inc(sink_ready, 1)
                    if u.heads_bias is not None and i >= BLOCKS:
                        load_bias(i + BLOCKS)

                def take(i):
                    u, b = units[i], (u0 + i) % 2
                    act.wait_ge(pt_made, u0 + i + 1)
                    if u0 + i >= 2:
                        act.wait_ge(pv_done, u0 + i - 1)
                    nc.scalar.activation(p_t[:, b, 0:u.width], ps_t[:, 0:u.width], ACT.Copy).then_inc(pt_ready, 1)

                def load_bias(i):
                    if i >= len(units) or not units[i].heads_bias[1]:
                        return
                    h = units[i].heads_bias[0]
                    if h >= 2:
                        act.wait_ge(s_used, u0 + i - BLOCKS)
                    act.dma_start(toeplitz[:, h % 2, :], ext_in[h]).then_inc(bias_in[h % 2], 16)

                if units[0].heads_bias is not None:
                    load_bias(0)
                    load_bias(BLOCKS)
                exps(0)
                exps(1)
                for i in range(len(units)):
                    take(i)
                    exps(i + 2)
                n["unit"] += len(units)

            act.wait_ge(small_in, 80)
            act.wait_ge(setup_done, 1)
            for i in range(DT):
                squared(x_res[:, i, :])
            root(DT, 1.0 / D, small["eps_d"][:])
            st = stages["qkv"]
            for c in range(2 * DT + 1):
                if c < 2 * DT:
                    act.wait_ge(st.free, c + 1)
                    squared(qk[:, c, :])
                if c:
                    root(DT + c, 1.0, small["eps_q"][:])
            act.wait_ge(setup_done, 2)
            nc.scalar.activation(small["lb_exp"][:], small["lb_exp"][:], ACT.Exp).then_inc(setup_act, 1)
            attention(units1, probs, probs_t)
            for c in range(2 * DT):
                act.wait_ge(stages["gate"].free, c + 1)
                nc.scalar.activation(gates[:, c, :], gates[:, c, :], ACT.Tanh, scale=0.5,
                                     bias=small["half_gate_b"][:, c:c + 1]).then_inc(gate_ready, 1)
            norm(x_res, stages["out"].free, 0)
            act.dma_start(mem[:], mem_in).then_inc(mem_loaded, 16)
            act.wait_ge(mem_loaded, 16)
            for i in range(DT):
                squared(mem[:, i, :], MEM)
            root(n["sq"], 1.0 / D, small["eps_d"][:], MEM)

            def gelus(layer):
                for i in range(FF2):
                    act.wait_ge(conv_ready, layer * FF2 + i + 1)
                    t_ = ffn_tmp[:, i % 2, :]
                    nc.scalar.activation(t_, t_, ACT.Gelu_apprx_tanh).then_inc(gelu_ready, 1)

            norm(x_res, stages["down1"].free, 0)
            attention(units_win, probs2, probs2_t)
            attention(units_x[0], probs2, probs2_t)
            norm(y_all, stages["a_out"].free, 0)
            norm(x_res, x_ready, 0)
            gelus(0)
            norm(y_all, stages["ffn_out0"].free, 0, sq=ffn_tmp)
            norm(x_res, x_ready, DT)
            attention(units_x[1], probs2, probs2_t)
            st = stages["b_in"]
            v0 = DT + 8 + 2

            def head_act(h, j, func, done):
                if 0 <= h < HG_HEADS:
                    act.wait_ge(st.free, X_HEADS + 5 * h + j + 1)
                    t_ = hg_in[h % 2][:, j, :]
                    nc.scalar.activation(t_, t_, func).then_inc(done, 1)

            def head_in(h):
                for j in (2, 3):
                    head_act(h, j, ACT.Sigmoid, hg_sig)
                head_act(h, 0, ACT.Silu, hg_silu_q)
                head_act(h - 1, 4, ACT.Silu, hg_silu_g)

            def head_square(h):
                act.wait_ge(hg_o, h + 1)
                squared(ps_o[:], sq=ffn_tmp[:, 0:1, :])

            def head_root():
                root(n["sq"], 1.0 / P, small["eps_v"][:], dst=ffn_tmp[:, 1, :])

            def head_keys(h, d):
                act.wait_ge(hg_ket, 2 * h + d + 1)
                if h:
                    act.wait_ge(hg_u, 2 * h - 1 + d)
                nc.scalar.activation([hg_ke_f, hg_ke_b][d][:].rearrange("p b n -> p (b n)"), ps_t[:], ACT.Copy).then_inc(hg_ke, 1)

            head_in(0)
            for h in range(HG_HEADS):
                for d in range(2):
                    act.wait_ge(hg_f, 2 * h + d + 1)
                    f_ = hg_in[h % 2][:, 2 + d, :]
                    nc.scalar.activation(f_, f_, ACT.Ln).then_inc(hg_ln, 1)
                for d, (qd, grow) in enumerate([(hg_qd_f, hg_grow_f), (hg_qd_b, hg_grow_b)]):
                    act.wait_ge(hg_cum, 2 * h + d + 1)
                    b_ = hg_in[h % 2][:, 2 + d, :]
                    nc.scalar.activation(qd[:], b_, ACT.Exp).then_inc(hg_exp, 1)
                    nc.scalar.activation(grow[:], b_, ACT.Exp, scale=-1.0).then_inc(hg_exp, 1)
                for d, way in enumerate("fb"):
                    act.wait_ge(hg_rest, 2 * h + d + 1)
                    end, near, rest = (end_f, end_b)[d][:, 1:CHUNKS + 1], (near_f, near_b)[d][:], hg_in[h % 2][:, 2 + d, :]
                    nc.scalar.activation(small["decay_" + way][:], end, ACT.Exp)
                    nc.scalar.activation(near, near, ACT.Exp)
                    nc.scalar.activation(rest, rest, ACT.Exp).then_inc(hg_rest_exp, 1)
                if h:
                    head_square(h - 1)
                act.wait_ge(vt_done, v0 + h + 1)
                nc.scalar.activation(hg_v[:].rearrange("p b n -> p (b n)"), ps_t[:], ACT.Copy).then_inc(v_ready, 1)
                if h:
                    head_root()
                head_keys(h, 0)
                head_in(h + 1)
                head_keys(h, 1)
            head_square(HG_HEADS - 1)
            head_root()
            norm(y_all, stages["b_out"].free, 0)
            norm(x_res, x_ready, 2 * DT)
            gelus(1)
            norm(y_all, stages["ffn_out1"].free, 0, sq=ffn_tmp)

        @block.vector
        def _(dve):
            step = Order(dve, dve_own)
            n = {"rms": 0, "v": 0, "unit": 0, "sink": 0, "vbuf": 0}

            def split(src, hi, lo, sem_, gain=None):
                step.wait()
                if gain is None:
                    step(nc.vector.tensor_copy(hi, src))
                    step.wait()
                    step(nc.vector.tensor_tensor(lo, src, f32(hi), ALU.subtract), sem_)
                else:
                    step(nc.vector.tensor_scalar(hi, src, gain, None, ALU.mult))
                    step.wait()
                    step(nc.vector.scalar_tensor_tensor(lo, src, gain, f32(hi), ALU.mult, ALU.subtract), sem_)

            def invert_rms(dst, src=rms, cols=T):
                n["rms"] += 1
                dve.wait_ge(rms_ready, n["rms"])
                step.wait()
                step(nc.vector.reciprocal(dst[:, 0:cols], src[:, 0:cols]), rms_used)

            def layer_input(src, gain, cols=T):
                for i in range(DT):
                    split(src[:, i, 0:cols], h_hi[:, i, 0:cols], h_lo[:, i, 0:cols], h_ready, gain(i))

            def add_norm(gain, next_gain=None):
                invert_rms(rstd)
                for i in range(DT):
                    step.wait()
                    t_ = normed[:, i % 2, :]
                    step(nc.vector.scalar_tensor_tensor(t_, y_all[:, i, :], gain(i), rstd[:], ALU.mult, ALU.mult))
                    step.wait()
                    step(nc.vector.tensor_tensor(x_res[:, i, :], x_res[:, i, :], t_, ALU.add), x_ready)
                    if next_gain is not None:
                        split(x_res[:, i, :], h_hi[:, i, :], h_lo[:, i, :], h_ready, next_gain(i))

            def take(st, c, dst):
                dve.wait_ge(slot_done, st.made(c))
                step.wait()
                step(nc.vector.tensor_copy(dst, acc[st.bank(c)][:]), st.free)

            def scaled(st, c, dst, factor=None):
                cols = dst.shape[-1]
                dve.wait_ge(slot_done, st.made(c))
                step.wait()
                src, by = acc[st.bank(c)][:, 0:cols], rstd_in[:, 0:cols]
                if factor is None:
                    step(nc.vector.tensor_tensor(dst, src, by, ALU.mult), st.free)
                else:
                    step(nc.vector.scalar_tensor_tensor(dst, src, factor, by, ALU.mult, ALU.mult), st.free)

            def feat_v(st, c, cols=T):
                if n["v"] >= 1:
                    dve.wait_ge(vt_done, n["v"])
                scaled(st, c, v_feat[:, c % 2, 0:cols])

            def tok_v(dst):
                n["v"] += 1
                dve.wait_ge(vt_done, n["v"])
                step.wait()
                blocks = dst.shape[1]
                step(nc.vector.tensor_copy(dst, ps_t[:, 0:blocks * P].rearrange("p (b n) -> p b n", n=P)), v_ready)

            def attention(units, p):
                u0 = n["unit"]

                def top(i):
                    if i >= len(units):
                        return
                    u, b = units[i], (u0 + i) % 3
                    dve.wait_ge(s_ready, u0 + i + 1)
                    if u.heads_bias is not None and u.heads_bias[1]:
                        h = u.heads_bias[0]
                        dve.wait_ge(bias_in[h % 2], 16 * (h // 2 + 1))
                        step.wait()
                        step(nc.vector.memset(toeplitz[0:CHUNK, h % 2, T - CHUNK:T], NEG))
                    if u0 + i >= 3:
                        dve.wait_ge(pt_made, u0 + i - 2)
                    step.wait()
                    step(nc.vector.tensor_tensor_reduce(p[:, b, 0:u.width], ps_s[(u0 + i) % 2][:, 0:u.width], u.bias, u.scale,
                                                        -3e38, ALU.add, ALU.max, small["row_max"][:, b:b + 1]), s_used)
                    step.wait()
                    if u.sink is None:
                        step(nc.vector.tensor_scalar(small["neg_max"][:, b:b + 1], small["row_max"][:, b:b + 1], -1.0, None,
                                                     ALU.mult), max_ready)
                    else:
                        step(nc.vector.tensor_scalar(small["neg_max"][:, b:b + 1], small["row_max"][:, b:b + 1], u.sink, -1.0,
                                                     ALU.max, ALU.mult), max_ready)

                def scale(i):
                    u, b = units[i], (u0 + i) % 3
                    total = small["row_sum"][:, b:b + 1]
                    dve.wait_ge(p_ready, u0 + i + 1)
                    if u.sink is not None:
                        n["sink"] += 1
                        dve.wait_ge(sink_ready, n["sink"])
                        step.wait()
                        step(nc.vector.tensor_scalar(total, total, small["sink_exp"][:, b:b + 1], None, ALU.add))
                    step.wait()
                    step(nc.vector.reciprocal(small["inv_sum"][:, b:b + 1], total))
                    step.wait()
                    step(nc.vector.tensor_scalar(p[:, b, 0:u.width], p[:, b, 0:u.width], small["inv_sum"][:, b:b + 1], None,
                                                 ALU.mult), pn_ready)

                def out_of(i):
                    if units[i].last:
                        dve.wait_ge(pv_done, u0 + i + 1)
                        step.wait()
                        step(nc.vector.tensor_copy(units[i].dst, ps_o[:]), o_taken)

                top(0)
                top(1)
                for i in range(len(units)):
                    scale(i)
                    top(i + 2)
                    if i:
                        out_of(i - 1)
                out_of(len(units) - 1)
                n["unit"] += len(units)

            for dst, value in [("eps_d", EPS), ("eps_q", HEAD_DIM * EPS), ("eps_v", EPS)]:
                step.wait()
                step(nc.vector.memset(small[dst][:], value), setup_done if dst == "eps_v" else None)
            dve.wait_ge(small_in, 80)
            layer_input(x_res, lambda i: param("norm1_g", i))
            step.wait()
            step(nc.vector.tensor_copy(masks[:], masks_f32[:]))
            step.wait()
            step(nc.vector.tensor_scalar(small["k_g8"][:], param("k_g"), float(HEAD_DIM) ** 0.5, None, ALU.mult))
            step.wait()
            c = PARAM_COLS["b_gate"]
            step(nc.vector.tensor_scalar(small["half_gate_b"][:], params[:, c:c + 16], 0.5, None, ALU.mult))
            lb = lambda d, l: params[:, PARAM_COLS["lb_logits"] + 16 * d + 8 * l:PARAM_COLS["lb_logits"] + 16 * d + 8 * l + 8]
            ex = lambda d, l: small["lb_exp"][:, 16 * d + 8 * l:16 * d + 8 * l + 8]
            for d in range(2):
                step.wait()
                step(nc.vector.tensor_tensor(small["lower"][:, 8 * d:8 * d + 8], lb(d, 0), lb(d, 1), ALU.max))
                for l in range(2):
                    step.wait()
                    step(nc.vector.tensor_tensor(ex(d, l), lb(d, l), small["lower"][:, 8 * d:8 * d + 8], ALU.subtract),
                         setup_done if d == 1 and l == 1 else None)

            invert_rms(rstd_in)
            st = stages["qkv"]
            plan = lagged(st.cbs, BANKS, 2 * DT)
            for c in range(st.cbs):
                if c < 2 * DT:
                    scaled(st, c, qk[:, c, :])
                else:
                    feat_v(st, c)
                for i in plan.get(c, []):
                    invert_rms(rstd)
                    step.wait()
                    step(nc.vector.scalar_tensor_tensor(qk[:, i, :], qk[:, i, :], param("q_g") if i < DT else
                                                        small["k_g8"][:], rstd[:], ALU.mult, ALU.mult), qk_ready)
                if c >= 2 * DT:
                    tok_v(v_tok1[:, :, (c - 2 * DT) * P:(c - 2 * DT + 1) * P])
            dve.wait_ge(setup_act, 1)
            for d in range(2):
                low, one = small["lower"][:, 8 * d:8 * d + 8], small["one_less"][:, 8 * d:8 * d + 8]
                step.wait()
                step(nc.vector.tensor_tensor(low, ex(d, 0), ex(d, 1), ALU.add))
                step.wait()
                step(nc.vector.reciprocal(one, low))
                step.wait()
                step(nc.vector.tensor_tensor(low, ex(d, 1), one, ALU.mult))
                step.wait()
                step(nc.vector.tensor_scalar(one, low, -1.0, 1.0, ALU.mult, ALU.add))
            attention(units1, probs)

            st = stages["conv"]
            cg, u, t_ = conv_tmp[:, 0, :], conv_tmp[:, 1, :], conv_tmp[:, 2, :]
            for i in range(DT):
                w = [param("conv_w", 8 * k + i) for k in range(3)]
                scaled(st, 3 * i, cg)
                scaled(st, 3 * i + 1, u)
                step.wait()
                step(nc.vector.tensor_tensor(u, u, cg, ALU.mult))
                step.wait()
                step(nc.vector.tensor_scalar(t_, u, w[2], param("conv_b", i), ALU.mult, ALU.add))
                step.wait()
                step(nc.vector.scalar_tensor_tensor(t_[:, 1:T], u[:, 0:T - 1], w[1], t_[:, 1:T], ALU.mult, ALU.add))
                step.wait()
                step(nc.vector.scalar_tensor_tensor(t_[:, 2:T], u[:, 0:T - 2], w[0], t_[:, 2:T], ALU.mult, ALU.add))
                scaled(st, 3 * i + 2, cg)
                step.wait()
                step(nc.vector.tensor_tensor(t_, cg, t_, ALU.mult))
                split(t_, y_hi[:, i, :], y_lo[:, i, :], y_ready)
            for i in range(DT):
                split(o_all[:, i, :], o_hi1[:, i, :], o_lo1[:, i, :], o_ready)
            for c in range(2 * DT):
                scaled(stages["gate"], c, gates[:, c, :])
            st = stages["proj"]
            dve.wait_ge(gate_ready, 2 * DT)
            for i in range(DT):
                for b in range(2):
                    g = gates[:, DT * b + i, :]
                    dve.wait_ge(slot_done, st.made(2 * i + b))
                    step.wait()
                    step(nc.vector.scalar_tensor_tensor(g, g, 1.0, acc[st.bank(2 * i + b)][:], ALU.add, ALU.mult), st.free)
                step.wait()
                step(nc.vector.tensor_tensor(gates[:, i, :], gates[:, i, :], gates[:, DT + i, :], ALU.add))
                split(gates[:, i, :], h_hi[:, i, :], h_lo[:, i, :], m_ready)
            st = stages["out"]
            for i in range(DT):
                dve.wait_ge(slot_done, st.made(i))
                step.wait()
                step(nc.vector.scalar_tensor_tensor(x_res[:, i, :], acc[st.bank(i)][:], 0.5, x_res[:, i, :], ALU.mult, ALU.add),
                     st.free)
            layer_input(x_res, lambda i: param("norm2_g", i))
            invert_rms(rstd_in)
            for half in range(2):
                st = stages[f"up{half}"]
                for i in range(HALF):
                    t_ = u_tmp[:, i % 2, :]
                    dve.wait_ge(slot_done, st.made(i))
                    step.wait()
                    step(nc.vector.scalar_tensor_tensor(t_, acc[st.bank(i)][:], 0.0, rstd_in[:], ALU.max, ALU.mult), st.free)
                    step.wait()
                    step(nc.vector.tensor_tensor(t_, t_, t_, ALU.mult))
                    split(t_, u_hi[:, i, :], u_lo[:, i, :], u_ready)
                if half == 1:
                    dve.wait_ge(mem_loaded, 16)
                    layer_input(mem, lambda i: param("mem_g", i), MEM)
                st = stages[f"down{half}"]
                for i in range(DT):
                    dve.wait_ge(slot_done, st.made(i))
                    step.wait()
                    step(nc.vector.tensor_tensor(x_res[:, i, :], acc[st.bank(i)][:], x_res[:, i, :], ALU.add), st.free)
            invert_rms(rstd_in, cols=MEM)
            st = stages["memkv"]
            for layer in range(2):
                for j in range(4):
                    scaled(st, 8 * layer + j, mem_k[layer][:, j, :])
                for j in range(4):
                    feat_v(st, 8 * layer + 4 + j, MEM)
                    tok_v(mem_v[layer][:, :, j * P:(j + 1) * P])

            def conv_mlp(layer, next_gain):
                invert_rms(rstd_in)
                st = stages[f"ffn_in{layer}"]

                def conv(i):
                    g, t_ = hid_tmp[:, i, :], ffn_tmp[:, i % 2, :]
                    w = [param("ffn_w", (3 * layer + k) * FF2 + i) for k in range(3)]
                    scaled(st, 2 * i, g)
                    step.wait()
                    step(nc.vector.tensor_scalar(t_, g, w[1], param("ffn_b", layer * FF2 + i), ALU.mult, ALU.add))
                    step.wait()
                    step(nc.vector.scalar_tensor_tensor(t_[:, 1:T], g[:, 0:T - 1], w[0], t_[:, 1:T], ALU.mult, ALU.add))
                    step.wait()
                    step(nc.vector.scalar_tensor_tensor(t_[:, 0:T - 1], g[:, 1:T], w[2], t_[:, 0:T - 1], ALU.mult, ALU.add),
                         conv_ready)

                def hidden(i):
                    up, t_ = hid_tmp[:, i, :], ffn_tmp[:, i % 2, :]
                    scaled(st, 2 * i + 1, up)
                    dve.wait_ge(gelu_ready, layer * FF2 + i + 1)
                    step.wait()
                    step(nc.vector.tensor_tensor(t_, up, t_, ALU.mult))
                    split(t_, hid_hi[:, i, :], hid_lo[:, i, :], hid_ready)

                for i in range(FF2):
                    conv(i)
                    hidden(i)
                st = stages[f"ffn_out{layer}"]
                for i in range(DT):
                    take(st, i, y_all[:, i, :])
                add_norm(lambda i: param("norm_g", 32 * layer + 24 + i), next_gain)

            def mixer_out(layer):
                for i in range(12):
                    split(o2[:, i, :], o_hi2[:, i, :], o_lo2[:, i, :], o_ready)
                st = stages["ab"[layer] + "_out"]
                for i in range(DT):
                    take(st, i, y_all[:, i, :])
                add_norm(lambda i: param("norm_g", 32 * layer + 8 + i), lambda i: param("norm_g", 32 * layer + 16 + i))

            layer_input(x_res, lambda i: param("norm_g", i))
            invert_rms(rstd_in)
            st = stages["a_in"]
            plan = lagged(st.cbs, BANKS, 10)
            for c in range(st.cbs):
                if c < 10:
                    scaled(st, c, q_win[:, c, :] if c < DT else k_win[:, c - DT, :],
                           float(HEAD_DIM) ** -0.5 if c < DT else None)
                elif c < 12:
                    feat_v(st, c)
                else:
                    scaled(st, c, xq[:, c - 12, :])
                for i in plan.get(c, []):
                    dst = q_win[:, i, :] if i < DT else k_win[:, i - DT, :]
                    dve.wait_ge(rope_rot, i + 1)
                    step.wait()
                    step(nc.vector.tensor_tensor(normed[:, 0, :], ps_t[:], rope[:, 1, :], ALU.mult), rope_done)
                    step.wait()
                    step(nc.vector.tensor_tensor(dst, dst, rope[:, 0, :], ALU.mult))
                    step.wait()
                    step(nc.vector.tensor_tensor(dst, dst, normed[:, 0, :], ALU.add), rope_ready)
                if 10 <= c < 12:
                    tok_v(v_win[:, :, (c - 10) * P:(c - 9) * P])
            attention(units_win, probs2)
            attention(units_x[0], probs2)
            mixer_out(0)
            conv_mlp(0, lambda i: param("norm_g", 32 + i))

            invert_rms(rstd_in)
            st = stages["b_in"]
            for j in range(X_HEADS):
                scaled(st, j, xq[:, j, :])
            attention(units_x[1], probs2)
            for s_ in (hg_s_f, hg_s_b):
                step.wait()
                step(nc.vector.memset(s_[:], 0.0))
            by_chunk = lambda ap: ap.rearrange("p (c t) -> p c t", t=HG_CHUNK)
            key, qd, grow, qb = (hg_key_f, hg_key_b), (hg_qd_f, hg_qd_b), (hg_grow_f, hg_grow_b), (hg_qb_f, hg_qb_b)
            small_of = lambda name, d: small[name + "_" + "fb"[d]]
            for t_ in [*hg_level_k, end_f, end_b]:
                step.wait()
                step(nc.vector.memset(t_[:], 0.0))

            def near_of(d, side, level):
                return (near_f, near_b)[d][:, (3 * side + level) * CHUNKS:(3 * side + level + 1) * CHUNKS]

            def head_in(h, j):
                if h < HG_HEADS:
                    scaled(st, X_HEADS + 5 * h + j, hg_in[h % 2][:, j, :])

            def head_decays(h):
                for d in range(2):
                    f_ = hg_in[h % 2][:, 2 + d, :]
                    i = 8 * d + h
                    dve.wait_ge(hg_sig, 2 * h + d + 1)
                    step.wait()
                    step(nc.vector.tensor_scalar(f_, f_, small["one_less"][:, i:i + 1], small["lower"][:, i:i + 1],
                                                 ALU.mult, ALU.add))
                    step.wait()
                    step(nc.vector.tensor_scalar(key[d][:], f_, -1.0, 1.0, ALU.mult, ALU.add), hg_f)
                for d in range(2):
                    b_ = hg_in[h % 2][:, 2 + d, :]
                    way = slice(None) if d == 0 else slice(None, None, -1)
                    dve.wait_ge(hg_ln, 2 * h + d + 1)
                    step.wait()
                    step(nc.vector.tensor_tensor_scan(b_[:, way], const("reset", T), b_[:, way], 0.0, ALU.mult, ALU.add),
                         hg_cum)
                for d in range(2):
                    b_, end, near = hg_in[h % 2][:, 2 + d, :], (end_f, end_b)[d], (near_f, near_b)[d]
                    step.wait()
                    step(nc.vector.tensor_copy(
                        end[:, 1:3 * CHUNKS + 1].rearrange("p (l c) -> p l c", c=CHUNKS),
                        by_chunk(b_)[:, :, 0 if d else HG_CHUNK - 1].unsqueeze(1).to_broadcast([P, 3, CHUNKS])))
                    for side in range(2):
                        back = d != side
                        way = slice(None, None, -1) if back else slice(None)
                        at_, reset = (2, 2 * CHUNKS) if back else (0, 0)
                        to = near[:, 3 * side * CHUNKS:3 * (side + 1) * CHUNKS]
                        step.wait()
                        step(nc.vector.tensor_tensor_scan(to[:, way], end[:, at_:at_ + 3 * CHUNKS][:, way],
                                                          const("span_reset", 5 * CHUNKS)[:, reset:reset + 3 * CHUNKS], 0.0,
                                                          ALU.add, ALU.mult))
                    dve.wait_ge(hg_exp, 4 * h + 2 * d + 2)
                    step.wait()
                    step(nc.vector.tensor_tensor(by_chunk(b_), end[:, 1:CHUNKS + 1].unsqueeze(2).to_broadcast(
                        [P, CHUNKS, HG_CHUNK]), by_chunk(b_), ALU.subtract), hg_rest)

            def head_queries(h):
                dve.wait_ge(hg_silu_q, h + 1)
                for d in range(2):
                    step.wait()
                    step(nc.vector.tensor_tensor(qd[d][:], qd[d][:], hg_in[h % 2][:, 0, :], ALU.mult))
                    step.wait()
                    step(nc.vector.tensor_tensor(grow[d][:], grow[d][:], key[d][:], ALU.mult))

            def head_levels(h):

                def decayed(dst, src, d, side, level, half, done=None):
                    by = near_of(d, side, level)
                    if half is None:
                        src, dst, by = by_chunk(src), by_chunk(dst), by.unsqueeze(2).to_broadcast([P, CHUNKS, HG_CHUNK])
                    else:
                        m = 2 << level
                        pick = lambda ap: ap.rearrange("p (s x c t) -> p s x c t", x=2, c=m, t=HG_CHUNK)[:, :, half]
                        src = pick(src)
                        dst = pick(dst) if side else dst.rearrange("p (s c t) -> p s c t", c=m, t=HG_CHUNK)
                        by = by.rearrange("p (s x c) -> p s x c", x=2, c=m)[:, :, half].unsqueeze(3).to_broadcast(
                            [P, CHUNKS // m // 2, m, HG_CHUNK])
                    step.wait()
                    step(nc.vector.tensor_tensor(dst, src, by, ALU.mult), done)

                for d in range(2):
                    rest = hg_in[h % 2][:, 2 + d, :]
                    dve.wait_ge(hg_rest_exp, 2 * h + d + 1)
                    step.wait()
                    step(nc.vector.tensor_tensor(rest, rest, key[d][:], ALU.mult))
                    for level in range(2):
                        decayed(hg_level_q[d][:, level, :], qd[d][:], d, 0, level, 1 - d)
                        decayed(hg_level_k[d][:, level, :], rest, d, 1, level, d)
                    decayed(hg_block_k[d][:], rest, d, 1, 2, None, hg_k if d else None)
                if h:
                    dve.wait_ge(hg_o, h)
                for d in range(2):
                    decayed(qb[d][:], qd[d][:], d, 0, 2, None)
                    before, decay, blk = near_of(d, 0, 2), small_of("decay", d), small_of("block", d)
                    at_ = slice(0 if d else BLOCK_CHUNKS - 1, None, BLOCK_CHUNKS)
                    step.wait()
                    step(nc.vector.tensor_tensor(blk[:], before[:, at_], decay[:, at_], ALU.mult))

            def head_scores(h, part):
                dve.wait_ge(hg_st, 3 * h + part + 1)
                into = [hg_s_f, hg_s_b]

                def keep(d, level, bank, at, done=None):
                    m = MASK_COLS["fb"[d] + str(level)]
                    mask = masks[:, m:m + (P if level == 0 else P // 2)]
                    if level == 0:
                        dst = into[d][:]
                        dims = [P, BLOCKS, P]
                        src = bank[:, at:at + T].rearrange("p (b n) -> p b n", n=P)
                        mask = mask.unsqueeze(1).to_broadcast(dims)
                    else:
                        half = HG_CHUNK << (level - 1)
                        spans = P // half // 2
                        dst = into[d][:].rearrange("p b (s x t) -> p b s x t", x=2, t=half)[:, :, :, 1 - d, :]
                        src = bank[:, at:at + T // 2].rearrange("p (b s t) -> p b s t", b=BLOCKS, t=half)
                        mask = mask.rearrange("p (s t) -> p s t", t=half).unsqueeze(1).to_broadcast(
                            [P, BLOCKS, spans, half])
                    step.wait()
                    step(nc.vector.copy_predicated(dst, mask, src), done)

                if part == 0:
                    keep(0, 0, ps_s[0], 0)
                    keep(0, 1, ps_s[1], 0)
                    keep(0, 2, ps_s[1], T // 2, hg_s)
                elif part == 1:
                    keep(0, 3, ps_s[0], 0)
                    keep(1, 3, ps_s[0], T // 2)
                    keep(1, 1, ps_s[1], 0)
                    keep(1, 2, ps_s[1], T // 2, hg_s)
                else:
                    keep(1, 0, ps_s[0], 0, hg_s)

            def head_states(h):
                for d, state in enumerate([hg_state_f, hg_state_b]):
                    dve.wait_ge(hg_u, 2 * h + d + 1)
                    blk = small_of("block", d)
                    u_ = ps_s[1 - d][:, 0:(BLOCKS - 1) * P].rearrange("p (b n) -> p b n", n=P)
                    for i in range(BLOCKS - 1):
                        b = BLOCKS - 2 - i if d else i
                        done = hg_chain if d and i == BLOCKS - 2 else None
                        step.wait()
                        if i == 0:
                            step(nc.vector.tensor_copy(state[:, b, :], u_[:, b, :]), done)
                        else:
                            over = b + d
                            step(nc.vector.scalar_tensor_tensor(state[:, b, :], state[:, b + 2 * d - 1, :], blk[:, over:over + 1],
                                                                u_[:, b, :], ALU.mult, ALU.add), done)

            def head_out(h):
                invert_rms(rstd_head, ffn_tmp[:, 1, :])
                step.wait()
                step(nc.vector.scalar_tensor_tensor(o2[:, h, :], ps_o[:], param("b_norm_g", h), rstd_head[:], ALU.mult, ALU.mult),
                     o_taken)
                dve.wait_ge(hg_silu_g, h + 1)
                step.wait()
                step(nc.vector.tensor_tensor(o2[:, h, :], o2[:, h, :], hg_in[h % 2][:, 4, :], ALU.mult))

            for j in range(5):
                head_in(0, j)
            for h in range(HG_HEADS):
                head_decays(h)
                head_in(h + 1, 0)
                head_queries(h)
                if h:
                    head_states(h - 1)
                head_in(h + 1, 1)
                head_levels(h)
                head_in(h + 1, 2)
                if h:
                    head_out(h - 1)
                head_scores(h, 0)
                head_in(h + 1, 3)
                head_scores(h, 1)
                head_in(h + 1, 4)
                head_scores(h, 2)
            head_states(HG_HEADS - 1)
            head_out(HG_HEADS - 1)
            mixer_out(1)
            conv_mlp(1, None)


def weight_tiles(w):
    k, n = w.shape
    return w.reshape(k // P, P, n // P, P).transpose(2, 0, 1, 3).reshape(-1, P, P)


def columns(a):
    return np.ascontiguousarray(a.reshape(-1, P).T)


def span_mask(i, half, d):
    queries = i[i // half % 2 == (1 if d == "f" else 0)]
    keys_in = i // half % 2 == (0 if d == "f" else 1)
    return keys_in[:, None] & (i[:, None] // half // 2 == queries[None, :] // half // 2)


def shape_constants():
    i = np.arange(P)
    q, k = i[:, None], i[None, :]
    rot = np.zeros((P, P), np.float32)
    half = HEAD_DIM // 2
    for m in range(P):
        if m % HEAD_DIM < half:
            rot[m + half, m] = -1.0
        else:
            rot[m - half, m] = 1.0
    mask = lambda keep: np.where(keep, 0.0, NEG)
    parts = {
        "ident": np.eye(P), "rot": rot, "pair_ones": q // HEAD_DIM == k // HEAD_DIM, "ones": np.ones((P, P)),
        "win_mask": np.concatenate([mask(k >= q), np.zeros((P, P)), mask(k <= q)], 1),
        "reset": np.broadcast_to(np.arange(T) % HG_CHUNK != 0, (P, T)),
        "span_reset": np.broadcast_to(np.concatenate([np.arange(CHUNKS) % n != 0 for n in (2, 4, 8, 4, 2)]), (P, 5 * CHUNKS)),
    }
    consts = np.concatenate([np.asarray(parts[c], np.float32) for c in CONST_COLS], 1)
    keep = {"f0": (q // HG_CHUNK == k // HG_CHUNK) & (q <= k), "b0": (q // HG_CHUNK == k // HG_CHUNK) & (q >= k),
            **{f"{d}{level}": span_mask(i, HG_CHUNK << (level - 1), d) for d in "fb" for level in range(1, 4)}}
    masks = np.concatenate([keep[c] for c in MASK_COLS], 1).astype(np.float32)
    inv = np.float32(10000.0) ** (-np.arange(half, dtype=np.float32) / np.float32(half))
    angle = (np.arange(T, dtype=np.float32)[None, :] * inv[i % half][:, None]).astype(np.float64)
    rope = np.stack([np.cos(angle), np.sin(angle)], 1).astype(np.float32)
    return consts, rope, masks


def layout(a):
    by_tile = lambda x: np.ascontiguousarray(x[0].T.reshape(DT, P, -1).transpose(1, 0, 2))
    blocks = {}
    for name in ["w_in", "w_gate", "w_attn_proj", "w_conv_proj", "w_out", "w_up", "w_down"]:
        blocks[name] = weight_tiles(a[name]).reshape(a[name].shape[1] // P, -1, P, P)
    win = blocks["w_in"]
    conv = [win[24 + 8 * part + i] for i in range(DT) for part in (1, 2, 0)]
    proj = [blocks[w][i] for i in range(DT) for w in ("w_attn_proj", "w_conv_proj")]
    perm = [4 * (2 * (s // 8) + s % 2) + (s % 8) // 2 for s in range(HEADS)]
    cols = np.concatenate([np.arange(h * HEAD_DIM, (h + 1) * HEAD_DIM) for h in perm])
    a_in, a_out = a["a_w_in_2"][0], a["a_w_out_2"][0]
    a_in = np.concatenate([a_in[:, cols], a_in[:, D:]], 1)
    a_out = np.concatenate([a_out[cols], a_out[D:]], 0)
    b_in = weight_tiles(a["b_w_in_2"][0]).reshape(-1, DT, P, P)
    b_in = [b_in[40 + i] for i in range(X_HEADS)] + [b_in[8 * part + h] for h in range(HG_HEADS) for part in range(5)]

    def ffn_in(layer):
        return weight_tiles(a["ffn_w_in_2"][layer]).reshape(2, FF2, DT, P, P).transpose(1, 0, 2, 3, 4)

    up, down = blocks["w_up"], blocks["w_down"]
    order = [win[:24], conv, blocks["w_gate"], proj, blocks["w_out"],
             up[:HALF], down[:, :HALF], up[HALF:], down[:, HALF:],
             weight_tiles(a["w_mem_kv_2"][0]), weight_tiles(a["w_mem_kv_2"][1]),
             weight_tiles(a_in), weight_tiles(a_out), ffn_in(0), weight_tiles(a["ffn_w_out_2"][0]),
             b_in, weight_tiles(a["b_w_out_2"][0]), ffn_in(1), weight_tiles(a["ffn_w_out_2"][1])]
    tiles = np.concatenate([np.asarray(o).reshape(-1, P, P) for o in order])
    at = 0
    for name, cbs, kt in STAGES:
        if name in LEAD:
            lead = tiles[at:at + BANKS * kt]
            tiles[at:at + BANKS * kt] = lead.reshape(BANKS, kt, P, P).transpose(1, 0, 2, 3).reshape(-1, P, P).copy()
        at += cbs * kt
    stream = np.ascontiguousarray(tiles.reshape(-1, SLOT_TILES, P, P).transpose(0, 2, 1, 3)).reshape(-1, P, SLOT_TILES * P)
    pair = lambda g: np.concatenate([g, g])
    params = np.concatenate([
        columns(a["norm1_g"]), columns(a["norm2_g"]), columns(pair(a["q_norm_g"])), columns(pair(a["k_norm_g"])),
        columns(a["conv_w"]), columns(a["conv_b"]), columns(a["b_gate"]), columns(a["norm_g_2"]), columns(a["mem_norm_g_2"]),
        columns(a["b_lb_logits_2"]), columns(a["b_norm_g_2"]), columns(a["ffn_conv_w_2"]), columns(a["ffn_conv_b_2"]),
        np.broadcast_to(a["a_sink_2"][0][perm][None, :], (P, HEADS))], 1)
    flipped = a["rel_bias"][:, ::-1]
    ext = np.concatenate([np.repeat(flipped[:, :1], T // 2 - 1, 1), flipped[:, :EXT_W - T // 2 + 1]], 1)
    consts, rope, masks = shape_constants()
    return {"stream": stream, "x_in": by_tile(a["x"]), "mem_in": by_tile(a["mem_2"]), "consts_in": consts, "rope_in": rope,
            "params_in": np.ascontiguousarray(params), "masks_in": masks, "ext_in": np.stack([ext[:, P - 1 - q:P - 1 - q + T] for q in range(P)], 1)}


def kernel(**inputs):
    import concourse.bacc as bacc
    from concourse.bass_utils import run_bass_kernel_spmd

    arrays = layout({k: np.asarray(v) for k, v in inputs.items()})
    nc = bacc.Bacc("TRN2", target_bir_lowering=False, num_devices=1)
    args = [nc.dram_tensor(k, v.shape, mybir.dt.from_np(v.dtype), kind="ExternalInput").ap() for k, v in arrays.items()]
    out = nc.dram_tensor("out", (P, DT, T), F32, kind="ExternalOutput").ap()
    build(nc, *args, out)
    result = run_bass_kernel_spmd(nc, [arrays], core_ids=[0]).results[0]["out"]
    return np.ascontiguousarray(result.transpose(1, 0, 2).reshape(1, D, T).transpose(0, 2, 1))
```

```python
from contextlib import ExitStack

import numpy as np

import concourse.bass as bass
from concourse import mybir

F32 = mybir.dt.float32
F32R = mybir.dt.float32r
ALU = mybir.AluOpType
ACT = mybir.ActivationFunctionType

P = 128
T = 512
D = 1024
DT = D // P
BLOCKS = T // P
EPS = 1e-6
NEG = -1e30

X_PARTS = 4
RING = 4
SLOT_TILES = 8
BANKS = 4

HEADS, HEAD_DIM, CHUNK, MAX_REL = 16, 64, 64, 256
FF1 = 4 * D
HALF = FF1 // P // 2
AHEAD = 3
P_BUFS = AHEAD + 2
EXT_W = 640
MEM = 256
KV_HEADS = 4
X_HEADS = 4
FF2 = 2816 // P
HG_HEADS, HG_CHUNK = 8, 16
CHUNKS = T // HG_CHUNK
BLOCK_CHUNKS = P // HG_CHUNK

LEAD = {"qkv", "up0", "memkv", "a_in", "a_out", "ffn_in0", "b_in", "b_out", "ffn_in1"}
STAGES = [
    ("qkv", 24, 8), ("conv", 24, 8), ("gate", 16, 8), ("proj", 16, 8), ("out", 8, 8),
    ("up0", HALF, 8), ("down0", 8, HALF), ("up1", HALF, 8), ("down1", 8, HALF),
    ("a_in", 16, 8), ("memkv", 16, 8), ("a_out", 8, 12), ("ffn_in0", 2 * FF2, 8), ("ffn_out0", 8, FF2),
    ("b_in", 44, 8), ("b_out", 8, 12), ("ffn_in1", 2 * FF2, 8), ("ffn_out1", 8, FF2),
]

PARAM_COLS = {}
_at = 0
for _name, _n in [
    ("norm1_g", 8), ("norm2_g", 8), ("q_g", 1), ("k_g", 1), ("conv_w", 24), ("conv_b", 8), ("b_gate", 16),
    ("norm_g", 64), ("mem_g", 8), ("lb_logits", 32), ("b_norm_g", 8), ("ffn_w", 2 * 3 * FF2), ("ffn_b", 2 * FF2),
    ("sink", 16),
]:
    PARAM_COLS[_name] = _at
    _at += _n
PARAM_W = _at

CONST_COLS = {}
_at = 0
for _name, _n in [
    ("ident", 128), ("rot", 128), ("pair_ones", 128), ("ones", 128), ("win_mask", 384), ("reset", 512), ("span_reset", 5 * CHUNKS),
]:
    CONST_COLS[_name] = _at
    _at += _n
CONST_W = _at

MASK_COLS = {}
_at = 0
for _name, _n in [(f"{d}{level}", P if level == 0 else P // 2) for d in "fb" for level in range(4)]:
    MASK_COLS[_name] = _at
    _at += _n
MASK_W = _at


class Stage:

    def __init__(self, name, cbs, kt, first_slot, first_cb, prev):
        self.name, self.cbs, self.kt = name, cbs, kt
        self.first_slot, self.first_cb, self.prev = first_slot, first_cb, prev
        self.slots = cbs * kt // SLOT_TILES
        self.lead = name in LEAD
        self.free = None

    def made(self, c):
        if self.lead and isinstance(c, int) and c < BANKS:
            return self.first_slot + BANKS * self.kt // SLOT_TILES
        if self.kt % SLOT_TILES == 0:
            return c * (self.kt // SLOT_TILES) + self.first_slot + self.kt // SLOT_TILES
        return self.first_slot + ((c + 1) * self.kt - 1) // SLOT_TILES + 1

    def bank(self, c):
        return (self.first_cb + c) % BANKS


class Order:

    def __init__(self, eng, own):
        self.eng, self.own, self.count, self.last = eng, own, {}, None

    def wait(self):
        if self.last is not None:
            self.eng.wait_ge(*self.last)

    def __call__(self, ins, sem=None):
        sem = self.own if sem is None else sem
        ins.then_inc(sem, 1)
        self.count[sem] = self.count.get(sem, 0) + 1
        self.last = (sem, self.count[sem])
        return self.last


def f32(ap):
    return ap.bitcast(F32)


class Joined:

    def __init__(self, first, tiles, second):
        self.first, self.tiles, self.second = first, tiles, second

    def __getitem__(self, index):
        _, k, cols = index
        return self.first[:, k, cols] if k < self.tiles else self.second[:, k - self.tiles, cols]


class Unit:

    def __init__(self, q, k, width, bias, scale, sink, v, out_part, out_cols, last, dst, heads_bias=None):
        self.q, self.k, self.width, self.bias, self.scale, self.sink = q, k, width, bias, scale, sink
        self.v, self.out_part, self.out_cols, self.last, self.dst = v, out_part, out_cols, last, dst
        self.heads_bias = heads_bias


def build(nc, stream, x_in, mem_in, consts_in, rope_in, params_in, masks_in, ext_in, out):
    stages = {}
    slot = cb = 0
    prev = None
    for name, cbs, kt in STAGES:
        prev = stages[name] = Stage(name, cbs, kt, slot, cb, prev)
        slot += prev.slots
        cb += cbs
        assert prev.cbs % BANKS == 0
    n_slots = slot
    assert n_slots % RING == 0

    with ExitStack() as ctx:
        def sem(name):
            return ctx.enter_context(nc.semaphore(name))

        KB = 1024
        base = (nc.sbuf_base + 63) // 64 * 64

        def sb(name, shape, offset, dtype=F32):
            return nc.alloc_sbuf_tensor_at(name, [P] + list(shape), dtype, offset=base + offset)

        w_raw = sb("w_raw", [RING, D], 0)
        w_hi = sb("w_hi", [RING, SLOT_TILES, P], 16 * KB, F32R)
        w_lo = sb("w_lo", [RING, SLOT_TILES, P], 32 * KB, F32R)
        x_res = sb("x_res", [DT, T], 48 * KB)
        h_hi = sb("h_hi", [DT, T], 64 * KB, F32R)
        h_lo = sb("h_lo", [DT, T], 80 * KB, F32R)
        consts = sb("consts", [CONST_W], 96 * KB)
        at = 96 * KB + -(-4 * CONST_W // 32) * 32
        masks = sb("masks", [MASK_W], at, mybir.dt.uint8)
        at += -(-MASK_W // 32) * 32
        params = sb("params", [PARAM_W], at)
        at += -(-4 * PARAM_W // 32) * 32
        small = {}
        for name, n in [("zero", 1), ("k_g8", 1), ("half_gate_b", 16), ("lower", 16), ("one_less", 16), ("eps_d", 1), ("eps_q", 1),
                        ("eps_v", 1), ("neg_sink", 16), ("neg_max", P_BUFS), ("row_sum", P_BUFS), ("sink_exp", P_BUFS), ("inv_sum", P_BUFS),
                        ("decay_f", CHUNKS), ("decay_b", CHUNKS),
                        ("block_f", BLOCKS), ("block_b", BLOCKS),
                        ("lb_exp", 32)]:
            small[name] = sb(name, [n], at)
            at += -(-4 * n // 32) * 32
        at = (at + 63) // 64 * 64
        rope = sb("rope", [2, T], at)
        ffn_tmp = sb("ffn_tmp", [2, T], at)
        at += 4 * KB
        rstd_in = sb("rstd_in", [T], at)
        at += 2 * KB
        arena = at
        assert base + arena + 96 * KB <= nc.sbuf_usable_end, (base + arena + 96 * KB, nc.sbuf_usable_end)

        def ar(name, shape, kb, dtype=F32):
            return sb(name, shape, arena + int(kb * KB), dtype)

        square = ar("square", [2, T], 70)
        rms = ar("rms", [T], 74)
        rstd = ar("rstd", [T], 56)
        normed = ar("normed", [2, T], 76)
        qk = ar("qk", [2 * DT, T], 0)
        v_tok1 = ar("v_tok1", [BLOCKS, D], 32)
        o_all = ar("o_all", [DT, T], 0)
        o_lo1 = ar("o_lo1", [DT, T], 0, F32R)
        o_hi1 = ar("o_hi1", [DT, T], 32, F32R)
        y_conv = ar("y_conv", [DT, T], 48)
        y_lo = ar("y_lo", [DT, T], 48, F32R)
        y_hi = ar("y_hi", [DT, T], 16, F32R)
        v_feat = ar("v_feat", [2, T], 64)
        toeplitz = ar("toeplitz", [2, T], 78)
        probs = ar("probs", [P_BUFS, T], 82)
        probs_t = ar("probs_t", [2, T], 92)
        gates = ar("gates", [2 * DT, T], 64)
        u_hi = ar("u_hi", [HALF, T], 0, F32R)
        u_lo = ar("u_lo", [HALF, T], 32, F32R)
        u_tmp = ar("u_tmp", [2, T], 64)
        mem = ar("mem", [DT, MEM], 80)
        mem_k = [ar(f"mem_k{i}", [X_HEADS, MEM], 80 + 8 * i) for i in range(2)]
        mem_v = [ar(f"mem_v{i}", [MEM // P, X_HEADS * P], 84 + 8 * i) for i in range(2)]
        o2 = ar("o2", [12, T], 0)
        o_lo2 = ar("o_lo2", [12, T], 0, F32R)
        o_hi2 = ar("o_hi2", [12, T], 24, F32R)
        o_hi3 = Joined(ar("o_hi_x", [X_HEADS, T], 24, F32R), X_HEADS, sb("o_hi_heads", [HG_HEADS, T], 80 * KB, F32R))
        q_win = ar("q_win", [DT, T], 24)
        k_win = ar("k_win", [2, T], 40)
        v_win = ar("v_win", [BLOCKS, KV_HEADS * HEAD_DIM], 44)
        xq = ar("xq", [X_HEADS, T], 48)
        probs2 = ar("probs2", [P_BUFS, T], 56)
        probs2_t = ar("probs2_t", [2, T], 66)
        y_all = sb("y_all", [DT, T], 64 * KB)
        hid_hi = ar("hid_hi", [FF2, T], 0, F32R)
        hid_lo = ar("hid_lo", [FF2, T], 44, F32R)
        hid_tmp = ar("hid_tmp", [FF2, T], 44)
        masks_f32 = ar("masks_f32", [MASK_W], 0)
        hg_in = [ar(f"hg_in{i}", [5, T], 24 + 10 * i) for i in range(2)]
        hg_v = ar("hg_v", [BLOCKS, P], 44)
        (hg_key_f, hg_key_b, hg_qd_f, hg_qd_b, hg_grow_f, hg_grow_b, hg_qb_f, hg_qb_b) = [
            ar(n, [T], 46 + 2 * i) for i, n in enumerate(
                ["hg_key_f", "hg_key_b", "hg_qd_f", "hg_qd_b", "hg_grow_f", "hg_grow_b", "hg_qb_f", "hg_qb_b"])]
        hg_s_f, hg_s_b, hg_ke_f, hg_ke_b = [ar(n, [BLOCKS, P], 62 + 2 * i) for i, n in enumerate(
            ["hg_s_f", "hg_s_b", "hg_ke_f", "hg_ke_b"])]
        hg_level_q = [ar(f"hg_level_q{d}", [2, T // 2], 70 + 2 * d) for d in range(2)]
        hg_level_k = [ar(f"hg_level_k{d}", [2, T], 74 + 4 * d) for d in range(2)]
        hg_block_k = [ar(f"hg_block_k{d}", [T], 82 + 2 * d) for d in range(2)]
        rstd_head = ar("rstd_head", [T], 88)
        hg_state_f = ar("hg_state_f", [BLOCKS - 1, P], 90)
        hg_state_b = ar("hg_state_b", [BLOCKS - 1, P], 92)
        near_f, near_b = ar("near_f", [6 * CHUNKS], 94), ar("near_b", [6 * CHUNKS], 94.75)
        end_f, end_b = ar("end_f", [3 * CHUNKS + 2], 93.5), ar("end_b", [3 * CHUNKS + 2], 95.5)

        def const(name, n=P):
            c = CONST_COLS[name]
            return consts[:, c:c + n]

        def param(name, i=0):
            c = PARAM_COLS[name]
            return params[:, c + i:c + i + 1]

        acc = [ctx.enter_context(nc.psum_tensor(f"acc{i}", [P, T], F32)) for i in range(BANKS)]
        ps_s = [ctx.enter_context(nc.psum_tensor(f"ps_s{i}", [P, T], F32)) for i in range(2)]
        ps_t = ctx.enter_context(nc.psum_tensor("ps_t", [P, T], F32))
        ps_o = ctx.enter_context(nc.psum_tensor("ps_o", [P, T], F32))

        params_loaded = sem("params_loaded")
        x_loaded = [sem(f"x_loaded{i}") for i in range(X_PARTS)]
        small_in = sem("small_in")
        masks_loaded = sem("masks_loaded")
        rope_loaded = sem("rope_loaded")
        mem_loaded = sem("mem_loaded")
        loaded = [sem(f"loaded{i}") for i in range(RING)]
        bias_in = [sem(f"bias_in{i}") for i in range(2)]
        hi_made = sem("hi_made")
        split_made = sem("split_made")
        slot_done = sem("slot_done")
        for s in stages.values():
            s.free = sem(f"free_{s.name}")
        dve_own = sem("dve_own")
        setup_done = sem("setup_done")
        setup_act = sem("setup_act")
        h_ready = sem("h_ready")
        o_ready = sem("o_ready")
        y_ready = sem("y_ready")
        m_ready = sem("m_ready")
        u_ready = sem("u_ready")
        hid_ready = sem("hid_ready")
        x_ready = sem("x_ready")
        sq_ready = sem("sq_ready")
        sq_used = sem("sq_used")
        y_sq = sem("y_sq")
        y_sq_used = sem("y_sq_used")
        y_sum = sem("y_sum")
        y_diag = sem("y_diag")
        y_rstd = sem("y_rstd")
        rms_ready = sem("rms_ready")
        rms_used = sem("rms_used")
        vt_done = sem("vt_done")
        v_ready = sem("v_ready")
        rope_rot = sem("rope_rot")
        rope_done = sem("rope_done")
        s_ready = sem("s_ready")
        s_used = sem("s_used")
        p_ready = sem("p_ready")
        sink_ready = sem("sink_ready")
        pn_ready = sem("pn_ready")
        pt_made = sem("pt_made")
        pt_ready = sem("pt_ready")
        pv_done = sem("pv_done")
        o_taken = sem("o_taken")
        gate_ready = sem("gate_ready")
        conv_ready = sem("conv_ready")
        qk_ready = sem("qk_ready")
        rope_ready = sem("rope_ready")
        gelu_ready = sem("gelu_ready")
        hg_sig = sem("hg_sig")
        hg_silu_q = sem("hg_silu_q")
        hg_silu_g = sem("hg_silu_g")
        hg_f = sem("hg_f")
        hg_ln = sem("hg_ln")
        hg_cum = sem("hg_cum")
        hg_exp = sem("hg_exp")
        hg_rest = sem("hg_rest")
        hg_rest_exp = sem("hg_rest_exp")
        hg_k = sem("hg_k")
        hg_st = sem("hg_st")
        hg_ket = sem("hg_ket")
        hg_s = sem("hg_s")
        hg_ke = sem("hg_ke")
        hg_u = sem("hg_u")
        hg_chain = sem("hg_chain")
        hg_o = sem("hg_o")
        stored = sem("stored")

        units1, units_win, units_x = [], [], [[], []]
        for h in range(HEADS):
            off = HEAD_DIM * (h % 2)
            for t in range(BLOCKS):
                units1.append(Unit(
                    q=qk[off:off + HEAD_DIM, h // 2, t * P:(t + 1) * P], k=qk[off:off + HEAD_DIM, DT + h // 2, 0:(t + 1) * P],
                    width=(t + 1) * P, bias=toeplitz[:, h % 2, T - (t + 1) * P:T], scale=1.0, sink=None,
                    v=[v_tok1[:, b, h * HEAD_DIM:(h + 1) * HEAD_DIM] for b in range(t + 1)],
                    out_part=off, out_cols=(t * P, (t + 1) * P), last=h % 2 == 1 and t == BLOCKS - 1,
                    dst=o_all[:, h // 2, :], heads_bias=(h, t == 0)))
            kv = 2 * (h // 8) + h % 2
            for t in range(BLOCKS):
                lo, hi = max(0, t - 1), min(BLOCKS, t + 2)
                m = CONST_COLS["win_mask"] + (lo - t + 1) * P
                units_win.append(Unit(
                    q=q_win[off:off + HEAD_DIM, h // 2, t * P:(t + 1) * P], k=k_win[off:off + HEAD_DIM, kv // 2, lo * P:hi * P],
                    width=(hi - lo) * P, bias=consts[:, m:m + (hi - lo) * P], scale=1.0, sink=(param("sink", h), small["neg_sink"][:, h:h + 1]),
                    v=[v_win[:, b, kv * HEAD_DIM:(kv + 1) * HEAD_DIM] for b in range(lo, hi)],
                    out_part=off, out_cols=(t * P, (t + 1) * P), last=h % 2 == 1 and t == BLOCKS - 1,
                    dst=o2[:, h // 2, :]))
        for layer in range(2):
            for h in range(X_HEADS):
                for t in range(BLOCKS):
                    units_x[layer].append(Unit(
                        q=xq[:, h, t * P:(t + 1) * P], k=mem_k[layer][:, h, :], width=MEM, bias=small["zero"][:].to_broadcast([P, MEM]),
                        scale=float(P) ** -0.5, sink=None, v=[mem_v[layer][:, b, h * P:(h + 1) * P] for b in range(MEM // P)],
                        out_part=0, out_cols=(t * P, (t + 1) * P), last=t == BLOCKS - 1,
                        dst=o2[:, h + (0 if layer else DT), :]))

        CONV_TILES = stages["conv"].cbs * DT // len(units1)
        conv_turn = lambda c: ((c + 1) * DT - 1) // CONV_TILES + 1
        XQ_FIRST, XQ_TILES = 13, 3
        xq_turn = lambda c: ((c - XQ_FIRST + 1) * DT - 1) // XQ_TILES + 1
        MEM_INPUT = xq_turn(stages["a_in"].cbs - 1)
        MEM_SUMS = MEM_INPUT + DT // 2 + 1
        MEM_LEAD = [MEM_INPUT + 1 + k for k in range(4)] + [MEM_SUMS, MEM_SUMS, MEM_SUMS + 1, MEM_SUMS + 2]
        MEM_FIRST, MEM_TILES = MEM_LEAD[-1] + 2, 3
        mem_turn = lambda c: MEM_FIRST + ((c - BANKS + 1) * DT - 1) // MEM_TILES + 1
        A_OUT_TURNS = [2, 3, 4, 5, 6, 7, 8, 9, 10, 12, 15]
        X_FIRST = len(units_win)
        B_IN_TILES = 3
        HEAD_TILES = [0, 8, 16, 26, 36, 40]
        b_in_turn = lambda j: ((j + 1) * DT - 1) // B_IN_TILES

        block = ctx.enter_context(nc.Block())

        @block.sync
        def _(sp):
            sp.dma_start(w_raw[:, 0, :], stream[0]).then_inc(loaded[0], 16)
            sp.dma_start(params[:], params_in).then_inc(params_loaded, 16)
            for i in range(X_PARTS):
                part = slice(i * DT // X_PARTS, (i + 1) * DT // X_PARTS)
                sp.dma_start(x_res[:, part, :], x_in[:, part, :]).then_inc(x_loaded[i], 16)
            sp.dma_start(w_raw[:, 1, :], stream[1]).then_inc(loaded[1], 16)
            sp.dma_start(consts[:], consts_in).then_inc(small_in, 16)
            for s in range(2, RING):
                sp.dma_start(w_raw[:, s, :], stream[s]).then_inc(loaded[s], 16)
            sp.dma_start(masks_f32[:], masks_in).then_inc(masks_loaded, 16)
            with sp.Fori(1, n_slots // RING, 1) as it:
                for s in range(RING):
                    sp.wait_ge(split_made, it * RING + (s + 1 - RING))
                    sp.dma_start(w_raw[:, s, :], stream[bass.ds(it * RING + s, 1)].rearrange("a p n -> p (a n)"))\
                        .then_inc(loaded[s], 16)
            for i in range(0, DT, 2):
                sp.wait_ge(x_ready, 3 * DT + i + 2)
                sp.dma_start(out[:, i:i + 2, :], x_res[:, i:i + 2, :]).then_inc(stored, 16)
            sp.wait_ge(stored, 16 * DT // 2)

        @block.gpsimd
        def _(pool):
            def split(it, s):
                pool.wait_ge(loaded[s], it * 16 + 16)
                if not isinstance(it, int):
                    pool.wait_ge(slot_done, it * RING + (s + 1 - RING))
                raw = w_raw[:, s, :]
                hi = w_hi[:, s, :, :].rearrange("p t n -> p (t n)")
                lo = w_lo[:, s, :, :].rearrange("p t n -> p (t n)")
                nc.gpsimd.tensor_tensor(hi, raw, small["zero"][:].to_broadcast([P, D]), ALU.add).then_inc(hi_made, 1)
                pool.wait_ge(hi_made, it * RING + (s + 2))
                nc.gpsimd.tensor_tensor(lo, raw, f32(hi), ALU.subtract).then_inc(split_made, 1)

            nc.gpsimd.memset(small["zero"][:], 0.0).then_inc(hi_made, 1)
            pool.wait_ge(hi_made, 1)
            for s in range(RING):
                split(0, s)
            with pool.Fori(1, n_slots // RING, 1) as it:
                for s in range(RING):
                    split(it, s)

        def lagged(cbs, first, upto):
            plan, nxt = {}, 0
            for c in range(first, cbs + 1):
                n_ = min(upto - nxt, upto if c == cbs else min(2, c - nxt))
                plan[c] = list(range(nxt, nxt + n_))
                nxt += n_
            return plan

        @block.tensor
        def _(pe):
            n = {"sq": 0, "y": 0, "rms": 0, "v": 0, "unit": 0, "o": 0, "h": 0}
            t_free = []

            def take_t(sem_, value):
                if t_free:
                    pe.wait_ge(*t_free[0])
                t_free[:] = [(sem_, value)]

            def three_passes(st, ps, s, t, x_hi, x_lo, k, cols):
                hi, lo = w_hi[:, s, t, :], w_lo[:, s, t, :]
                nc.tensor.matmul(ps, hi, x_hi[:, k, 0:cols], start=(k == 0), stop=False)
                nc.tensor.matmul(ps, hi, x_lo[:, k, 0:cols], start=False, stop=False)
                mm = nc.tensor.matmul(ps, lo, x_hi[:, k, 0:cols], start=False, stop=(k == st.kt - 1))
                if t == SLOT_TILES - 1:
                    mm.then_inc(slot_done, 1)

            def bank_free(st, c):
                if isinstance(c, int) and c < BANKS:
                    if st.prev is not None:
                        pe.wait_ge(st.prev.free, st.prev.cbs - BANKS + c + 1)
                else:
                    pe.wait_ge(st.free, c - (BANKS - 1))

            def products(st, it, body, j, x_hi, x_lo, cols=T, ready=None):
                bank_free(st, it * body + j)
                for k in range(st.kt):
                    tile = j * st.kt + k
                    if tile % SLOT_TILES == 0:
                        pe.wait_ge(split_made, it * (body * st.kt // SLOT_TILES) + (st.first_slot + tile // SLOT_TILES + 1))
                    if ready is not None:
                        ready(k)
                    three_passes(st, acc[st.bank(j)][:, 0:cols], (st.first_slot + tile // SLOT_TILES) % RING,
                                 tile % SLOT_TILES, x_hi, x_lo, k, cols)

            def lead_step(st, k, x_hi, x_lo, cols=T):
                for c in range(BANKS):
                    tile = k * BANKS + c
                    if k == 0:
                        bank_free(st, c)
                    if tile % SLOT_TILES == 0:
                        pe.wait_ge(split_made, st.first_slot + tile // SLOT_TILES + 1)
                    three_passes(st, acc[st.bank(c)][:, 0:cols], (st.first_slot + tile // SLOT_TILES) % RING,
                                 tile % SLOT_TILES, x_hi, x_lo, k, cols)

            def lead(st, x_hi, x_lo, ready, then=None):
                for k in range(st.kt):
                    ready(k)
                    lead_step(st, k, x_hi, x_lo)
                    if then is not None:
                        then(k)

            def block_tiles(st, first, end, x_hi, x_lo, cols=T):
                for tile in range(first, end):
                    c, k = divmod(tile, st.kt)
                    if k == 0:
                        bank_free(st, c)
                    if tile % SLOT_TILES == 0:
                        pe.wait_ge(split_made, st.first_slot + tile // SLOT_TILES + 1)
                    three_passes(st, acc[st.bank(c)][:, 0:cols], (st.first_slot + tile // SLOT_TILES) % RING,
                                 tile % SLOT_TILES, x_hi, x_lo, k, cols)

            def block_at(st, c, x_hi, x_lo):
                block_tiles(st, c * st.kt, (c + 1) * st.kt, x_hi, x_lo)

            def looped(st, body, x_hi, x_lo, ready=None, then=None):
                if st.lead:
                    lead(st, x_hi, x_lo, ready, then)
                else:
                    for j in range(body):
                        products(st, 0, body, j, x_hi, x_lo, T, ready if j == 0 else None)
                assert body % BANKS == 0 and body * st.kt // SLOT_TILES % RING == 0 and (body == BANKS or not st.lead)
                with pe.Fori(1, st.cbs // body, 1) as it:
                    for j in range(body):
                        products(st, it, body, j, x_hi, x_lo)

            def waits_for(sem_, first):
                return lambda k: pe.wait_ge(sem_, first + k + 1)

            def sum_square(i, tiles, ones, cols=T, sq=square):
                if i == 0:
                    n["rms"] += 1
                    take_t(rms_ready, n["rms"])
                pe.wait_ge(sq_ready, n["sq"] + 1)
                nc.tensor.matmul(ps_t[:, 0:cols], ones, sq[:, n["sq"] % sq.shape[1], 0:cols],
                                 start=(i == 0), stop=(i == tiles - 1)).then_inc(sq_used, 1)
                n["sq"] += 1

            def input_norm(k):
                for i in [k] if k < 5 else range(5, DT) if k == 5 else []:
                    sum_square(i, DT, const("ones"))

            def transpose_v(st, c, src, blocks=BLOCKS):
                n["v"] += 1
                take_t(v_ready, n["v"])
                pe.wait_ge(st.free, c + 1)
                for b in range(blocks):
                    mm = nc.tensor.transpose(ps_t[:, b * P:(b + 1) * P], src[:, b * P:(b + 1) * P], const("ident"))
                mm.then_inc(vt_done, 1)

            def rotate(st, i):
                take_t(rope_done, i + 1)
                pe.wait_ge(st.free, i + 1)
                src = q_win[:, i, :] if i < DT else k_win[:, i - DT, :]
                nc.tensor.matmul(ps_t[:], const("rot"), src, start=True, stop=True).then_inc(rope_rot, 1)

            def attention(units, p, p_t, also):
                u0 = n["unit"]

                def scores(i):
                    if i >= len(units):
                        return
                    u = units[i]
                    if u0 + i >= 2:
                        pe.wait_ge(s_used, u0 + i - 1)
                    nc.tensor.matmul(ps_s[(u0 + i) % 2][:, 0:u.width], u.q, u.k, start=True, stop=True).then_inc(s_ready, 1)

                def turn(i):
                    u = units[i]
                    take_t(pt_ready, u0 + i + 1)
                    pe.wait_ge(pn_ready, u0 + i + 1)
                    src = p[:, (u0 + i) % P_BUFS, :]
                    for b in range(u.width // P):
                        mm = nc.tensor.transpose(ps_t[:, b * P:(b + 1) * P], src[:, b * P:(b + 1) * P], const("ident"))
                    mm.then_inc(pt_made, 1)

                def weigh(i):
                    u = units[i]
                    if n["o"]:
                        pe.wait_ge(o_taken, n["o"])
                    pe.wait_ge(pt_ready, u0 + i + 1)
                    rows = u.v[0].shape[1]
                    for b in range(u.width // P):
                        mm = nc.tensor.matmul(ps_o[u.out_part:u.out_part + rows, u.out_cols[0]:u.out_cols[1]], u.v[b],
                                              p_t[:, (u0 + i) % 2, b * P:(b + 1) * P],
                                              start=(b == 0), stop=(b == u.width // P - 1))
                    mm.then_inc(pv_done, 1)
                    if u.last:
                        n["o"] += 1

                for i in range(AHEAD + 1):
                    scores(i)
                for i in range(len(units)):
                    scores(i + AHEAD + 1)
                    turn(i)
                    if i:
                        weigh(i - 1)
                    for work in also.get(i, []):
                        work()
                weigh(len(units) - 1)
                n["unit"] += len(units)

            st = stages["qkv"]
            def first_norm(k):
                if k == 0:
                    pe.wait_ge(small_in, 16)
                input_norm(k)

            lead(st, h_hi, h_lo, waits_for(h_ready, 0), first_norm)
            n["h"] += DT
            plan = lagged(st.cbs, BANKS, 2 * DT)
            for c in range(BANKS, st.cbs):
                block_at(st, c, h_hi, h_lo)
                for i in plan[c]:
                    sum_square(0, 1, const("pair_ones"))
                if c > 2 * DT:
                    transpose_v(st, c - 1, v_feat[:, (c - 1) % 2, :])
            transpose_v(st, st.cbs - 1, v_feat[:, (st.cbs - 1) % 2, :])
            pe.wait_ge(v_ready, n["v"])
            pe.wait_ge(qk_ready, 2 * DT)
            conv_st = stages["conv"]
            attention(units1, probs, probs_t, {
                i: [lambda i=i: block_tiles(conv_st, CONV_TILES * i, CONV_TILES * (i + 1), h_hi, h_lo)] for i in range(len(units1))})
            looped(stages["gate"], 4, h_hi, h_lo)
            st = stages["proj"]

            def proj(it):
                first = isinstance(it, int)
                for j in range(4):
                    if j % 2 == 0:
                        products(st, it, 4, j, o_hi1, o_lo1, ready=waits_for(o_ready, 0) if first and j == 0 else None)
                    else:
                        products(st, it, 4, j, y_hi, y_lo, ready=waits_for(y_ready, 0) if first and j == 1 else None)

            proj(0)
            with pe.Fori(1, st.cbs // 4, 1) as it:
                proj(it)
            looped(stages["out"], 4, h_hi, h_lo, ready=waits_for(m_ready, 0))
            for half in range(2):
                looped(stages[f"up{half}"], 4, h_hi, h_lo, ready=waits_for(h_ready, n["h"]),
                       then=input_norm if half == 0 else None)
                looped(stages[f"down{half}"], 4, u_hi, u_lo, ready=waits_for(u_ready, half * HALF))
            n["h"] += DT

            def post_norm():
                n["rms"] += 1
                n["y"] += 1
                take_t(rms_ready, n["rms"])
                pe.wait_ge(y_sq_used, DT * n["y"])
                for b in range(BLOCKS):
                    mm = nc.tensor.matmul(ps_t[:, b:b + 1], rstd_in[:, b * P:(b + 1) * P], const("ones")[:, 0:1],
                                          start=True, stop=True)
                mm.then_inc(y_sum, 1)
                pe.wait_ge(o_taken, n["o"])
                pe.wait_ge(y_diag, n["y"])
                nc.tensor.matmul(ps_o[:], const("ones"), normed[:, 1, :], start=True, stop=True).then_inc(y_rstd, 1)
                n["o"] += 1

            def conv_mlp(layer):
                looped(stages[f"ffn_in{layer}"], 4, h_hi, h_lo, ready=waits_for(h_ready, n["h"]), then=input_norm)
                n["h"] += DT
                st = stages[f"ffn_out{layer}"]
                for c in range(st.cbs):
                    if c == 0:
                        products(st, 0, st.cbs, 0, hid_hi, hid_lo, ready=waits_for(hid_ready, layer * FF2))
                    else:
                        block_at(st, c, hid_hi, hid_lo)
                post_norm()

            def mixer_out(st, x_hi):
                for c in range(BANKS, st.cbs):
                    block_at(st, c, x_hi, o_lo2)
                post_norm()

            st = stages["a_in"]
            lead(st, h_hi, h_lo, waits_for(h_ready, n["h"]), input_norm)
            n["h"] += DT
            plan = lagged(XQ_FIRST, BANKS, 10)
            for c in range(BANKS, XQ_FIRST):
                block_at(st, c, h_hi, h_lo)
                for i in plan[c]:
                    rotate(st, i)
                if 11 <= c <= 12:
                    transpose_v(st, c - 1, v_feat[:, (c - 1) % 2, :])
            pe.wait_ge(rope_ready, 10)

            mem_st = stages["memkv"]

            def mem_sums():
                for i in range(DT):
                    sum_square(i, DT, const("ones"), MEM, mem)

            def mem_lead(k):
                pe.wait_ge(h_ready, 3 * DT + k + 1)
                lead_step(mem_st, k, h_hi, h_lo, MEM)

            also = {i: [] for i in range(len(units_win) + len(units_x[0]))}
            first_xq, end_xq = XQ_FIRST * DT, st.cbs * DT
            for i, a in enumerate(range(first_xq, end_xq, XQ_TILES)):
                also[i].append(lambda a=a: block_tiles(st, a, min(a + XQ_TILES, end_xq), h_hi, h_lo))
            also[MEM_SUMS].append(mem_sums)
            for k in range(DT):
                also[MEM_LEAD[k]].append(lambda k=k: mem_lead(k))
            for c in range(BANKS, mem_st.cbs):
                if c % 8 >= 4:
                    also[mem_turn(c) + 1].append(lambda c=c: transpose_v(mem_st, c, normed[:, c % 2, :], MEM // P))
            for i in range((mem_st.cbs - BANKS) * DT // MEM_TILES):
                first = BANKS * DT + MEM_TILES * i
                also[MEM_FIRST + i].append(lambda first=first: block_tiles(mem_st, first, first + MEM_TILES, h_hi, h_lo, MEM))
            def mem_ready():
                pe.wait_ge(stages["a_in"].free, stages["a_in"].cbs)
                pe.wait_ge(mem_st.free, mem_st.cbs)

            also[X_FIRST - AHEAD - 2].append(mem_ready)
            out_st = stages["a_out"]

            def out_lead(k):
                pe.wait_ge(o_ready, DT + k + 1)
                lead_step(out_st, k, o_hi2, o_lo2)

            for k, turn_ in enumerate(A_OUT_TURNS):
                also[X_FIRST + turn_].append(lambda k=k: out_lead(k))
            n["h"] += DT
            attention(units_win + units_x[0], probs2, probs2_t, also)
            st = out_st
            for k in range(len(A_OUT_TURNS), st.kt):
                out_lead(k)
            mixer_out(st, o_hi2)
            conv_mlp(0)
            st = stages["b_in"]
            lead(st, h_hi, h_lo, waits_for(h_ready, n["h"]), input_norm)
            n["h"] += DT
            def head_in(h, j):
                if h < HG_HEADS:
                    first = (X_HEADS + 5 * h) * DT
                    block_tiles(st, first + HEAD_TILES[j], first + HEAD_TILES[j + 1], h_hi, h_lo)
                else:
                    out_lead(2 * j)
                    out_lead(2 * j + 1)

            def out_lead(k):
                pe.wait_ge(o_ready, DT + 12 + k + 1)
                lead_step(stages["b_out"], k, o_hi3, o_lo2)

            first = X_HEADS * DT
            block_tiles(st, first, first + B_IN_TILES, h_hi, h_lo)
            pe.wait_ge(st.free, X_HEADS)
            attention(units_x[1], probs2, probs2_t, {
                i: [lambda a=a: block_tiles(st, first + a, first + min(a + B_IN_TILES, 5 * DT), h_hi, h_lo)]
                for i, a in enumerate(range(B_IN_TILES, 5 * DT, B_IN_TILES))})

            def head_scores(h, part):
                pe.wait_ge(hg_k, h + 1)
                qd, key, rest = (hg_qd_f, hg_qd_b), (hg_grow_f, hg_grow_b), hg_in[h % 2][:, 2:4, :]

                def own(d, bank, at):
                    for b in range(BLOCKS):
                        mm = nc.tensor.matmul(bank[:, at + b * P:at + (b + 1) * P], key[d][:, b * P:(b + 1) * P],
                                              qd[d][:, b * P:(b + 1) * P], start=True, stop=True)
                    return mm

                def level(d, i, bank, at):
                    half = HG_CHUNK << i
                    for b in range(BLOCKS):
                        cols = slice(b * P, (b + 1) * P)
                        if i == 0:
                            k_ = rest[:, d, cols]
                            q_ = qd[d][:, cols].rearrange("p (s x t) -> p s x t", x=2, t=half)[:, :, 1 - d, :]
                        else:
                            k_, q_ = hg_level_k[d][:, i - 1, cols], hg_level_q[d][:, i - 1, b * P // 2:(b + 1) * P // 2]
                        mm = nc.tensor.matmul(bank[:, at + b * P // 2:at + (b + 1) * P // 2], k_, q_, start=True, stop=True)
                    return mm

                if part == 0:
                    if h:
                        pe.wait_ge(hg_chain, h)
                    else:
                        pe.wait_ge(s_used, n["unit"])
                    own(0, ps_s[0], 0)
                    level(0, 0, ps_s[1], 0)
                    mm = level(0, 1, ps_s[1], T // 2)
                else:
                    pe.wait_ge(hg_s, 3 * h + part)
                    if part == 1:
                        level(0, 2, ps_s[0], 0)
                        level(1, 2, ps_s[0], T // 2)
                        level(1, 0, ps_s[1], 0)
                        mm = level(1, 1, ps_s[1], T // 2)
                    else:
                        mm = own(1, ps_s[0], 0)
                mm.then_inc(hg_st, 1)

            def head_keys(h, d):
                take_t(hg_ke, 2 * h + d + 1)
                for b in range(BLOCKS):
                    mm = nc.tensor.transpose(ps_t[:, b * P:(b + 1) * P], hg_block_k[d][:, b * P:(b + 1) * P], const("ident"))
                mm.then_inc(hg_ket, 1)

            def head_updates(h, d):
                bank = ps_s[1 - d]
                pe.wait_ge(v_ready, v0 + h + 1)
                pe.wait_ge(hg_s, 3 * h + 2 + d)
                pe.wait_ge(hg_ke, 2 * h + d + 1)
                for b in range(BLOCKS - 1):
                    src = b + d
                    mm = nc.tensor.matmul(bank[:, b * P:(b + 1) * P], [hg_ke_f, hg_ke_b][d][:, src, :], hg_v[:, src, :],
                                          start=True, stop=True)
                mm.then_inc(hg_u, 1)

            def head_out(h):
                pe.wait_ge(hg_chain, h + 1)
                pe.wait_ge(o_taken, n["o"])
                for b in range(BLOCKS):
                    cols = slice(b * P, (b + 1) * P)
                    parts = [(hg_v[:, b, :], hg_s_f[:, b, :]), (hg_v[:, b, :], hg_s_b[:, b, :])]
                    if b:
                        parts.append((hg_state_f[:, b - 1, :], hg_qb_f[:, cols]))
                    if b < BLOCKS - 1:
                        parts.append((hg_state_b[:, b, :], hg_qb_b[:, cols]))
                    for i, (left, right) in enumerate(parts):
                        mm = nc.tensor.matmul(ps_o[:, cols], left, right, start=(i == 0), stop=(i == len(parts) - 1))
                mm.then_inc(hg_o, 1)
                n["o"] += 1

            v0 = n["v"]
            for h in range(HG_HEADS):
                head_in(h + 1, 0)
                if h:
                    head_updates(h - 1, 1)
                head_in(h + 1, 1)
                if h:
                    head_out(h - 1)
                transpose_v(st, X_HEADS + 5 * h + 1, hg_in[h % 2][:, 1, :])
                head_in(h + 1, 2)
                if h:
                    sum_square(0, 1, const("ones"), sq=ffn_tmp[:, 0:1, :])
                else:
                    head_in(1, 3)
                    head_in(1, 4)
                head_scores(h, 0)
                head_keys(h, 0)
                if h:
                    head_in(h + 1, 3)
                head_scores(h, 1)
                head_keys(h, 1)
                if h:
                    head_in(h + 1, 4)
                head_scores(h, 2)
                head_updates(h, 0)
            head_updates(HG_HEADS - 1, 1)
            out_lead(10)
            head_out(HG_HEADS - 1)
            sum_square(0, 1, const("ones"), sq=ffn_tmp[:, 0:1, :])
            out_lead(11)
            mixer_out(stages["b_out"], o_hi3)
            conv_mlp(1)

        @block.scalar
        def _(act):
            n = {"sq": 0, "y": 0, "rms": 0, "unit": 0}

            def squared(src, cols=T, sq=square):
                bufs = sq.shape[1]
                if n["sq"] >= bufs:
                    act.wait_ge(sq_used, n["sq"] - bufs + 1)
                nc.scalar.activation(sq[:, n["sq"] % bufs, 0:cols], src, ACT.Square).then_inc(sq_ready, 1)
                n["sq"] += 1

            def post_norm(st, sq=square):
                for i in range(DT):
                    if i < 2:
                        act.wait_ge(sq_used, n["sq"])
                    else:
                        act.wait_ge(y_sq_used, DT * n["y"] + i - 1)
                    if i < DT - 1:
                        act.wait_ge(st.free, i + 1)
                        src = y_all[:, i, :]
                    else:
                        act.wait_ge(slot_done, st.made(i))
                        src = acc[st.bank(i)][:]
                    nc.scalar.activation(sq[:, i % 2, :], src, ACT.Square).then_inc(y_sq, 1)
                n["y"] += 1
                root(n["y"], 1.0 / D, small["eps_d"][:], BLOCKS, summed=y_sum)

            def root(sums, scale, eps, cols=T, dst=rms, summed=sq_used):
                act.wait_ge(summed, sums)
                if n["rms"]:
                    act.wait_ge(rms_used, n["rms"])
                nc.scalar.activation(dst[:, 0:cols], ps_t[:, 0:cols], ACT.Sqrt, scale=scale, bias=eps).then_inc(rms_ready, 1)
                n["rms"] += 1

            def norm(src, sem_, first, cols=T, sq=square):
                for i in range(DT):
                    act.wait_ge(sem_, first + i + 1)
                    squared(src[:, i, 0:cols], cols, sq)
                root(n["sq"], 1.0 / D, small["eps_d"][:], cols)

            def attention(units, p, p_t, also):
                u0 = n["unit"]

                def exps(i):
                    if i >= len(units):
                        return
                    u, b = units[i], (u0 + i) % P_BUFS
                    act.wait_ge(s_used, u0 + i + 1)
                    nc.scalar.activation(p[:, b, 0:u.width], p[:, b, 0:u.width], ACT.Exp, scale=-1.0,
                                         bias=small["neg_max"][:, b:b + 1],
                                         accum_out=small["row_sum"][:, b:b + 1]).then_inc(p_ready, 1)
                    if u.sink is not None:
                        nc.scalar.activation(small["sink_exp"][:, b:b + 1], u.sink[0], ACT.Exp,
                                             bias=small["neg_max"][:, b:b + 1]).then_inc(sink_ready, 1)
                    if u.heads_bias is not None and i >= BLOCKS:
                        load_bias(i + BLOCKS)

                def take(i):
                    u, b = units[i], (u0 + i) % 2
                    act.wait_ge(pt_made, u0 + i + 1)
                    if u0 + i >= 2:
                        act.wait_ge(pv_done, u0 + i - 1)
                    nc.scalar.activation(p_t[:, b, 0:u.width], ps_t[:, 0:u.width], ACT.Copy).then_inc(pt_ready, 1)

                def load_bias(i):
                    if i >= len(units) or not units[i].heads_bias[1]:
                        return
                    h = units[i].heads_bias[0]
                    if h >= 2:
                        act.wait_ge(s_used, u0 + i - BLOCKS)
                    act.dma_start(toeplitz[:, h % 2, :], ext_in[h]).then_inc(bias_in[h % 2], 16)

                if units[0].heads_bias is not None:
                    load_bias(0)
                    load_bias(BLOCKS)
                for i in range(AHEAD):
                    exps(i)
                for i in range(len(units)):
                    take(i)
                    exps(i + AHEAD)
                    if i in also:
                        also[i]()
                n["unit"] += len(units)

            act.wait_ge(setup_done, 1)
            for i in range(DT):
                act.wait_ge(x_loaded[X_PARTS * i // DT], 16)
                squared(x_res[:, i, :])
            root(DT, 1.0 / D, small["eps_d"][:])
            st = stages["qkv"]
            for c in range(2 * DT + 1):
                if c < 2 * DT:
                    act.wait_ge(st.free, c + 1)
                    squared(qk[:, c, :])
                if c:
                    root(DT + c, 1.0, small["eps_q"][:])
            act.wait_ge(setup_done, 2)
            nc.scalar.activation(small["lb_exp"][:], small["lb_exp"][:], ACT.Exp).then_inc(setup_act, 1)
            attention(units1, probs, probs_t, {})
            for c in range(2 * DT):
                act.wait_ge(stages["gate"].free, c + 1)
                nc.scalar.activation(gates[:, c, :], gates[:, c, :], ACT.Tanh, scale=0.5,
                                     bias=small["half_gate_b"][:, c:c + 1]).then_inc(gate_ready, 1)
            norm(x_res, stages["out"].free, 0)
            act.dma_start(mem[:], mem_in).then_inc(mem_loaded, 16)
            act.wait_ge(y_ready, DT)
            act.dma_start(rope[:], rope_in).then_inc(rope_loaded, 16)

            def gelus(layer):
                for i in range(FF2):
                    act.wait_ge(conv_ready, layer * FF2 + i + 1)
                    t_ = ffn_tmp[:, i % 2, :]
                    nc.scalar.activation(t_, t_, ACT.Gelu_apprx_tanh).then_inc(gelu_ready, 1)

            norm(x_res, stages["down1"].free, 0)

            def mem_squares(tiles):
                for i in tiles:
                    act.wait_ge(h_ready, 3 * DT + i + 1)
                    squared(mem[:, i, :], MEM, mem)

            also = {MEM_INPUT + 1 + i // 2: lambda i=i: mem_squares([i, i + 1]) for i in range(0, DT, 2)}
            also[MEM_SUMS] = lambda: root(n["sq"], 1.0 / D, small["eps_d"][:], MEM)
            attention(units_win + units_x[0], probs2, probs2_t, also)
            post_norm(stages["a_out"])
            norm(x_res, x_ready, 0)
            gelus(0)
            post_norm(stages["ffn_out0"], sq=ffn_tmp)
            norm(x_res, x_ready, DT)
            attention(units_x[1], probs2, probs2_t, {})
            st = stages["b_in"]
            v0 = DT + 8 + 2

            def head_act(h, j, func, done):
                if 0 <= h < HG_HEADS:
                    act.wait_ge(st.free, X_HEADS + 5 * h + j + 1)
                    t_ = hg_in[h % 2][:, j, :]
                    nc.scalar.activation(t_, t_, func).then_inc(done, 1)

            def head_in(h):
                for j in (2, 3):
                    head_act(h, j, ACT.Sigmoid, hg_sig)
                head_act(h, 0, ACT.Silu, hg_silu_q)
                head_act(h - 1, 4, ACT.Silu, hg_silu_g)

            def head_square(h):
                act.wait_ge(hg_o, h + 1)
                squared(ps_o[:], sq=ffn_tmp[:, 0:1, :])

            def head_root():
                root(n["sq"], 1.0 / P, small["eps_v"][:], dst=ffn_tmp[:, 1, :])

            def head_keys(h, d):
                act.wait_ge(hg_ket, 2 * h + d + 1)
                if h:
                    act.wait_ge(hg_u, 2 * h - 1 + d)
                nc.scalar.activation([hg_ke_f, hg_ke_b][d][:].rearrange("p b n -> p (b n)"), ps_t[:], ACT.Copy).then_inc(hg_ke, 1)

            head_in(0)
            for h in range(HG_HEADS):
                for d in range(2):
                    act.wait_ge(hg_f, 2 * h + d + 1)
                    f_ = hg_in[h % 2][:, 2 + d, :]
                    nc.scalar.activation(f_, f_, ACT.Ln).then_inc(hg_ln, 1)
                for d, (qd, grow) in enumerate([(hg_qd_f, hg_grow_f), (hg_qd_b, hg_grow_b)]):
                    act.wait_ge(hg_cum, 2 * h + d + 1)
                    b_ = hg_in[h % 2][:, 2 + d, :]
                    nc.scalar.activation(qd[:], b_, ACT.Exp).then_inc(hg_exp, 1)
                    nc.scalar.activation(grow[:], b_, ACT.Exp, scale=-1.0).then_inc(hg_exp, 1)
                for d, way in enumerate("fb"):
                    act.wait_ge(hg_rest, 2 * h + d + 1)
                    end, near, rest = (end_f, end_b)[d][:, 1:CHUNKS + 1], (near_f, near_b)[d][:], hg_in[h % 2][:, 2 + d, :]
                    nc.scalar.activation(small["decay_" + way][:], end, ACT.Exp)
                    nc.scalar.activation(near, near, ACT.Exp)
                    nc.scalar.activation(rest, rest, ACT.Exp).then_inc(hg_rest_exp, 1)
                if h:
                    head_square(h - 1)
                act.wait_ge(vt_done, v0 + h + 1)
                nc.scalar.activation(hg_v[:].rearrange("p b n -> p (b n)"), ps_t[:], ACT.Copy).then_inc(v_ready, 1)
                if h:
                    head_root()
                head_keys(h, 0)
                head_in(h + 1)
                head_keys(h, 1)
            head_square(HG_HEADS - 1)
            head_root()
            post_norm(stages["b_out"])
            norm(x_res, x_ready, 2 * DT)
            gelus(1)
            post_norm(stages["ffn_out1"], sq=ffn_tmp)

        @block.vector
        def _(dve):
            step = Order(dve, dve_own)
            n = {"y": 0, "rms": 0, "v": 0, "unit": 0, "sink": 0}

            def split(src, hi, lo, sem_, gain=None):
                step.wait()
                if gain is None:
                    step(nc.vector.tensor_copy(hi, src))
                    step.wait()
                    step(nc.vector.tensor_tensor(lo, src, f32(hi), ALU.subtract), sem_)
                else:
                    step(nc.vector.tensor_scalar(hi, src, gain, None, ALU.mult))
                    step.wait()
                    step(nc.vector.scalar_tensor_tensor(lo, src, gain, f32(hi), ALU.mult, ALU.subtract), sem_)

            def invert_rms(dst, src=rms, cols=T):
                n["rms"] += 1
                dve.wait_ge(rms_ready, n["rms"])
                step.wait()
                step(nc.vector.reciprocal(dst[:, 0:cols], src[:, 0:cols]), rms_used)

            def layer_input(src, gain, cols=T, tiles=range(DT)):
                for i in tiles:
                    split(src[:, i, 0:cols], h_hi[:, i, 0:cols], h_lo[:, i, 0:cols], h_ready, gain(i))

            def add_norm(gain, next_gain=None):
                n["y"] += 1
                invert_rms(rstd, cols=BLOCKS)
                step.wait()
                dims = [P, BLOCKS, P]
                step(nc.vector.tensor_tensor(normed[:, 1, :].rearrange("p (b n) -> p b n", n=P),
                                             const("ident").unsqueeze(1).to_broadcast(dims),
                                             rstd[:, 0:BLOCKS].unsqueeze(2).to_broadcast(dims), ALU.mult), y_diag)
                dve.wait_ge(y_rstd, n["y"])
                for i in range(DT):
                    step.wait()
                    t_ = normed[:, i % 2, :]
                    step(nc.vector.scalar_tensor_tensor(t_, y_all[:, i, :], gain(i), ps_o[:], ALU.mult, ALU.mult),
                         o_taken if i == DT - 1 else None)
                    step.wait()
                    step(nc.vector.tensor_tensor(x_res[:, i, :], x_res[:, i, :], t_, ALU.add), x_ready)
                    if next_gain is not None:
                        split(x_res[:, i, :], h_hi[:, i, :], h_lo[:, i, :], h_ready, next_gain(i))

            def take(st, c, dst):
                dve.wait_ge(slot_done, st.made(c))
                step.wait()
                step(nc.vector.tensor_copy(dst, acc[st.bank(c)][:]), st.free)

            def take_y(st, sq):
                for i in range(DT + 1):
                    if i < DT - 1:
                        take(st, i, y_all[:, i, :])
                    if i:
                        dve.wait_ge(y_sq, DT * n["y"] + i)
                        step.wait()
                        if i == 1:
                            step(nc.vector.tensor_copy(rstd_in[:], sq[:, 0, :]), y_sq_used)
                        else:
                            step(nc.vector.tensor_tensor(rstd_in[:], rstd_in[:], sq[:, (i - 1) % 2, :], ALU.add), y_sq_used)
                take(st, DT - 1, y_all[:, DT - 1, :])

            def scaled(st, c, dst, factor=None):
                cols = dst.shape[-1]
                dve.wait_ge(slot_done, st.made(c))
                step.wait()
                src, by = acc[st.bank(c)][:, 0:cols], rstd_in[:, 0:cols]
                if factor is None:
                    step(nc.vector.tensor_tensor(dst, src, by, ALU.mult), st.free)
                else:
                    step(nc.vector.scalar_tensor_tensor(dst, src, factor, by, ALU.mult, ALU.mult), st.free)

            def feat_v(st, c, buf, cols=T):
                if n["v"] >= 1:
                    dve.wait_ge(vt_done, n["v"])
                scaled(st, c, buf[:, c % 2, 0:cols])

            def tok_v(dst):
                n["v"] += 1
                dve.wait_ge(vt_done, n["v"])
                step.wait()
                blocks = dst.shape[1]
                step(nc.vector.tensor_copy(dst, ps_t[:, 0:blocks * P].rearrange("p (b n) -> p b n", n=P)), v_ready)

            def attention(units, p, also):
                u0 = n["unit"]

                def top(i):
                    u, b = units[i], (u0 + i) % P_BUFS
                    dve.wait_ge(s_ready, u0 + i + 1)
                    if u.heads_bias is not None and u.heads_bias[1]:
                        h = u.heads_bias[0]
                        dve.wait_ge(bias_in[h % 2], 16 * (h // 2 + 1))
                        dve.wait_ge(*step(nc.vector.memset(toeplitz[0:CHUNK, h % 2, T - CHUNK:T], NEG)))
                    if u0 + i >= P_BUFS:
                        dve.wait_ge(pt_made, u0 + i - P_BUFS + 1)
                    step(nc.vector.tensor_tensor_reduce(p[:, b, 0:u.width], ps_s[(u0 + i) % 2][:, 0:u.width], u.bias, -u.scale,
                                                        3e38 if u.sink is None else u.sink[1], ALU.add, ALU.min,
                                                        small["neg_max"][:, b:b + 1]), s_used)

                def scale(i):
                    u, b = units[i], (u0 + i) % P_BUFS
                    total = small["row_sum"][:, b:b + 1]
                    dve.wait_ge(p_ready, u0 + i + 1)
                    if u.sink is not None:
                        n["sink"] += 1
                        dve.wait_ge(sink_ready, n["sink"])
                        step(nc.vector.tensor_scalar(total, total, small["sink_exp"][:, b:b + 1], None, ALU.add))
                        step.wait()
                    inverse = step(nc.vector.reciprocal(small["inv_sum"][:, b:b + 1], total))
                    dve.wait_ge(*inverse)
                    step(nc.vector.tensor_scalar(p[:, b, 0:u.width], p[:, b, 0:u.width], small["inv_sum"][:, b:b + 1], None,
                                                 ALU.mult), pn_ready)
                    if i + AHEAD < len(units):
                        top(i + AHEAD)

                def out_of(i):
                    if units[i].last:
                        dve.wait_ge(pv_done, u0 + i + 1)
                        step.wait()
                        step(nc.vector.tensor_copy(units[i].dst, ps_o[:]), o_taken)

                step.wait()
                for i in range(AHEAD):
                    top(i)
                for i in range(len(units)):
                    scale(i)
                    for work in also.get(i, []):
                        work()
                    if i:
                        out_of(i - 1)
                out_of(len(units) - 1)
                n["unit"] += len(units)

            for dst, value in [("eps_d", EPS), ("eps_q", HEAD_DIM * EPS), ("eps_v", EPS)]:
                step.wait()
                step(nc.vector.memset(small[dst][:], value), setup_done if dst == "eps_v" else None)
            dve.wait_ge(params_loaded, 16)
            for i in range(X_PARTS):
                dve.wait_ge(x_loaded[i], 16)
                layer_input(x_res, lambda i: param("norm1_g", i), tiles=range(i * DT // X_PARTS, (i + 1) * DT // X_PARTS))
            dve.wait_ge(masks_loaded, 16)
            step.wait()
            step(nc.vector.tensor_copy(masks[:], masks_f32[:]))
            step.wait()
            step(nc.vector.tensor_scalar(small["k_g8"][:], param("k_g"), float(HEAD_DIM) ** 0.5, None, ALU.mult))
            step.wait()
            c = PARAM_COLS["sink"]
            step(nc.vector.tensor_scalar(small["neg_sink"][:], params[:, c:c + HEADS], -1.0, None, ALU.mult))
            step.wait()
            c = PARAM_COLS["b_gate"]
            step(nc.vector.tensor_scalar(small["half_gate_b"][:], params[:, c:c + 16], 0.5, None, ALU.mult))
            lb = lambda d, l: params[:, PARAM_COLS["lb_logits"] + 16 * d + 8 * l:PARAM_COLS["lb_logits"] + 16 * d + 8 * l + 8]
            ex = lambda d, l: small["lb_exp"][:, 16 * d + 8 * l:16 * d + 8 * l + 8]
            for d in range(2):
                step.wait()
                step(nc.vector.tensor_tensor(small["lower"][:, 8 * d:8 * d + 8], lb(d, 0), lb(d, 1), ALU.max))
                for l in range(2):
                    step.wait()
                    step(nc.vector.tensor_tensor(ex(d, l), lb(d, l), small["lower"][:, 8 * d:8 * d + 8], ALU.subtract),
                         setup_done if d == 1 and l == 1 else None)

            invert_rms(rstd_in)
            st = stages["qkv"]
            plan = lagged(st.cbs, BANKS, 2 * DT)
            for c in range(st.cbs):
                if c < 2 * DT:
                    scaled(st, c, qk[:, c, :])
                else:
                    feat_v(st, c, v_feat)
                for i in plan.get(c, []):
                    invert_rms(rstd)
                    step.wait()
                    step(nc.vector.scalar_tensor_tensor(qk[:, i, :], qk[:, i, :], param("q_g") if i < DT else
                                                        small["k_g8"][:], rstd[:], ALU.mult, ALU.mult), qk_ready)
                if c >= 2 * DT:
                    tok_v(v_tok1[:, :, (c - 2 * DT) * P:(c - 2 * DT + 1) * P])
            dve.wait_ge(setup_act, 1)
            for d in range(2):
                low, one = small["lower"][:, 8 * d:8 * d + 8], small["one_less"][:, 8 * d:8 * d + 8]
                step.wait()
                step(nc.vector.tensor_tensor(low, ex(d, 0), ex(d, 1), ALU.add))
                step.wait()
                step(nc.vector.reciprocal(one, low))
                step.wait()
                step(nc.vector.tensor_tensor(low, ex(d, 1), one, ALU.mult))
                step.wait()
                step(nc.vector.tensor_scalar(one, low, -1.0, 1.0, ALU.mult, ALU.add))
            conv_st = stages["conv"]

            def conv(c):
                i, part = divmod(c, 3)
                t_, u = ffn_tmp[:, 0, :], ffn_tmp[:, 1, :]
                scaled(conv_st, c, t_ if part == 0 else u)
                step.wait()
                if part == 1:
                    w = [param("conv_w", 8 * k + i) for k in range(3)]
                    step(nc.vector.tensor_tensor(u, u, t_, ALU.mult))
                    step.wait()
                    step(nc.vector.tensor_scalar(t_, u, w[2], param("conv_b", i), ALU.mult, ALU.add))
                    step.wait()
                    step(nc.vector.scalar_tensor_tensor(t_[:, 1:T], u[:, 0:T - 1], w[1], t_[:, 1:T], ALU.mult, ALU.add))
                    step.wait()
                    step(nc.vector.scalar_tensor_tensor(t_[:, 2:T], u[:, 0:T - 2], w[0], t_[:, 2:T], ALU.mult, ALU.add))
                elif part == 2:
                    step(nc.vector.tensor_tensor(y_conv[:, i, :], u, t_, ALU.mult))

            also = {i: [] for i in range(len(units1) + 1)}
            for c in range(conv_st.cbs):
                also[conv_turn(c)].append(lambda c=c: conv(c))
            attention(units1, probs, also)
            for work in also[len(units1)]:
                work()
            for i in range(DT):
                split(y_conv[:, i, :], y_hi[:, i, :], y_lo[:, i, :], y_ready)
            for i in range(DT):
                split(o_all[:, i, :], o_hi1[:, i, :], o_lo1[:, i, :], o_ready)
            for c in range(2 * DT):
                scaled(stages["gate"], c, gates[:, c, :])
            st = stages["proj"]
            dve.wait_ge(gate_ready, 2 * DT)
            for i in range(DT):
                for b in range(2):
                    g = gates[:, DT * b + i, :]
                    dve.wait_ge(slot_done, st.made(2 * i + b))
                    step.wait()
                    step(nc.vector.scalar_tensor_tensor(g, g, 1.0, acc[st.bank(2 * i + b)][:], ALU.add, ALU.mult), st.free)
                step.wait()
                step(nc.vector.tensor_tensor(gates[:, i, :], gates[:, i, :], gates[:, DT + i, :], ALU.add))
                split(gates[:, i, :], h_hi[:, i, :], h_lo[:, i, :], m_ready)
            st = stages["out"]
            for i in range(DT):
                dve.wait_ge(slot_done, st.made(i))
                step.wait()
                step(nc.vector.scalar_tensor_tensor(x_res[:, i, :], acc[st.bank(i)][:], 0.5, x_res[:, i, :], ALU.mult, ALU.add),
                     st.free)
            layer_input(x_res, lambda i: param("norm2_g", i))
            invert_rms(rstd_in)
            for half in range(2):
                st = stages[f"up{half}"]
                for i in range(HALF):
                    t_ = u_tmp[:, i % 2, :]
                    dve.wait_ge(slot_done, st.made(i))
                    step.wait()
                    step(nc.vector.scalar_tensor_tensor(t_, acc[st.bank(i)][:], 0.0, rstd_in[:], ALU.max, ALU.mult), st.free)
                    step.wait()
                    step(nc.vector.tensor_tensor(t_, t_, t_, ALU.mult))
                    split(t_, u_hi[:, i, :], u_lo[:, i, :], u_ready)
                st = stages[f"down{half}"]
                for i in range(DT):
                    dve.wait_ge(slot_done, st.made(i))
                    step.wait()
                    step(nc.vector.tensor_tensor(x_res[:, i, :], acc[st.bank(i)][:], x_res[:, i, :], ALU.add), st.free)
            def conv_mlp(layer, next_gain):
                invert_rms(rstd_in)
                st = stages[f"ffn_in{layer}"]

                def conv(i):
                    g, t_ = hid_tmp[:, i, :], ffn_tmp[:, i % 2, :]
                    w = [param("ffn_w", (3 * layer + k) * FF2 + i) for k in range(3)]
                    scaled(st, 2 * i, g)
                    step.wait()
                    step(nc.vector.tensor_scalar(t_, g, w[1], param("ffn_b", layer * FF2 + i), ALU.mult, ALU.add))
                    step.wait()
                    step(nc.vector.scalar_tensor_tensor(t_[:, 1:T], g[:, 0:T - 1], w[0], t_[:, 1:T], ALU.mult, ALU.add))
                    step.wait()
                    step(nc.vector.scalar_tensor_tensor(t_[:, 0:T - 1], g[:, 1:T], w[2], t_[:, 0:T - 1], ALU.mult, ALU.add),
                         conv_ready)

                def hidden(i):
                    up, t_ = hid_tmp[:, i, :], ffn_tmp[:, i % 2, :]
                    scaled(st, 2 * i + 1, up)
                    dve.wait_ge(gelu_ready, layer * FF2 + i + 1)
                    step.wait()
                    step(nc.vector.tensor_tensor(t_, up, t_, ALU.mult))
                    split(t_, hid_hi[:, i, :], hid_lo[:, i, :], hid_ready)

                for i in range(FF2):
                    conv(i)
                    hidden(i)
                take_y(stages[f"ffn_out{layer}"], ffn_tmp)
                add_norm(lambda i: param("norm_g", 32 * layer + 24 + i), next_gain)

            def mixer_out(layer):
                take_y(stages["ab"[layer] + "_out"], square)
                add_norm(lambda i: param("norm_g", 32 * layer + 8 + i), lambda i: param("norm_g", 32 * layer + 16 + i))

            def split_out(i, o_hi):
                split(o2[:, i, :], o_hi[:, i, 0:T], o_lo2[:, i, :], o_ready)

            layer_input(x_res, lambda i: param("norm_g", i))
            invert_rms(rstd_in)
            st = stages["a_in"]
            plan = lagged(XQ_FIRST, BANKS, 10)
            for c in range(XQ_FIRST):
                if c < 10:
                    scaled(st, c, q_win[:, c, :] if c < DT else k_win[:, c - DT, :],
                           float(HEAD_DIM) ** -0.5 if c < DT else None)
                elif c < 12:
                    feat_v(st, c, v_feat)
                else:
                    scaled(st, c, xq[:, c - 12, :])
                for i in plan.get(c, []):
                    dst = q_win[:, i, :] if i < DT else k_win[:, i - DT, :]
                    if i == 0:
                        dve.wait_ge(rope_loaded, 16)
                    dve.wait_ge(rope_rot, i + 1)
                    step.wait()
                    step(nc.vector.tensor_tensor(normed[:, 0, :], ps_t[:], rope[:, 1, :], ALU.mult), rope_done)
                    step.wait()
                    step(nc.vector.tensor_tensor(dst, dst, rope[:, 0, :], ALU.mult))
                    step.wait()
                    step(nc.vector.tensor_tensor(dst, dst, normed[:, 0, :], ALU.add), rope_ready)
                if 10 <= c < 12:
                    tok_v(v_win[:, :, (c - 10) * P:(c - 9) * P])

            mem_st = stages["memkv"]

            def mem_block(c):
                layer, j = divmod(c, 8)
                if j < 4:
                    scaled(mem_st, c, mem_k[layer][:, j, :])
                else:
                    feat_v(mem_st, c, normed, MEM)

            def mem_tokens(c):
                layer, j = divmod(c, 8)
                if j >= 4:
                    tok_v(mem_v[layer][:, :, (j - 4) * P:(j - 3) * P])

            also = {i: [] for i in range(len(units_win) + len(units_x[0]))}
            for c in range(XQ_FIRST, st.cbs):
                also[xq_turn(c)].append(lambda c=c: scaled(st, c, xq[:, c - 12, :]))
            also[MEM_INPUT].append(lambda: dve.wait_ge(mem_loaded, 16))
            for i in range(DT):
                also[MEM_INPUT + i // 2].append(lambda i=i: layer_input(mem, lambda i: param("mem_g", i), MEM, [i]))
            also[MEM_SUMS + 1].append(lambda: invert_rms(rstd_in, cols=MEM))
            for c in range(mem_st.cbs):
                also[MEM_FIRST + c // 2 - 1 if c < BANKS else mem_turn(c)].append(lambda c=c: mem_block(c))
                if c >= BANKS:
                    also[mem_turn(c) + 1].append(lambda c=c: mem_tokens(c))
            for i in range(DT):
                also[X_FIRST + i].append(lambda i=i: split_out(i, o_hi2))
            for j in range(X_HEADS - 1):
                also[X_FIRST + BLOCKS * (j + 1) + 1].append(lambda j=j: split_out(DT + j, o_hi2))
            attention(units_win + units_x[0], probs2, also)
            split_out(DT + X_HEADS - 1, o_hi2)
            mixer_out(0)
            conv_mlp(0, lambda i: param("norm_g", 32 + i))

            invert_rms(rstd_in)
            st = stages["b_in"]
            for j in range(X_HEADS):
                scaled(st, j, xq[:, j, :])

            def head_in(h, j):
                if h < HG_HEADS:
                    scaled(st, X_HEADS + 5 * h + j, hg_in[h % 2][:, j, :])
                else:
                    for i in [(4, 5), (), (6, 7), (8, 9), (10,)][j]:
                        split_out(i, o_hi3)

            attention(units_x[1], probs2, {b_in_turn(j): [lambda j=j: head_in(0, j)] for j in range(5)})
            for s_ in (hg_s_f, hg_s_b):
                step.wait()
                step(nc.vector.memset(s_[:], 0.0))
            by_chunk = lambda ap: ap.rearrange("p (c t) -> p c t", t=HG_CHUNK)
            key, qd, grow, qb = (hg_key_f, hg_key_b), (hg_qd_f, hg_qd_b), (hg_grow_f, hg_grow_b), (hg_qb_f, hg_qb_b)
            small_of = lambda name, d: small[name + "_" + "fb"[d]]
            for t_ in [*hg_level_k, end_f, end_b]:
                step.wait()
                step(nc.vector.memset(t_[:], 0.0))

            def near_of(d, side, level):
                return (near_f, near_b)[d][:, (3 * side + level) * CHUNKS:(3 * side + level + 1) * CHUNKS]

            def head_decays(h):
                for d in range(2):
                    f_ = hg_in[h % 2][:, 2 + d, :]
                    i = 8 * d + h
                    dve.wait_ge(hg_sig, 2 * h + d + 1)
                    step.wait()
                    step(nc.vector.tensor_scalar(f_, f_, small["one_less"][:, i:i + 1], small["lower"][:, i:i + 1],
                                                 ALU.mult, ALU.add))
                    step.wait()
                    step(nc.vector.tensor_scalar(key[d][:], f_, -1.0, 1.0, ALU.mult, ALU.add), hg_f)
                for d in range(2):
                    b_ = hg_in[h % 2][:, 2 + d, :]
                    way = slice(None) if d == 0 else slice(None, None, -1)
                    dve.wait_ge(hg_ln, 2 * h + d + 1)
                    step.wait()
                    step(nc.vector.tensor_tensor_scan(b_[:, way], const("reset", T), b_[:, way], 0.0, ALU.mult, ALU.add),
                         hg_cum)
                for d in range(2):
                    b_, end, near = hg_in[h % 2][:, 2 + d, :], (end_f, end_b)[d], (near_f, near_b)[d]
                    step.wait()
                    step(nc.vector.tensor_copy(
                        end[:, 1:3 * CHUNKS + 1].rearrange("p (l c) -> p l c", c=CHUNKS),
                        by_chunk(b_)[:, :, 0 if d else HG_CHUNK - 1].unsqueeze(1).to_broadcast([P, 3, CHUNKS])))
                    for side in range(2):
                        back = d != side
                        way = slice(None, None, -1) if back else slice(None)
                        at_, reset = (2, 2 * CHUNKS) if back else (0, 0)
                        to = near[:, 3 * side * CHUNKS:3 * (side + 1) * CHUNKS]
                        step.wait()
                        step(nc.vector.tensor_tensor_scan(to[:, way], end[:, at_:at_ + 3 * CHUNKS][:, way],
                                                          const("span_reset", 5 * CHUNKS)[:, reset:reset + 3 * CHUNKS], 0.0,
                                                          ALU.add, ALU.mult))
                    dve.wait_ge(hg_exp, 4 * h + 2 * d + 2)
                    step.wait()
                    step(nc.vector.tensor_tensor(by_chunk(b_), end[:, 1:CHUNKS + 1].unsqueeze(2).to_broadcast(
                        [P, CHUNKS, HG_CHUNK]), by_chunk(b_), ALU.subtract), hg_rest)

            def head_queries(h):
                dve.wait_ge(hg_silu_q, h + 1)
                for d in range(2):
                    step.wait()
                    step(nc.vector.tensor_tensor(qd[d][:], qd[d][:], hg_in[h % 2][:, 0, :], ALU.mult))
                    step.wait()
                    step(nc.vector.tensor_tensor(grow[d][:], grow[d][:], key[d][:], ALU.mult))

            def head_levels(h):

                def decayed(dst, src, d, side, level, half, done=None):
                    by = near_of(d, side, level)
                    if half is None:
                        src, dst, by = by_chunk(src), by_chunk(dst), by.unsqueeze(2).to_broadcast([P, CHUNKS, HG_CHUNK])
                    else:
                        m = 2 << level
                        pick = lambda ap: ap.rearrange("p (s x c t) -> p s x c t", x=2, c=m, t=HG_CHUNK)[:, :, half]
                        src = pick(src)
                        dst = pick(dst) if side else dst.rearrange("p (s c t) -> p s c t", c=m, t=HG_CHUNK)
                        by = by.rearrange("p (s x c) -> p s x c", x=2, c=m)[:, :, half].unsqueeze(3).to_broadcast(
                            [P, CHUNKS // m // 2, m, HG_CHUNK])
                    step.wait()
                    step(nc.vector.tensor_tensor(dst, src, by, ALU.mult), done)

                for d in range(2):
                    rest = hg_in[h % 2][:, 2 + d, :]
                    dve.wait_ge(hg_rest_exp, 2 * h + d + 1)
                    step.wait()
                    step(nc.vector.tensor_tensor(rest, rest, key[d][:], ALU.mult))
                    for level in range(2):
                        decayed(hg_level_q[d][:, level, :], qd[d][:], d, 0, level, 1 - d)
                        decayed(hg_level_k[d][:, level, :], rest, d, 1, level, d)
                    decayed(hg_block_k[d][:], rest, d, 1, 2, None, hg_k if d else None)
                if h:
                    dve.wait_ge(hg_o, h)
                for d in range(2):
                    decayed(qb[d][:], qd[d][:], d, 0, 2, None)
                    before, decay, blk = near_of(d, 0, 2), small_of("decay", d), small_of("block", d)
                    at_ = slice(0 if d else BLOCK_CHUNKS - 1, None, BLOCK_CHUNKS)
                    step.wait()
                    step(nc.vector.tensor_tensor(blk[:], before[:, at_], decay[:, at_], ALU.mult))

            def head_scores(h, part):
                dve.wait_ge(hg_st, 3 * h + part + 1)
                into = [hg_s_f, hg_s_b]

                def keep(d, level, bank, at, done=None):
                    m = MASK_COLS["fb"[d] + str(level)]
                    mask = masks[:, m:m + (P if level == 0 else P // 2)]
                    if level == 0:
                        dst = into[d][:]
                        dims = [P, BLOCKS, P]
                        src = bank[:, at:at + T].rearrange("p (b n) -> p b n", n=P)
                        mask = mask.unsqueeze(1).to_broadcast(dims)
                    else:
                        half = HG_CHUNK << (level - 1)
                        spans = P // half // 2
                        dst = into[d][:].rearrange("p b (s x t) -> p b s x t", x=2, t=half)[:, :, :, 1 - d, :]
                        src = bank[:, at:at + T // 2].rearrange("p (b s t) -> p b s t", b=BLOCKS, t=half)
                        mask = mask.rearrange("p (s t) -> p s t", t=half).unsqueeze(1).to_broadcast(
                            [P, BLOCKS, spans, half])
                    step.wait()
                    step(nc.vector.copy_predicated(dst, mask, src), done)

                if part == 0:
                    keep(0, 0, ps_s[0], 0)
                    keep(0, 1, ps_s[1], 0)
                    keep(0, 2, ps_s[1], T // 2, hg_s)
                elif part == 1:
                    keep(0, 3, ps_s[0], 0)
                    keep(1, 3, ps_s[0], T // 2)
                    keep(1, 1, ps_s[1], 0)
                    keep(1, 2, ps_s[1], T // 2, hg_s)
                else:
                    keep(1, 0, ps_s[0], 0, hg_s)

            def head_states(h):
                for d, state in enumerate([hg_state_f, hg_state_b]):
                    dve.wait_ge(hg_u, 2 * h + d + 1)
                    blk = small_of("block", d)
                    u_ = ps_s[1 - d][:, 0:(BLOCKS - 1) * P].rearrange("p (b n) -> p b n", n=P)
                    for i in range(BLOCKS - 1):
                        b = BLOCKS - 2 - i if d else i
                        done = hg_chain if d and i == BLOCKS - 2 else None
                        step.wait()
                        if i == 0:
                            step(nc.vector.tensor_copy(state[:, b, :], u_[:, b, :]), done)
                        else:
                            over = b + d
                            step(nc.vector.scalar_tensor_tensor(state[:, b, :], state[:, b + 2 * d - 1, :], blk[:, over:over + 1],
                                                                u_[:, b, :], ALU.mult, ALU.add), done)

            def head_out(h):
                invert_rms(rstd_head, ffn_tmp[:, 1, :])
                step.wait()
                step(nc.vector.scalar_tensor_tensor(o2[:, X_HEADS + h, :], ps_o[:], param("b_norm_g", h), rstd_head[:], ALU.mult, ALU.mult),
                     o_taken)
                dve.wait_ge(hg_silu_g, h + 1)
                step.wait()
                step(nc.vector.tensor_tensor(o2[:, X_HEADS + h, :], o2[:, X_HEADS + h, :], hg_in[h % 2][:, 4, :], ALU.mult))

            for h in range(HG_HEADS):
                head_decays(h)
                if h < HG_HEADS - 1:
                    head_in(h + 1, 0)
                if h:
                    head_states(h - 1)
                if h == HG_HEADS - 1:
                    head_in(h + 1, 0)
                head_queries(h)
                head_in(h + 1, 1)
                head_levels(h)
                head_in(h + 1, 2)
                if h:
                    head_out(h - 1)
                head_scores(h, 0)
                head_in(h + 1, 3)
                head_scores(h, 1)
                if h == HG_HEADS - 2:
                    for i in range(X_HEADS):
                        split_out(i, o_hi3)
                head_in(h + 1, 4)
                head_scores(h, 2)
            head_states(HG_HEADS - 1)
            head_out(HG_HEADS - 1)
            split_out(X_HEADS + HG_HEADS - 1, o_hi3)
            mixer_out(1)
            conv_mlp(1, None)


def weight_tiles(w):
    k, n = w.shape
    return w.reshape(k // P, P, n // P, P).transpose(2, 0, 1, 3).reshape(-1, P, P)


def columns(a):
    return np.ascontiguousarray(a.reshape(-1, P).T)


def span_mask(i, half, d):
    queries = i[i // half % 2 == (1 if d == "f" else 0)]
    keys_in = i // half % 2 == (0 if d == "f" else 1)
    return keys_in[:, None] & (i[:, None] // half // 2 == queries[None, :] // half // 2)


def shape_constants():
    i = np.arange(P)
    q, k = i[:, None], i[None, :]
    rot = np.zeros((P, P), np.float32)
    half = HEAD_DIM // 2
    for m in range(P):
        if m % HEAD_DIM < half:
            rot[m + half, m] = -1.0
        else:
            rot[m - half, m] = 1.0
    mask = lambda keep: np.where(keep, 0.0, NEG)
    parts = {
        "ident": np.eye(P), "rot": rot, "pair_ones": q // HEAD_DIM == k // HEAD_DIM, "ones": np.ones((P, P)),
        "win_mask": np.concatenate([mask(k >= q), np.zeros((P, P)), mask(k <= q)], 1),
        "reset": np.broadcast_to(np.arange(T) % HG_CHUNK != 0, (P, T)),
        "span_reset": np.broadcast_to(np.concatenate([np.arange(CHUNKS) % n != 0 for n in (2, 4, 8, 4, 2)]), (P, 5 * CHUNKS)),
    }
    consts = np.concatenate([np.asarray(parts[c], np.float32) for c in CONST_COLS], 1)
    keep = {"f0": (q // HG_CHUNK == k // HG_CHUNK) & (q <= k), "b0": (q // HG_CHUNK == k // HG_CHUNK) & (q >= k),
            **{f"{d}{level}": span_mask(i, HG_CHUNK << (level - 1), d) for d in "fb" for level in range(1, 4)}}
    masks = np.concatenate([keep[c] for c in MASK_COLS], 1).astype(np.float32)
    inv = np.float32(10000.0) ** (-np.arange(half, dtype=np.float32) / np.float32(half))
    angle = (np.arange(T, dtype=np.float32)[None, :] * inv[i % half][:, None]).astype(np.float64)
    rope = np.stack([np.cos(angle), np.sin(angle)], 1).astype(np.float32)
    return consts, rope, masks


def layout(a):
    by_tile = lambda x: np.ascontiguousarray(x[0].T.reshape(DT, P, -1).transpose(1, 0, 2))
    blocks = {}
    for name in ["w_in", "w_gate", "w_attn_proj", "w_conv_proj", "w_out", "w_up", "w_down"]:
        blocks[name] = weight_tiles(a[name]).reshape(a[name].shape[1] // P, -1, P, P)
    win = blocks["w_in"]
    conv = [win[24 + 8 * part + i] for i in range(DT) for part in (1, 2, 0)]
    proj = [blocks[w][i] for i in range(DT) for w in ("w_attn_proj", "w_conv_proj")]
    perm = [4 * (2 * (s // 8) + s % 2) + (s % 8) // 2 for s in range(HEADS)]
    cols = np.concatenate([np.arange(h * HEAD_DIM, (h + 1) * HEAD_DIM) for h in perm])
    a_in, a_out, b_out = a["a_w_in_2"][0], a["a_w_out_2"][0], a["b_w_out_2"][0]
    a_in = np.concatenate([a_in[:, cols], a_in[:, D:]], 1)
    a_out = np.concatenate([a_out[cols], a_out[D:]], 0)
    b_in = weight_tiles(a["b_w_in_2"][0]).reshape(-1, DT, P, P)
    b_in = [b_in[40 + i] for i in range(X_HEADS)] + [b_in[8 * part + h] for h in range(HG_HEADS) for part in range(5)]

    def ffn_in(layer):
        return weight_tiles(a["ffn_w_in_2"][layer]).reshape(2, FF2, DT, P, P).transpose(1, 0, 2, 3, 4)

    up, down = blocks["w_up"], blocks["w_down"]
    order = [win[:24], conv, blocks["w_gate"], proj, blocks["w_out"],
             up[:HALF], down[:, :HALF], up[HALF:], down[:, HALF:],
             weight_tiles(a_in), weight_tiles(a["w_mem_kv_2"][0]), weight_tiles(a["w_mem_kv_2"][1]), weight_tiles(a_out), ffn_in(0), weight_tiles(a["ffn_w_out_2"][0]),
             b_in, weight_tiles(np.concatenate([b_out[D:], b_out[:D]], 0)), ffn_in(1), weight_tiles(a["ffn_w_out_2"][1])]
    tiles = np.concatenate([np.asarray(o).reshape(-1, P, P) for o in order])
    at = 0
    for name, cbs, kt in STAGES:
        if name in LEAD:
            lead = tiles[at:at + BANKS * kt]
            tiles[at:at + BANKS * kt] = lead.reshape(BANKS, kt, P, P).transpose(1, 0, 2, 3).reshape(-1, P, P).copy()
        at += cbs * kt
    stream = np.ascontiguousarray(tiles.reshape(-1, SLOT_TILES, P, P).transpose(0, 2, 1, 3)).reshape(-1, P, SLOT_TILES * P)
    pair = lambda g: np.concatenate([g, g])
    params = np.concatenate([
        columns(a["norm1_g"]), columns(a["norm2_g"]), columns(pair(a["q_norm_g"])), columns(pair(a["k_norm_g"])),
        columns(a["conv_w"]), columns(a["conv_b"]), columns(a["b_gate"]), columns(a["norm_g_2"]), columns(a["mem_norm_g_2"]),
        columns(a["b_lb_logits_2"]), columns(a["b_norm_g_2"]), columns(a["ffn_conv_w_2"]), columns(a["ffn_conv_b_2"]),
        np.broadcast_to(a["a_sink_2"][0][perm][None, :], (P, HEADS))], 1)
    flipped = a["rel_bias"][:, ::-1]
    ext = np.concatenate([np.repeat(flipped[:, :1], T // 2 - 1, 1), flipped[:, :EXT_W - T // 2 + 1]], 1)
    consts, rope, masks = shape_constants()
    return {"stream": stream, "x_in": by_tile(a["x"]), "mem_in": by_tile(a["mem_2"]), "consts_in": consts, "rope_in": rope,
            "params_in": np.ascontiguousarray(params), "masks_in": masks, "ext_in": np.stack([ext[:, P - 1 - q:P - 1 - q + T] for q in range(P)], 1)}


def kernel(**inputs):
    import concourse.bacc as bacc
    from concourse.bass_utils import run_bass_kernel_spmd

    arrays = layout({k: np.asarray(v) for k, v in inputs.items()})
    nc = bacc.Bacc("TRN2", target_bir_lowering=False, num_devices=1)
    args = [nc.dram_tensor(k, v.shape, mybir.dt.from_np(v.dtype), kind="ExternalInput").ap() for k, v in arrays.items()]
    out = nc.dram_tensor("out", (P, DT, T), F32, kind="ExternalOutput").ap()
    build(nc, *args, out)
    result = run_bass_kernel_spmd(nc, [arrays], core_ids=[0]).results[0]["out"]
    return np.ascontiguousarray(result.transpose(1, 0, 2).reshape(1, D, T).transpose(0, 2, 1))
```
